# Optimizing a Trainium2 kernel written in Bass

```python
import math
import jax, jax.numpy as jnp
from jax import lax
import numpy as np

D_MODEL = 1024
BATCH = 1
SEQ = 512
DEPTH = 2
DEC_BATCH = 8
DEC_SEQ = 8
PAST_LEN = 1024
PAGE_SIZE = 128

HEAD_DIM = 64
MIX_HALF = D_MODEL // 2
A_HEADS = MIX_HALF // HEAD_DIM
B_HEADS = MIX_HALF // HEAD_DIM
N_IN_COLS = 7 * MIX_HALF
MOBA_BLOCK = 256
MOBA_TOPK = 3
MOBA_QCHUNK = 64
RET_CHUNK = 128
S5_GROUP = 16
S5_GROUPS = D_MODEL // S5_GROUP
S5_STATE = 64
S5_CHUNK = 256
D_FF = ((8 * D_MODEL // 3 + 127) // 128) * 128
ROPE_THETA = 10000.0
LN_EPS = 1e-5
GN_EPS = 1e-6
NEG_INF = -1e30
N_AB_LAYERS = (DEPTH + 1) // 2
N_SSM_LAYERS = DEPTH // 2
DEEPNORM_ALPHA = (2 * DEPTH) ** 0.25
DEEPNORM_BETA = (8 * DEPTH) ** -0.25

kernel_name = 'moba_retnet_s5_macaron_deepnorm_decoder_step'

def layer_norm(x, g, b):
    xf = x.astype(jnp.float32)
    mu = jnp.mean(xf, -1, keepdims=True)
    var = jnp.mean(jnp.square(xf - mu), -1, keepdims=True)
    y = (xf - mu) * lax.rsqrt(var + LN_EPS) * g.astype(jnp.float32) + b.astype(jnp.float32)
    return y.astype(x.dtype)

def swiglu(x, w_gate, w_up, w_down):
    return (jax.nn.silu(x @ w_gate) * (x @ w_up)) @ w_down

def rope(x, pos):
    half = x.shape[-1] // 2
    inv = ROPE_THETA ** (-jnp.arange(half, dtype=jnp.float32) / half)
    ang = pos.astype(jnp.float32)[:, None] * inv[None, :]
    cos = jnp.cos(ang)[None, :, None, :]
    sin = jnp.sin(ang)[None, :, None, :]
    xf = x.astype(jnp.float32)
    x1, x2 = xf[..., :half], xf[..., half:]
    return jnp.concatenate([x1 * cos - x2 * sin, x1 * sin + x2 * cos], -1).astype(x.dtype)

def moba_seq(q, k, v, q_pos):
    n_heads, hd = q.shape[1], q.shape[2]
    nb = k.shape[0] // MOBA_BLOCK
    kb = k.reshape(nb, MOBA_BLOCK, n_heads, hd)
    vb = v.reshape(nb, MOBA_BLOCK, n_heads, hd)
    k_mean = jnp.mean(kb.astype(jnp.float32), axis=1)
    kh = jnp.transpose(kb, (2, 0, 1, 3))
    vh = jnp.transpose(vb, (2, 0, 1, 3))
    n_top = min(MOBA_TOPK, nb)
    n_q = q.shape[0]
    qc = math.gcd(n_q, MOBA_QCHUNK)
    head_ix = jnp.arange(n_heads)[None, :, None]
    blk_ix = jnp.arange(nb)
    scale = hd ** -0.5

    def chunk(args):
        qq, qp = args
        qf = qq.astype(jnp.float32) * scale
        q_blk = qp // MOBA_BLOCK
        own = q_blk[0]
        gate = jnp.einsum('qhd,nhd->qhn', qf, k_mean)
        gate = jnp.where(blk_ix[None, None, :] < q_blk[:, None, None], gate, NEG_INF)
        _, sel = lax.top_k(gate, n_top)
        sel_ok = sel < q_blk[:, None, None]
        kg = kh[head_ix, sel].astype(jnp.float32)
        vg = vh[head_ix, sel].astype(jnp.float32)
        s_sel = jnp.einsum('qhd,qhskd->qhsk', qf, kg)
        s_sel = jnp.where(sel_ok[..., None], s_sel, NEG_INF)
        k_own = lax.dynamic_slice_in_dim(k, own * MOBA_BLOCK, MOBA_BLOCK, 0).astype(jnp.float32)
        v_own = lax.dynamic_slice_in_dim(v, own * MOBA_BLOCK, MOBA_BLOCK, 0).astype(jnp.float32)
        s_own = jnp.einsum('qhd,khd->qhk', qf, k_own)
        k_pos = own * MOBA_BLOCK + jnp.arange(MOBA_BLOCK)
        s_own = jnp.where(k_pos[None, None, :] <= qp[:, None, None], s_own, NEG_INF)
        logits = jnp.concatenate([s_sel.reshape(qc, n_heads, n_top * MOBA_BLOCK), s_own], axis=-1)
        p = jax.nn.softmax(logits, axis=-1)
        p_sel = p[..., : n_top * MOBA_BLOCK].reshape(qc, n_heads, n_top, MOBA_BLOCK)
        out = (jnp.einsum('qhsk,qhskd->qhd', p_sel, vg)
               + jnp.einsum('qhk,khd->qhd', p[..., n_top * MOBA_BLOCK:], v_own))
        return out.astype(qq.dtype)

    out = lax.map(chunk, (q.reshape(n_q // qc, qc, n_heads, hd), q_pos.reshape(n_q // qc, qc)))
    return out.reshape(n_q, n_heads, hd)

def moba_prompt(q, k, v, pos):
    pad = (-k.shape[1]) % MOBA_BLOCK
    widths = ((0, 0), (0, pad), (0, 0), (0, 0))
    kp = jnp.pad(k, widths)
    vp = jnp.pad(v, widths)
    return lax.map(lambda a: moba_seq(a[0], a[1], a[2], pos), (q, kp, vp))

def moba_sample(q, k_new, v_new, k_pool, v_pool, page_table, pos):
    def one(a):
        qq, kn, vn, pt = a
        hs = kn.shape[1:]
        k_full = jnp.concatenate([k_pool[pt].reshape((-1,) + hs).astype(kn.dtype), kn], 0)
        v_full = jnp.concatenate([v_pool[pt].reshape((-1,) + hs).astype(vn.dtype), vn], 0)
        pad = (-k_full.shape[0]) % MOBA_BLOCK
        k_full = jnp.pad(k_full, ((0, pad), (0, 0), (0, 0)))
        v_full = jnp.pad(v_full, ((0, pad), (0, 0), (0, 0)))
        return moba_seq(qq, k_full, v_full, pos)
    return lax.map(one, (q, k_new, v_new, page_table))

def retention(q, k, v, s0):
    bn, n_len, n_heads, dk = q.shape
    dv = v.shape[-1]
    c = math.gcd(n_len, RET_CHUNK)
    n = n_len // c
    log_g = jnp.log1p(-jnp.exp2(-5.0 - jnp.arange(n_heads, dtype=jnp.float32)))
    idx = jnp.arange(c, dtype=jnp.float32)
    diff = idx[:, None] - idx[None, :]
    dmask = jnp.where(diff >= 0, jnp.exp(log_g[:, None, None] * jnp.maximum(diff, 0.0)), 0.0)
    q_dec = jnp.exp(log_g[None, :] * (idx[:, None] + 1.0))
    k_dec = jnp.exp(log_g[None, :] * (c - 1.0 - idx[:, None]))
    c_dec = jnp.exp(log_g * c)
    qs = jnp.moveaxis(q.astype(jnp.float32).reshape(bn, n, c, n_heads, dk), 1, 0)
    ks = jnp.moveaxis((k.astype(jnp.float32) * dk ** -0.5).reshape(bn, n, c, n_heads, dk), 1, 0)
    vs = jnp.moveaxis(v.astype(jnp.float32).reshape(bn, n, c, n_heads, dv), 1, 0)

    def step(s, inp):
        qc, kc, vc = inp
        inner = jnp.einsum('bnhd,bmhd->bhnm', qc, kc) * dmask[None]
        o = (jnp.einsum('bhnm,bmhe->bnhe', inner, vc)
             + jnp.einsum('bnhd,bhde->bnhe', qc, s) * q_dec[None, :, :, None])
        s = c_dec[None, :, None, None] * s + jnp.einsum('bmhd,bmhe->bhde', kc * k_dec[None, :, :, None], vc)
        return s, o

    s_fin, o = lax.scan(step, s0.astype(jnp.float32), (qs, ks, vs))
    return jnp.moveaxis(o, 0, 1).reshape(bn, n_len, n_heads, dv), s_fin

def ab_project(x, pos, w_in):
    bn, n_len, _ = x.shape
    qa, ka, va, qb, kb, vb, gb = jnp.split(x @ w_in, 7, axis=-1)
    heads = lambda t: t.reshape(bn, n_len, -1, HEAD_DIM)
    return (rope(heads(qa), pos), rope(heads(ka), pos), heads(va),
            rope(heads(qb), pos), rope(heads(kb), pos), heads(vb), gb)

def ab_merge(attn, ret, gb, w_out):
    bn, n_len = attn.shape[:2]
    mu = jnp.mean(ret, -1, keepdims=True)
    var = jnp.mean(jnp.square(ret - mu), -1, keepdims=True)
    rn = ((ret - mu) * lax.rsqrt(var + GN_EPS)).reshape(bn, n_len, MIX_HALF).astype(gb.dtype)
    out_b = jax.nn.silu(gb) * rn
    return jnp.concatenate([attn.reshape(bn, n_len, MIX_HALF), out_b], -1) @ w_out

def _s5_combine(e1, e2):
    a1, b1 = e1
    a2, b2 = e2
    return a1 * a2, a2 * b1 + b2

def s5_ssm(u, s0_re, s0_im, lam_re, lam_im, b_re, b_im, c_re, c_im, d_skip, log_dt):
    bn, n_len, _ = u.shape
    uf = u.astype(jnp.float32)
    lam = lax.complex(lam_re.astype(jnp.float32), lam_im.astype(jnp.float32))
    dt = jnp.exp(log_dt.astype(jnp.float32))[:, None]
    lam_bar = jnp.exp(lam * dt)
    b_bar = ((lam_bar - 1.0) / lam)[:, :, None] * lax.complex(b_re.astype(jnp.float32), b_im.astype(jnp.float32))
    cm = lax.complex(c_re.astype(jnp.float32), c_im.astype(jnp.float32))
    c = math.gcd(n_len, S5_CHUNK)
    n = n_len // c
    us = jnp.moveaxis(uf.reshape(bn, n, c, S5_GROUPS, S5_GROUP), 1, 0)
    a_elems = jnp.broadcast_to(lam_bar, (bn, c, S5_GROUPS, S5_STATE))

    def step(s, uc):
        bu = jnp.einsum('bcgh,gph->bcgp', uc.astype(jnp.complex64), b_bar)
        a_cum, s_loc = lax.associative_scan(_s5_combine, (a_elems, bu), axis=1)
        s_all = s_loc + a_cum * s[:, None]
        y = jnp.real(jnp.einsum('bcgp,ghp->bcgh', s_all, cm))
        return s_all[:, -1], y

    s0 = lax.complex(s0_re.astype(jnp.float32), s0_im.astype(jnp.float32))
    s_fin, ys = lax.scan(step, s0, us)
    y = jnp.moveaxis(ys, 0, 1).reshape(bn, n_len, D_MODEL) + uf * d_skip.astype(jnp.float32)
    return y, jnp.real(s_fin), jnp.imag(s_fin)

def s5_layer(x, s0_re, s0_im, lam_re, lam_im, b_re, b_im, c_re, c_im, d_skip, log_dt, w_out, w_gate):
    y, s_re, s_im = s5_ssm(x, s0_re, s0_im, lam_re, lam_im, b_re, b_im, c_re, c_im, d_skip, log_dt)
    g = jax.nn.gelu(y.astype(x.dtype))
    return (g @ w_out) * jax.nn.sigmoid(g @ w_gate), s_re, s_im

def setup_inputs(seed: int = 0) -> dict:
    key = jax.random.key(seed)
    ks = jax.random.split(key, 32)
    f32 = jnp.float32
    n_pages = PAST_LEN // PAGE_SIZE
    n_pool = (DEC_BATCH * n_pages * 5) // 4
    nrm = lambda k, shape, s: jax.random.normal(k, shape, f32) * s
    x_prompt = nrm(ks[0], (BATCH, SEQ, D_MODEL), 1.0)
    x_sample = nrm(ks[1], (DEC_BATCH, DEC_SEQ, D_MODEL), 1.0)
    cache_k = nrm(ks[2], (N_AB_LAYERS, n_pool, PAGE_SIZE, A_HEADS, HEAD_DIM), 1.0)
    cache_v = nrm(ks[3], (N_AB_LAYERS, n_pool, PAGE_SIZE, A_HEADS, HEAD_DIM), 1.0)
    page_table = jax.random.permutation(ks[4], n_pool)[: DEC_BATCH * n_pages].reshape(DEC_BATCH, n_pages).astype(jnp.int32)
    state_ret = nrm(ks[5], (N_AB_LAYERS, DEC_BATCH, B_HEADS, HEAD_DIM, HEAD_DIM), 0.5)
    state_s5_re = nrm(ks[6], (N_SSM_LAYERS, DEC_BATCH, S5_GROUPS, S5_STATE), 0.1)
    state_s5_im = nrm(ks[7], (N_SSM_LAYERS, DEC_BATCH, S5_GROUPS, S5_STATE), 0.1)
    ffn1_w_gate = nrm(ks[8], (DEPTH, D_MODEL, D_FF), D_MODEL ** -0.5)
    ffn1_w_up = nrm(ks[9], (DEPTH, D_MODEL, D_FF), D_MODEL ** -0.5)
    ffn1_w_down = nrm(ks[10], (DEPTH, D_FF, D_MODEL), D_FF ** -0.5 * DEEPNORM_BETA)
    ffn2_w_gate = nrm(ks[11], (DEPTH, D_MODEL, D_FF), D_MODEL ** -0.5)
    ffn2_w_up = nrm(ks[12], (DEPTH, D_MODEL, D_FF), D_MODEL ** -0.5)
    ffn2_w_down = nrm(ks[13], (DEPTH, D_FF, D_MODEL), D_FF ** -0.5 * DEEPNORM_BETA)
    ln_g = 1.0 + nrm(ks[14], (DEPTH, 3, D_MODEL), 0.02)
    ln_b = nrm(ks[15], (DEPTH, 3, D_MODEL), 0.02)
    w_in_ab = nrm(ks[16], (N_AB_LAYERS, D_MODEL, N_IN_COLS), D_MODEL ** -0.5)
    w_out_ab = nrm(ks[17], (N_AB_LAYERS, 2 * MIX_HALF, D_MODEL), (2 * MIX_HALF) ** -0.5 * DEEPNORM_BETA)
    s5_lam_re = -0.5 + nrm(ks[18], (N_SSM_LAYERS, S5_GROUPS, S5_STATE), 0.01)
    s5_lam_im = math.pi * jnp.arange(S5_STATE, dtype=f32) + nrm(ks[19], (N_SSM_LAYERS, S5_GROUPS, S5_STATE), 0.01)
    s5_b_re = nrm(ks[20], (N_SSM_LAYERS, S5_GROUPS, S5_STATE, S5_GROUP), (2 * S5_GROUP) ** -0.5)
    s5_b_im = nrm(ks[21], (N_SSM_LAYERS, S5_GROUPS, S5_STATE, S5_GROUP), (2 * S5_GROUP) ** -0.5)
    s5_c_re = nrm(ks[22], (N_SSM_LAYERS, S5_GROUPS, S5_GROUP, S5_STATE), S5_STATE ** -0.5)
    s5_c_im = nrm(ks[23], (N_SSM_LAYERS, S5_GROUPS, S5_GROUP, S5_STATE), S5_STATE ** -0.5)
    s5_d = nrm(ks[24], (N_SSM_LAYERS, D_MODEL), 1.0)
    s5_log_dt = jax.random.uniform(ks[25], (N_SSM_LAYERS, S5_GROUPS), f32, math.log(1e-3), math.log(1e-1))
    s5_w_out = nrm(ks[26], (N_SSM_LAYERS, D_MODEL, D_MODEL), D_MODEL ** -0.5 * DEEPNORM_BETA)
    s5_w_gate = nrm(ks[27], (N_SSM_LAYERS, D_MODEL, D_MODEL), D_MODEL ** -0.5)
    return {'x_prompt': x_prompt, 'x_sample': x_sample, 'cache_k': cache_k, 'cache_v': cache_v,
            'page_table': page_table, 'state_ret': state_ret, 'state_s5_re': state_s5_re,
            'state_s5_im': state_s5_im, 'ffn1_w_gate': ffn1_w_gate, 'ffn1_w_up': ffn1_w_up,
            'ffn1_w_down': ffn1_w_down, 'ffn2_w_gate': ffn2_w_gate, 'ffn2_w_up': ffn2_w_up,
            'ffn2_w_down': ffn2_w_down, 'ln_g': ln_g, 'ln_b': ln_b, 'w_in_ab': w_in_ab,
            'w_out_ab': w_out_ab, 's5_lam_re': s5_lam_re, 's5_lam_im': s5_lam_im, 's5_b_re': s5_b_re,
            's5_b_im': s5_b_im, 's5_c_re': s5_c_re, 's5_c_im': s5_c_im, 's5_d': s5_d,
            's5_log_dt': s5_log_dt, 's5_w_out': s5_w_out, 's5_w_gate': s5_w_gate}

def reference(x_prompt, x_sample, cache_k, cache_v, page_table, state_ret, state_s5_re, state_s5_im,
              ffn1_w_gate, ffn1_w_up, ffn1_w_down, ffn2_w_gate, ffn2_w_up, ffn2_w_down, ln_g, ln_b,
              w_in_ab, w_out_ab, s5_lam_re, s5_lam_im, s5_b_re, s5_b_im, s5_c_re, s5_c_im, s5_d,
              s5_log_dt, s5_w_out, s5_w_gate):
    bp, lp, _ = x_prompt.shape
    bs, ls, _ = x_sample.shape
    page = cache_k.shape[2]
    past_len = page_table.shape[1] * page
    pos_p = jnp.arange(lp, dtype=jnp.int32)
    pos_s = past_len + jnp.arange(ls, dtype=jnp.int32)
    xp, xs = x_prompt, x_sample
    k_p, v_p, k_s, v_s, r_p, r_s = [], [], [], [], [], []
    sre_p, sim_p, sre_s, sim_s = [], [], [], []
    for layer in range(DEPTH):
        li = layer // 2
        f1 = (ffn1_w_gate[layer], ffn1_w_up[layer], ffn1_w_down[layer])
        f2 = (ffn2_w_gate[layer], ffn2_w_up[layer], ffn2_w_down[layer])
        xp = layer_norm(DEEPNORM_ALPHA * xp + 0.5 * swiglu(xp, *f1), ln_g[layer, 0], ln_b[layer, 0])
        xs = layer_norm(DEEPNORM_ALPHA * xs + 0.5 * swiglu(xs, *f1), ln_g[layer, 0], ln_b[layer, 0])
        if layer % 2 == 0:
            qa, ka, va, qb, kb, vb, gb = ab_project(xp, pos_p, w_in_ab[li])
            attn = moba_prompt(qa, ka, va, pos_p)
            ret, s_fin = retention(qb, kb, vb, jnp.zeros((bp, B_HEADS, HEAD_DIM, HEAD_DIM), jnp.float32))
            mix_p = ab_merge(attn, ret, gb, w_out_ab[li])
            k_p.append(ka.reshape(bp, lp // page, page, A_HEADS, HEAD_DIM))
            v_p.append(va.reshape(bp, lp // page, page, A_HEADS, HEAD_DIM))
            r_p.append(s_fin)
            qa, ka, va, qb, kb, vb, gb = ab_project(xs, pos_s, w_in_ab[li])
            attn = moba_sample(qa, ka, va, cache_k[li], cache_v[li], page_table, pos_s)
            ret, s_fin = retention(qb, kb, vb, state_ret[li])
            mix_s = ab_merge(attn, ret, gb, w_out_ab[li])
            k_s.append(ka)
            v_s.append(va)
            r_s.append(s_fin)
        else:
            ssm = (s5_lam_re[li], s5_lam_im[li], s5_b_re[li], s5_b_im[li], s5_c_re[li], s5_c_im[li],
                   s5_d[li], s5_log_dt[li], s5_w_out[li], s5_w_gate[li])
            zero = jnp.zeros((bp, S5_GROUPS, S5_STATE), jnp.float32)
            mix_p, a_re, a_im = s5_layer(xp, zero, zero, *ssm)
            sre_p.append(a_re)
            sim_p.append(a_im)
            mix_s, a_re, a_im = s5_layer(xs, state_s5_re[li], state_s5_im[li], *ssm)
            sre_s.append(a_re)
            sim_s.append(a_im)
        xp = layer_norm(DEEPNORM_ALPHA * xp + mix_p, ln_g[layer, 1], ln_b[layer, 1])
        xs = layer_norm(DEEPNORM_ALPHA * xs + mix_s, ln_g[layer, 1], ln_b[layer, 1])
        xp = layer_norm(DEEPNORM_ALPHA * xp + 0.5 * swiglu(xp, *f2), ln_g[layer, 2], ln_b[layer, 2])
        xs = layer_norm(DEEPNORM_ALPHA * xs + 0.5 * swiglu(xs, *f2), ln_g[layer, 2], ln_b[layer, 2])
    new_cache_k_prompt = jnp.stack(k_p)
    new_cache_v_prompt = jnp.stack(v_p)
    new_cache_k_sample = jnp.stack(k_s)
    new_cache_v_sample = jnp.stack(v_s)
    new_state_ret_prompt = jnp.stack(r_p)
    new_state_ret_sample = jnp.stack(r_s)
    new_state_s5_re_prompt = jnp.stack(sre_p)
    new_state_s5_im_prompt = jnp.stack(sim_p)
    new_state_s5_re_sample = jnp.stack(sre_s)
    new_state_s5_im_sample = jnp.stack(sim_s)
    return (xp, xs, new_cache_k_prompt, new_cache_v_prompt, new_cache_k_sample, new_cache_v_sample,
            new_state_ret_prompt, new_state_ret_sample, new_state_s5_re_prompt, new_state_s5_im_prompt,
            new_state_s5_re_sample, new_state_s5_im_sample)


_drawn_inputs = setup_inputs


def setup_inputs(seed=0):
    import zlib

    import numpy as np

    out = dict(_drawn_inputs(seed))
    spreads = {}
    factors = {'cache_k': 4.482, 'cache_v': 3.806, 's5_lam_re': 3.899, 's5_c_re': 4.795, 's5_c_im': 4.826}
    for name, (base, spread) in spreads.items():
        noise = np.random.default_rng([zlib.crc32(name.encode()), seed]).standard_normal(out[name].shape)
        drawn = base * np.exp(spread * noise) if base else spread * noise
        out[name] = __import__('jax').numpy.asarray(drawn.astype(out[name].dtype))
    for name, factor in factors.items():
        out[name] = (out[name] * factor).astype(out[name].dtype)
    return out
```

```python
import math
from contextlib import ExitStack

import concourse.bass as bass
import numpy as np
from concourse import mybir
from concourse.alu_op_type import AluOpType as ALU

F32 = mybir.dt.float32
F32R = mybir.dt.float32r
I32 = mybir.dt.int32
ACT = mybir.ActivationFunctionType
AX_X = mybir.AxisListType.X

P = 128
D_MODEL, SEQ, DEC_BATCH, DEC_SEQ, PAST_LEN, PAGE = 1024, 512, 8, 8, 1024, 128
NS = DEC_BATCH * DEC_SEQ
NT = SEQ + NS
NH = NT // 2
KT = D_MODEL // P
D_FF = ((8 * D_MODEL // 3 + 127) // 128) * 128
FT = D_FF // P
HF = FT // 2
DEPTH = 2
ALPHA = (2 * DEPTH) ** 0.25
LN_EPS = 1e-5
GN_EPS = 1e-6
NEG = -1e30
PT = SEQ // P
HD = 64
HEADS = 8
PAIRS = HEADS // 2
MIX = HEADS * HD


class Count:

    def __init__(self, ctx, nc, name):
        self.h = ctx.enter_context(nc.semaphore(name))
        self.n = 0

    def done(self, k):
        return self.n + k

    def close(self, k):
        self.n += k


class Chain:

    def __init__(self, ctx, nc, name):
        self.h = ctx.enter_context(nc.semaphore(name))
        self.n = 0

    def __call__(self, eng, ins):
        self.n += 1
        ins.then_inc(self.h, 1)
        eng.wait_ge(self.h, self.n)


class Trunk:
    pass


def halves(ap):
    return ap.rearrange("p (n t) -> p n t", n=2)


def open_trunk(ctx, nc):
    T = Trunk()
    T.ctx, T.nc = ctx, nc

    def sb(name, shape, dt=F32):
        return ctx.enter_context(nc.sbuf_tensor(name, shape, dt))

    def count(name):
        return Count(ctx, nc, name)

    T.x = sb("x", [P, KT, NT])
    T.x_hi = sb("x_hi", [P, KT, NT], F32R)
    T.x_lo = sb("x_lo", [P, KT, NT], F32R)
    T.w_raw = sb("w_raw", [P, 2, HF * P])
    T.w_hi = sb("w_hi", [P, 2, HF * P], F32R)
    T.w_lo = sb("w_lo", [P, 2, HF * P], F32R)
    T.ident = sb("ident", [P, P])
    T.ones = sb("ones", [P, P])
    T.ln_gain = sb("ln_gain", [P, DEPTH * 3, KT])
    T.ln_bias = sb("ln_bias", [P, DEPTH * 3, KT])
    T.ps = ctx.enter_context(nc.psum_tensor("ps", [P, 8, 512], F32))
    T.w_loaded = [count("w_loaded0"), count("w_loaded1")]
    T.w_hi_ready = [count("w_hi_ready0"), count("w_hi_ready1")]
    T.w_split = [count("w_split0"), count("w_split1")]
    T.w_used = [count("w_used0"), count("w_used1")]
    T.pieces = 0
    T.const_ready, T.const_loaded = count("const_ready"), count("const_loaded")
    T.silu_done, T.glu_done, T.h_rounded, T.h_done = map(count, ("silu_done", "glu_done", "h_rounded", "h_done"))
    T.res_done, T.acc_added, T.sum_done, T.centred = map(count, ("res_done", "acc_added", "sum_done", "centred"))
    T.squared, T.var_done, T.rstd_ready, T.normed = map(count, ("squared", "var_done", "rstd_ready", "normed"))
    T.affine_done, T.x_rounded, T.x_ready = map(count, ("affine_done", "x_rounded", "x_ready"))
    T.pe_done, T.dve_done, T.act_done, T.pool_done = map(count, ("pe_done", "dve_done", "act_done", "pool_done"))
    T.stored = count("stored")
    T.act_chain = Chain(ctx, nc, "act_chain")
    T.dve_chain = Chain(ctx, nc, "dve_chain")
    T.pool_chain = Chain(ctx, nc, "pool_chain")
    return T



def load_piece(T, sp, slot, u, src, shape=None):
    n = src.shape[1] * src.shape[2]
    dst = T.w_raw[:, slot, 0:n].rearrange("p (a b) -> p a b", a=src.shape[1])
    sp.wait_ge(T.w_split[slot].h, u + 1)
    sp.dma_start(dst, src).then_inc(T.w_loaded[slot].h, 16)


def round_piece(T, act, slot, u, n):
    act.wait_ge(T.w_loaded[slot].h, (u + 1) * 16)
    act.wait_ge(T.w_used[slot].h, u + 1)
    act.activation(T.w_hi[:, slot, 0:n], T.w_raw[:, slot, 0:n], ACT.Copy).then_inc(T.w_hi_ready[slot].h, 1)


def rest_piece(T, dve, slot, u, n):
    dve.wait_ge(T.w_hi_ready[slot].h, u + 1)
    dve.tensor_tensor(T.w_lo[:, slot, 0:n], T.w_raw[:, slot, 0:n], T.w_hi[:, slot, 0:n].bitcast(F32),
                      ALU.subtract).then_inc(T.w_split[slot].h, 1)


def product3(pe, out, w_hi, w_lo, m_hi, m_lo, first, last):
    pe.matmul(out, w_hi, m_hi, start=first, stop=False)
    pe.matmul(out, w_hi, m_lo, start=False, stop=False)
    return pe.matmul(out, w_lo, m_hi, start=False, stop=last)



class Norm:

    def __init__(self, T, row, scale, acc, acc_steps, squares, rstd):
        self.acc_steps = acc_steps
        self.T, self.row, self.acc, self.squares, self.rstd = T, row, acc, squares, rstd
        self.eps = LN_EPS * D_MODEL * scale * scale
        self.mean_ps = T.ps[:, 4:6, 0:NH]
        self.var_ps = T.ps[:, 6:8, 0:NH]

    def tensor(self, pe):
        T = self.T
        pe.wait_ge(T.acc_added.h, T.acc_added.done(self.acc_steps))
        for n in range(2):
            mm = pe.matmul(self.mean_ps[:, n], T.ones[:, :], self.acc[:, n * NH:(n + 1) * NH],
                           start=True, stop=True)
        mm.then_inc(T.sum_done.h, 1)
        for k in range(KT):
            pe.wait_ge(T.squared.h, T.squared.done(k + 1))
            for n in range(2):
                mm = pe.matmul(self.var_ps[:, n], T.ones[:, :], self.squares[:, k % 2, n * NH:(n + 1) * NH],
                               start=(k == 0), stop=(k == KT - 1))
            mm.then_inc(T.var_done.h, 1)

    def scalar(self, act):
        T = self.T
        for k in range(KT):
            act.wait_ge(T.centred.h, T.centred.done(k + 1))
            if k >= 2:
                act.wait_ge(T.var_done.h, T.var_done.done(k - 1))
            act.activation(self.squares[:, k % 2], T.x[:, k], ACT.Square).then_inc(T.squared.h, 1)
        act.wait_ge(T.rstd_ready.h, T.rstd_ready.done(1))
        act.activation(self.rstd[:, :], self.rstd[:, :], ACT.Sqrt).then_inc(T.rstd_ready.h, 1)
        for k in range(KT):
            act.wait_ge(T.normed.h, T.normed.done(k + 1))
            act.activation(T.x[:, k], T.x[:, k], ACT.Identity, bias=T.ln_bias[:, self.row, k:k + 1],
                           scale=T.ln_gain[:, self.row, k:k + 1]).then_inc(T.affine_done.h, 1)

    def vector(self, dve):
        T = self.T
        dve.wait_ge(T.sum_done.h, T.sum_done.done(1))
        for k in range(KT):
            dve.scalar_tensor_tensor(halves(T.x[:, k]), self.mean_ps, -1.0 / D_MODEL, halves(T.x[:, k]),
                                     ALU.mult, ALU.add).then_inc(T.centred.h, 1)
        dve.wait_ge(T.var_done.h, T.var_done.done(KT))
        dve.tensor_scalar(halves(self.rstd[:, :]), self.var_ps, self.eps, None, ALU.add)\
           .then_inc(T.rstd_ready.h, 1)
        dve.wait_ge(T.rstd_ready.h, T.rstd_ready.done(2))
        dve.reciprocal(self.rstd[:, :], self.rstd[:, :]).then_inc(T.rstd_ready.h, 1)
        dve.wait_ge(T.rstd_ready.h, T.rstd_ready.done(3))
        for k in range(KT):
            dve.tensor_tensor(T.x[:, k], T.x[:, k], self.rstd[:, :], ALU.mult).then_inc(T.normed.h, 1)
        for k in range(KT):
            dve.wait_ge(T.x_rounded.h, T.x_rounded.done(k + 1))
            dve.tensor_tensor(T.x_lo[:, k], T.x[:, k], T.x_hi[:, k].bitcast(F32), ALU.subtract)\
               .then_inc(T.x_ready.h, 1)

    def gpsimd(self, pool):
        T = self.T
        for k in range(KT):
            pool.wait_ge(T.affine_done.h, T.affine_done.done(k + 1))
            pool.tensor_copy(T.x_hi[:, k], T.x[:, k]).then_inc(T.x_rounded.h, 1)

    def close(self):
        T = self.T
        for c, k in ((T.acc_added, self.acc_steps), (T.sum_done, 1), (T.squared, KT), (T.var_done, KT), (T.centred, KT),
                     (T.normed, KT), (T.affine_done, KT), (T.rstd_ready, 3), (T.x_rounded, KT), (T.x_ready, KT)):
            c.close(k)



def phase_load(T, x_prompt, x_sample, ln_g, ln_b, ident, first):
    nc = T.nc
    with ExitStack() as ctx:
        rows = ctx.enter_context(nc.sbuf_tensor("x_rows", [P, PT + 1, D_MODEL], F32))
        credit = ctx.enter_context(nc.sbuf_tensor("credit", [P, 8], F32))
        block = ctx.enter_context(nc.Block())
        loaded = T.const_loaded

        @block.sync
        def _(sp):
            sp.dma_start(T.ident[:, :], ident).then_inc(loaded.h, 16)
            for t in range(PT):
                sp.dma_start(rows[:, t], x_prompt[t * P:(t + 1) * P, :]).then_inc(loaded.h, 16)
            sp.dma_start(rows[NS:P, PT], x_sample).then_inc(loaded.h, 16)
            with nc.allow_non_contiguous_dma(reason="layer norm gains and biases, feature-major"):
                sp.dma_start(T.ln_gain[:, :, :], ln_g.rearrange("r (k p) -> p r k", p=P)).then_inc(loaded.h, 16)
                sp.dma_start(T.ln_bias[:, :, :], ln_b.rearrange("r (k p) -> p r k", p=P)).then_inc(loaded.h, 16)
            for slot in range(2):
                load_piece(T, sp, slot, T.pieces, first[slot])

        @block.tensor
        def _(pe):
            pe.wait_ge(loaded.h, (PT + 4) * 16)
            for k in range(KT):
                b = 2 * (k % 4)
                if k >= 4:
                    pe.wait_ge(T.dve_done.h, T.dve_done.done(k - 3))
                for t in range(PT):
                    pe.transpose(T.ps[:, b, t * P:(t + 1) * P], rows[:, t, k * P:(k + 1) * P], T.ident[:, :])
                pe.transpose(T.ps[:, b + 1, 0:NS], rows[NS:P, PT, k * P:(k + 1) * P], T.ident[NS:P, NS:P])\
                  .then_inc(T.pe_done.h, 1)

        @block.vector
        def _(dve):
            dve.memset(T.ones[:, :], 1.0).then_inc(T.const_ready.h, 1)
            for slot in range(2):
                dve.memset(credit[:, slot:slot + 1], 0.0).then_inc(T.w_split[slot].h, 1)
                dve.memset(credit[:, 2 + slot:3 + slot], 0.0).then_inc(T.w_used[slot].h, 1)
                dve.memset(credit[:, 4 + slot:5 + slot], 0.0).then_inc(T.glu_done.h, 1)
                dve.memset(credit[:, 6 + slot:7 + slot], 0.0).then_inc(T.res_done.h, 1)
            dve.wait_ge(loaded.h, (PT + 4) * 16)
            dve.tensor_scalar(T.ln_gain[:, :, :], T.ln_gain[:, :, :], math.sqrt(D_MODEL), None, ALU.mult)\
               .then_inc(T.const_ready.h, 1)
            for k in range(KT):
                b = 2 * (k % 4)
                dve.wait_ge(T.pe_done.h, T.pe_done.done(k + 1))
                T.dve_chain(dve, dve.tensor_copy(T.x[:, k, 0:SEQ], T.ps[:, b, 0:SEQ]))
                T.dve_chain(dve, dve.tensor_copy(T.x[:, k, SEQ:NT], T.ps[:, b + 1, 0:NS]))
                T.dve_chain(dve, dve.tensor_copy(T.x_hi[:, k], T.x[:, k]))
                dve.tensor_tensor(T.x_lo[:, k], T.x[:, k], T.x_hi[:, k].bitcast(F32), ALU.subtract)\
                   .then_inc(T.dve_done.h, 1)
    T.const_loaded.close((PT + 4) * 16)
    T.pe_done.close(KT)
    T.dve_done.close(KT)
    T.glu_done.close(2)
    T.res_done.close(2)


def gate_piece(w, ft):
    return w.rearrange("(k p) f -> p k f", p=P)[:, :, bass.ds(ft * P, P)]


def down_piece(w, half, d):
    return w[half * HF * P:(half + 1) * HF * P, :].rearrange("(f p) d -> p f d", p=P)[:, :, bass.ds(d * P, P)]


def phase_ffn(T, w_gate, w_up, w_down, row, nxt):
    nc = T.nc
    U = T.pieces
    G = KT * P
    D = HF * P
    LOOPED = FT - 2
    DLOOPED = KT - 2
    with ExitStack() as ctx:
        def sb(name, shape, dt=F32):
            return ctx.enter_context(nc.sbuf_tensor(f"{name}_{row}", shape, dt))

        h_hi = sb("h_hi", [P, FT, NT], F32R)
        h_lo = sb("h_lo", [P, FT, NT], F32R)
        gate = sb("gate", [P, 2, NT])
        prod = sb("prod", [P, 2, NT])
        acc, rstd, squares = prod[:, 0], prod[:, 1], gate
        norm = Norm(T, row, 2.0, acc, KT + 1, squares, rstd)
        silu0, glu0, hr0, h0 = T.silu_done.n, T.glu_done.n, T.h_rounded.n, T.h_done.n
        res0, acc0 = T.res_done.n, T.acc_added.n
        block = ctx.enter_context(nc.Block())

        @block.sync
        def _(sp):
            with sp.Fori(1, FT) as ft:
                for slot, w in ((0, w_gate), (1, w_up)):
                    src = gate_piece(w, ft)
                    load_piece(T, sp, slot, U + ft, src)
            with sp.Fori(0, KT) as d:
                for slot in range(2):
                    src = down_piece(w_down, slot, d)
                    load_piece(T, sp, slot, U + FT + d, src)
            for slot in range(2):
                if nxt:
                    load_piece(T, sp, slot, U + FT + KT, nxt[slot])

        @block.tensor
        def _(pe):
            def gate_up(ft, j):
                pe.wait_ge(T.glu_done.h, ft + (glu0 - 1))
                for slot in range(2):
                    pe.wait_ge(T.w_split[slot].h, ft + (U + 2))
                    for n in range(2):
                        for k in range(KT):
                            cols = slice(n * NH, (n + 1) * NH)
                            mm = product3(pe, T.ps[:, 4 * j + 2 * slot + n, 0:NH],
                                          T.w_hi[:, slot, k * P:(k + 1) * P], T.w_lo[:, slot, k * P:(k + 1) * P],
                                          T.x_hi[:, k, cols], T.x_lo[:, k, cols], k == 0, k == KT - 1)
                    mm.then_inc(T.w_used[slot].h, 1)

            def down(d, j):
                pe.wait_ge(T.res_done.h, d + (res0 - 1))
                for slot in range(2):
                    pe.wait_ge(T.w_split[slot].h, d + (U + FT + 2))
                    for n in range(2):
                        for f in range(HF):
                            cols = slice(n * NH, (n + 1) * NH)
                            ft = slot * HF + f
                            mm = product3(pe, T.ps[:, 2 * j + n, 0:NH],
                                          T.w_hi[:, slot, f * P:(f + 1) * P], T.w_lo[:, slot, f * P:(f + 1) * P],
                                          h_hi[:, ft, cols], h_lo[:, ft, cols], ft == 0, ft == FT - 1)
                    mm.then_inc(T.w_used[slot].h, 1)

            with pe.Fori(0, FT, 2) as ft:
                for j in range(2):
                    gate_up(ft + j, j)
            pe.wait_ge(T.h_done.h, h0 + FT)
            with pe.Fori(0, KT, 2) as d:
                for j in range(2):
                    down(d + j, j)
            norm.tensor(pe)

        @block.scalar
        def _(act):
            def step(ft, j, n):
                for slot in range(2):
                    round_piece(T, act, slot, ft + (U + 1), n)
                act.wait_ge(T.w_used[1].h, ft + (U + 2))
                act.activation(halves(gate[:, j]), T.ps[:, 4 * j:4 * j + 2, 0:NH], ACT.Silu)\
                   .then_inc(T.silu_done.h, 1)

            for slot in range(2):
                round_piece(T, act, slot, U, G)
            with act.Fori(0, LOOPED, 2) as ft:
                for j in range(2):
                    step(ft + j, j, G)
            step(FT - 2, 0, G)
            step(FT - 1, 1, D)
            with act.Fori(1, KT) as d:
                for slot in range(2):
                    round_piece(T, act, slot, d + (U + FT), D)
            norm.scalar(act)

        @block.vector
        def _(dve):
            def step(ft, j, n):
                for slot in range(2):
                    rest_piece(T, dve, slot, ft + (U + 1), n)
                dve.wait_ge(T.silu_done.h, ft + (silu0 + 1))
                dve.tensor_tensor(halves(prod[:, j]), halves(gate[:, j]), T.ps[:, 4 * j + 2:4 * j + 4, 0:NH],
                                  ALU.mult).then_inc(T.glu_done.h, 1)
                dve.wait_ge(T.glu_done.h, ft + (glu0 + 1))
                hi = h_hi[:, bass.ds(ft, 1), :].rearrange("p a t -> p (a t)")
                lo = h_lo[:, bass.ds(ft, 1), :].rearrange("p a t -> p (a t)")
                dve.tensor_copy(hi, prod[:, j]).then_inc(T.h_rounded.h, 1)
                dve.wait_ge(T.h_rounded.h, ft + (hr0 + 1))
                dve.tensor_tensor(lo, prod[:, j], hi.bitcast(F32), ALU.subtract).then_inc(T.h_done.h, 1)

            for slot in range(2):
                rest_piece(T, dve, slot, U, G)
            with dve.Fori(0, LOOPED, 2) as ft:
                for j in range(2):
                    step(ft + j, j, G)
            step(FT - 2, 0, G)
            step(FT - 1, 1, D)
            dve.wait_ge(T.h_done.h, h0 + FT)
            dve.memset(acc, 0.0).then_inc(T.acc_added.h, 1)

            def add(d, j):
                dve.wait_ge(T.w_used[1].h, d + (U + FT + 2))
                xd = T.x[:, bass.ds(d, 1), :].rearrange("p a t -> p (a t)")
                dve.scalar_tensor_tensor(halves(xd), halves(xd), 2.0 * ALPHA, T.ps[:, 2 * j:2 * j + 2, 0:NH],
                                         ALU.mult, ALU.add).then_inc(T.res_done.h, 1)
                dve.wait_ge(T.res_done.h, d + (res0 + 1))
                dve.wait_ge(T.acc_added.h, d + (acc0 + 1))
                dve.tensor_tensor(acc, acc, xd, ALU.add).then_inc(T.acc_added.h, 1)

            with dve.Fori(0, DLOOPED, 2) as d:
                for j in range(2):
                    for slot in range(2):
                        rest_piece(T, dve, slot, d + (j + U + FT + 1), D)
                    add(d + j, j)
            for slot in range(2):
                rest_piece(T, dve, slot, U + FT + KT - 1, D)
            add(KT - 2, 0)
            add(KT - 1, 1)
            norm.vector(dve)

        @block.gpsimd
        def _(pool):
            norm.gpsimd(pool)
    for c, k in ((T.silu_done, FT), (T.glu_done, FT), (T.h_rounded, FT), (T.h_done, FT), (T.res_done, KT)):
        c.close(k)
    T.pieces += FT + KT
    norm.close()


def phase_store(T, y_prompt, y_sample):
    nc = T.nc
    with ExitStack() as ctx:
        rows = ctx.enter_context(nc.sbuf_tensor("y_rows", [P, PT + 1, D_MODEL], F32))
        block = ctx.enter_context(nc.Block())
        banks = [(t, q) for t in range(PT + 1) for q in range(2)]

        @block.tensor
        def _(pe):
            for i, (t, q) in enumerate(banks):
                m = P if t < PT else NS
                if i >= 8:
                    pe.wait_ge(T.dve_done.h, T.dve_done.done(i - 7))
                for k in range(4):
                    mm = pe.transpose(T.ps[0:m, i % 8, k * P:(k + 1) * P],
                                      T.x[:, 4 * q + k, t * P:t * P + m], T.ident[:, :])
                mm.then_inc(T.pe_done.h, 1)

        @block.vector
        def _(dve):
            for i, (t, q) in enumerate(banks):
                m = P if t < PT else NS
                dve.wait_ge(T.pe_done.h, T.pe_done.done(i + 1))
                dve.tensor_copy(rows[0:m, t, q * 512:(q + 1) * 512], T.ps[0:m, i % 8, 0:512])\
                   .then_inc(T.dve_done.h, 1)

        @block.sync
        def _(sp):
            for t in range(PT + 1):
                sp.wait_ge(T.dve_done.h, T.dve_done.done(2 * t + 2))
                if t < PT:
                    sp.dma_start(y_prompt[t * P:(t + 1) * P, :], rows[:, t]).then_inc(T.stored.h, 16)
                else:
                    sp.dma_start(y_sample, rows[0:NS, t]).then_inc(T.stored.h, 16)
            sp.wait_ge(T.stored.h, T.stored.done((PT + 1) * 16))
    T.pe_done.close(len(banks))
    T.dve_done.close(len(banks))
    T.stored.close((PT + 1) * 16)



SECTIONS = 7
Q_A, K_A, V_A, Q_B, K_B, V_B, G_B = range(SECTIONS)
ROPED = (Q_A, K_A, Q_B, K_B)
TT = PT + 1
KPP = 2
SECTION_PIECES = KT // KPP


def tile_cols(t):
    return slice(t * P, (t + 1) * P) if t < PT else slice(NT - P, NT)


def in_piece(w_in, g):
    s, q = divmod(g, SECTION_PIECES)
    return w_in.rearrange("(k p) c -> p k c", p=P)[:, q * KPP:(q + 1) * KPP, s * MIX:(s + 1) * MIX]


def open_mix(ctx, nc, M, part):

    def sb(name, shape, dt=F32):
        return ctx.enter_context(nc.sbuf_tensor(name, shape, dt))

    if part == "attention":
        M.qaT, M.kaT = sb("qaT", [P, PAIRS, NT]), sb("kaT", [P, PAIRS, NT])
        M.va = sb("va", [P, TT, MIX])
    else:
        M.qbT, M.kbT = sb("qbT", [P, PAIRS, NT]), sb("kbT", [P, PAIRS, NT])
        M.kb, M.vb, M.gb = (sb(n, [P, TT, MIX]) for n in ("kb", "vb", "gb"))


def phase_project(T, M, w_in, rope_cos, rope_sin, decay_q, decay_k, O, nxt):
    nc = T.nc
    U = T.pieces
    NP = SECTIONS * SECTION_PIECES
    N = KPP * MIX
    staged, roped, turned, moved, k_stored, v_stored, tables = (
        Count(T.ctx, nc, n) for n in ("staged", "roped", "turned", "moved", "k_stored", "v_stored", "tables_loaded"))
    with ExitStack() as ctx:
        def sb(name, shape, dt=F32):
            return ctx.enter_context(nc.sbuf_tensor(name, shape, dt))

        stage, rot = sb("stage", [P, TT, MIX]), sb("rot", [P, TT, MIX])
        by_cos, by_sin = sb("by_cos", [P, MIX]), sb("by_sin", [P, MIX])
        cos, sin = sb("cos", [P, TT, HD // 2]), sb("sin", [P, TT, 2, HD // 2])
        dq, dk = sb("dq", [P, TT, HEADS]), sb("dk", [P, TT, HEADS])
        block = ctx.enter_context(nc.Block())

        def bank(s, t):
            return (TT * s + t) % 6

        @block.sync
        def _(sp):
            sp.dma_start(cos[:, :, :], rope_cos).then_inc(tables.h, 16)
            sp.dma_start(sin[:, :, :, :], rope_sin).then_inc(tables.h, 16)
            sp.dma_start(dq[:, :, :], decay_q).then_inc(tables.h, 16)
            sp.dma_start(dk[:, :, :], decay_k).then_inc(tables.h, 16)
            for g in range(2, NP):
                load_piece(T, sp, g % 2, U + g // 2, in_piece(w_in, g))
            for slot in range(2):
                load_piece(T, sp, slot, U + NP // 2, nxt[slot])

        @block.tensor
        def _(pe):
            def turn(r):
                src = M.kb if ROPED[r] == K_B else rot
                for t in range(TT):
                    pe.wait_ge(roped.h, TT * r + t + 1)
                    if TT * r + t >= 2:
                        pe.wait_ge(moved.h, TT * r + t - 1)
                    for p in range(PAIRS):
                        lo = 0 if t < PT else NS
                        mm = pe.transpose(T.ps[:, 6 + t % 2, p * P:p * P + P - lo],
                                          src[lo:P, t, p * P:(p + 1) * P], T.ident[lo:P, lo:P])
                    mm.then_inc(turned.h, 1)

            for g in range(NP):
                s, q = divmod(g, SECTION_PIECES)
                slot = g % 2
                pe.wait_ge(T.w_split[slot].h, U + g // 2 + 2)
                for t in range(TT):
                    if q == 0 and TT * s + t >= 6:
                        pe.wait_ge(staged.h, TT * s + t - 5)
                    for k in range(KPP):
                        cols = slice(k * MIX, (k + 1) * MIX)
                        kk = q * KPP + k
                        x_hi, x_lo = T.x_hi[:, kk, tile_cols(t)], T.x_lo[:, kk, tile_cols(t)]
                        w_hi, w_lo = T.w_hi[:, slot, cols], T.w_lo[:, slot, cols]
                        out = T.ps[:, bank(s, t), 0:MIX]
                        pe.matmul(out, x_hi, w_hi, start=(kk == 0), stop=False)
                        pe.matmul(out, x_hi, w_lo, start=False, stop=False)
                        mm = pe.matmul(out, x_lo, w_hi, start=False, stop=(kk == KT - 1))
                mm.then_inc(T.w_used[slot].h, 1)
                if q == 2 and s - 1 in ROPED:
                    turn(ROPED.index(s - 1))

        @block.scalar
        def _(act):
            def empty(s):
                act.wait_ge(T.w_used[1].h, U + (4 * s + 3) // 2 + 2)
                dst = {V_A: M.va, V_B: M.vb, G_B: M.gb}.get(s, stage)
                for t in range(TT):
                    if s in ROPED and s > 0:
                        act.wait_ge(roped.h, TT * (ROPED.index(s) - 1) + t + 1)
                    act.activation(dst[:, t], T.ps[:, bank(s, t), 0:MIX], ACT.Silu if s == G_B else ACT.Copy)\
                       .then_inc(staged.h, 1)

            def move(r):
                dst = (M.qaT, M.kaT, M.qbT, M.kbT)[r]
                for t in range(TT):
                    m = P if t < PT else NS
                    act.wait_ge(turned.h, TT * r + t + 1)
                    act.activation(dst[:, :, t * P:t * P + m],
                                   T.ps[:, 6 + t % 2, :].rearrange("p (a t) -> p a t", a=PAIRS)[:, :, 0:m],
                                   ACT.Copy).then_inc(moved.h, 1)

            round_piece(T, act, 0, U, N)
            for g in range(NP):
                if g + 1 < NP:
                    round_piece(T, act, (g + 1) % 2, U + (g + 1) // 2, N)
                s, q = divmod(g, SECTION_PIECES)
                if q == 2 and s - 1 in ROPED:
                    move(ROPED.index(s - 1))
                if q == 3:
                    empty(s)

        @block.vector
        def _(dve):
            def rotate(s, t):
                r = ROPED.index(s)
                dve.wait_ge(staged.h, TT * s + t + 1)
                heads = stage[:, t].rearrange("p (h j d) -> p h j d", h=HEADS, j=2)
                sums = by_sin[:, :].rearrange("p (h j d) -> p h j d", h=HEADS, j=2)
                flat = [P, HEADS * 2, HD // 2]
                dve.tensor_tensor(by_cos[:, :].rearrange("p (h d) -> p h d", d=HD // 2),
                                  stage[:, t].rearrange("p (h d) -> p h d", d=HD // 2),
                                  cos[:, t:t + 1, :].to_broadcast(flat), ALU.mult)
                for j in range(2):
                    last = dve.tensor_tensor(sums[:, :, j], heads[:, :, 1 - j],
                                             sin[:, t, j:j + 1, :].to_broadcast([P, HEADS, HD // 2]), ALU.mult)
                T.dve_chain(dve, last)
                dst = M.kb if s == K_B else rot
                if r and dst is rot:
                    dve.wait_ge(turned.h, TT * (r - 1) + t + 1)
                    if s == Q_B:
                        dve.wait_ge(k_stored.h, 16 * TT)
                last = dve.tensor_tensor(dst[:, t], by_cos[:, :], by_sin[:, :], ALU.add)
                if s in (Q_B, K_B):
                    T.dve_chain(dve, last)
                    d = (dq if s == Q_B else dk)[:, t, :].unsqueeze(2).to_broadcast([P, HEADS, HD])
                    last = dve.tensor_tensor(dst[:, t].rearrange("p (h d) -> p h d", h=HEADS),
                                             dst[:, t].rearrange("p (h d) -> p h d", h=HEADS), d, ALU.mult)
                last.then_inc(roped.h, 1)
                dve.wait_ge(roped.h, TT * r + t + 1)

            dve.wait_ge(tables.h, 64)
            rest_piece(T, dve, 0, U, N)
            for g in range(NP):
                if g + 1 < NP:
                    rest_piece(T, dve, (g + 1) % 2, U + (g + 1) // 2, N)
                s, q = divmod(g, SECTION_PIECES)
                if s - 1 in ROPED and q < 2:
                    for t in (0, 1) if q == 0 else (2, 3, 4):
                        rotate(s - 1, t)

        @block.gpsimd
        def _(pool):
            for stored, src, wait, of_prompt, of_sample in (
                    (k_stored, rot, lambda t: (roped.h, TT + t + 1), O["k_prompt"], O["k_sample"]),
                    (v_stored, M.va, lambda t: (staged.h, TT * V_A + t + 1), O["v_prompt"], O["v_sample"])):
                for t in range(TT):
                    pool.wait_ge(*wait(t))
                    if t < PT:
                        pool.dma_start(of_prompt[t * P:(t + 1) * P, :], src[:, t]).then_inc(stored.h, 16)
                    else:
                        pool.dma_start(of_sample, src[NS:P, t]).then_inc(stored.h, 16)
            pool.wait_ge(k_stored.h, TT * 16)
            pool.wait_ge(v_stored.h, TT * 16)
    T.pieces += NP // 2



def phase_attend_prompt(T, M, causal_in):
    nc = T.nc
    N = PT * HEADS
    scored, maxed, expd, turned, moved, valued, normed, oturned, rounded, rested, loaded, shifted = (
        Count(T.ctx, nc, "pa_" + n) for n in (
            "scored", "maxed", "expd", "turned", "moved", "valued", "normed", "oturned", "rounded", "rested",
            "loaded", "shifted"))
    with ExitStack() as ctx:
        def sb(name, shape, dt=F32):
            return ctx.enter_context(nc.sbuf_tensor(name, shape, dt))

        prob, prob_t = sb("prob", [P, 2, SEQ]), sb("prob_t", [P, 2, SEQ])
        out = sb("attn_out", [P, 2, MIX])
        causal = sb("causal", [P, P])
        top, shift, total, inv = (sb(n, [P, N]) for n in ("top", "shift", "total", "inv"))
        block = ctx.enter_context(nc.Block())
        jobs = [(i, h) for i in range(PT) for h in range(HEADS)]
        half = [slice(0, HD), slice(HD, P)]

        @block.sync
        def _(sp):
            sp.dma_start(causal[:, :], causal_in).then_inc(loaded.h, 16)

        @block.tensor
        def _(pe):
            def score(n):
                i, h = jobs[n]
                if n >= 2:
                    pe.wait_ge(expd.h, n - 1)
                rows = half[h % 2]
                pe.matmul(T.ps[:, n % 2, 0:(i + 1) * P], M.qaT[rows, h // 2, i * P:(i + 1) * P],
                          M.kaT[rows, h // 2, 0:(i + 1) * P], start=True, stop=True).then_inc(scored.h, 1)

            def turn(n):
                i, h = jobs[n]
                pe.wait_ge(expd.h, n + 1)
                if n >= 2:
                    pe.wait_ge(moved.h, n - 1)
                for j in range(i + 1):
                    mm = pe.transpose(T.ps[:, 2 + n % 2, j * P:(j + 1) * P], prob[:, n % 2, j * P:(j + 1) * P],
                                      T.ident[:, :])
                mm.then_inc(turned.h, 1)

            def value(n):
                i, h = jobs[n]
                pe.wait_ge(moved.h, n + 1)
                if h == 0 and i >= 2:
                    pe.wait_ge(normed.h, i - 1)
                for j in range(i + 1):
                    mm = pe.matmul(T.ps[:, 4 + i % 2, h * HD:(h + 1) * HD], prob_t[:, n % 2, j * P:(j + 1) * P],
                                   M.va[:, j, h * HD:(h + 1) * HD], start=(h == 0 and j == 0),
                                   stop=(h == HEADS - 1 and j == i), skip_group_check=True)
                mm.then_inc(valued.h, 1)

            def turn_out(i):
                pe.wait_ge(normed.h, i + 1)
                if i >= 2:
                    pe.wait_ge(rested.h, i - 1)
                for p in range(PAIRS):
                    mm = pe.transpose(T.ps[:, 6 + i % 2, p * P:(p + 1) * P], out[:, i % 2, p * P:(p + 1) * P],
                                      T.ident[:, :])
                mm.then_inc(oturned.h, 1)

            for n in range(N + 2):
                if n < N:
                    score(n)
                if 1 <= n <= N:
                    turn(n - 1)
                if n >= 2:
                    value(n - 2)
                if n >= HEADS + 4 and (n - 4) % HEADS == 0:
                    turn_out((n - 4) // HEADS - 1)
            turn_out(PT - 1)

        @block.vector
        def _(dve):
            dve.wait_ge(loaded.h, 16)

            def rest(i):
                dve.wait_ge(rounded.h, i + 1)
                cols = slice(i * P, (i + 1) * P)
                dve.tensor_tensor(T.x_lo[:, 0:PAIRS, cols],
                                  T.ps[:, 6 + i % 2, :].rearrange("p (a t) -> p a t", a=PAIRS),
                                  T.x_hi[:, 0:PAIRS, cols].bitcast(F32), ALU.subtract).then_inc(rested.h, 1)

            def norm(i):
                dve.wait_ge(valued.h, HEADS * (i + 1))
                cols = slice(HEADS * i, HEADS * (i + 1))
                T.dve_chain(dve, dve.reciprocal(inv[:, cols], total[:, cols]))
                if i >= 2:
                    dve.wait_ge(oturned.h, i - 1)
                dve.tensor_tensor(out[:, i % 2].rearrange("p (h d) -> p h d", h=HEADS),
                                  T.ps[:, 4 + i % 2, :].rearrange("p (h d) -> p h d", h=HEADS),
                                  inv[:, cols].unsqueeze(2).to_broadcast([P, HEADS, HD]), ALU.mult)\
                   .then_inc(normed.h, 1)

            for n in range(N):
                i, h = jobs[n]
                dve.wait_ge(scored.h, n + 1)
                diag = T.ps[:, n % 2, i * P:(i + 1) * P]
                T.dve_chain(dve, dve.tensor_tensor(diag, diag, causal[:, :], ALU.add))
                T.dve_chain(dve, dve.reduce_max(top[:, n:n + 1], T.ps[:, n % 2, 0:(i + 1) * P], AX_X))
                dve.tensor_scalar(shift[:, n:n + 1], top[:, n:n + 1], -HD ** -0.5, None, ALU.mult)\
                   .then_inc(maxed.h, 1)
                if i and h == 2:
                    norm(i - 1)
                if i and h == 5:
                    rest(i - 1)
            norm(PT - 1)
            rest(PT - 1)

        @block.scalar
        def _(act):
            def move(n):
                i, h = jobs[n]
                act.wait_ge(turned.h, n + 1)
                if n >= 2:
                    act.wait_ge(valued.h, n - 1)
                act.activation(prob_t[:, n % 2, 0:(i + 1) * P], T.ps[:, 2 + n % 2, 0:(i + 1) * P], ACT.Copy)\
                   .then_inc(moved.h, 1)

            def round_out(i):
                act.wait_ge(oturned.h, i + 1)
                act.activation(T.x_hi[:, 0:PAIRS, i * P:(i + 1) * P],
                               T.ps[:, 6 + i % 2, :].rearrange("p (a t) -> p a t", a=PAIRS), ACT.Copy)\
                   .then_inc(rounded.h, 1)

            for n in range(N):
                i, h = jobs[n]
                act.wait_ge(maxed.h, n + 1)
                if n >= 2:
                    act.wait_ge(turned.h, n - 1)
                act.activation(prob[:, n % 2, 0:(i + 1) * P], T.ps[:, n % 2, 0:(i + 1) * P], ACT.Exp,
                               bias=shift[:, n:n + 1], scale=HD ** -0.5, accum_out=total[:, n:n + 1])\
                   .then_inc(expd.h, 1)
                if n >= 1:
                    move(n - 1)
                if i and h == 5:
                    round_out(i - 1)
            move(N - 1)
            round_out(PT - 1)



class GroupNorm:

    def __init__(self, T, M, ctx, name):
        def sb(part, shape):
            return ctx.enter_context(T.nc.sbuf_tensor(name + part, shape, F32))

        self.T, self.M = T, M
        self.ready, self.rooted, self.gated, self.turned, self.rounded, self.rested = (
            Count(T.ctx, T.nc, name + n) for n in ("ready", "rooted", "gated", "turned", "rounded", "rested"))
        self.centred, self.squares, self.gate = (sb(n, [P, MIX]) for n in ("centred", "squares", "gate"))
        self.mean, self.var = sb("mean", [P, HEADS]), sb("var", [P, HEADS])

    def vector(self, dve, n, ps, t):
        T, M = self.T, self.M
        r = slice(0 if t < PT else NS, P)
        rows = P - r.start
        wide = [rows, HEADS, HD]

        def heads(ap):
            return ap.rearrange("p (h d) -> p h d", h=HEADS)

        def each(ap):
            return ap.unsqueeze(2).to_broadcast(wide)

        mean, var, centred, squares = self.mean[r, :], self.var[r, :], self.centred[r, :], self.squares[r, :]
        T.dve_chain(dve, dve.tensor_reduce(mean, heads(ps[r, :]), AX_X, ALU.add))
        T.dve_chain(dve, dve.tensor_scalar(mean, mean, -1.0 / HD, None, ALU.mult))
        T.dve_chain(dve, dve.tensor_tensor(heads(centred), heads(ps[r, :]), each(mean), ALU.add))
        T.dve_chain(dve, dve.tensor_tensor(squares, centred, centred, ALU.mult))
        T.dve_chain(dve, dve.tensor_reduce(var, heads(squares), AX_X, ALU.add))
        dve.tensor_scalar(var, var, 1.0 / HD, GN_EPS, ALU.mult, ALU.add).then_inc(self.ready.h, 1)
        dve.wait_ge(self.rooted.h, n + 1)
        T.dve_chain(dve, dve.reciprocal(var, var))
        T.dve_chain(dve, dve.tensor_tensor(heads(centred), heads(centred), each(var), ALU.mult))
        if n >= 1:
            dve.wait_ge(self.turned.h, n)
        dve.tensor_tensor(self.gate[r, :], centred, M.gb[r, t], ALU.mult).then_inc(self.gated.h, 1)

    def rest(self, dve, n, t):
        T = self.T
        m = P if t < PT else NS
        dve.wait_ge(self.rounded.h, n + 1)
        cols = slice(t * P, t * P + m)
        dve.tensor_tensor(T.x_lo[:, PAIRS:KT, cols],
                          T.ps[:, 6 + n % 2, :].rearrange("p (a t) -> p a t", a=PAIRS)[:, :, 0:m],
                          T.x_hi[:, PAIRS:KT, cols].bitcast(F32), ALU.subtract).then_inc(self.rested.h, 1)

    def scalar(self, act, n, t):
        T = self.T
        r = slice(0 if t < PT else NS, P)
        act.wait_ge(self.ready.h, n + 1)
        act.activation(self.var[r, :], self.var[r, :], ACT.Sqrt).then_inc(self.rooted.h, 1)

    def round(self, act, n, t):
        T = self.T
        m = P if t < PT else NS
        act.wait_ge(self.turned.h, n + 1)
        act.activation(T.x_hi[:, PAIRS:KT, t * P:t * P + m],
                       T.ps[:, 6 + n % 2, :].rearrange("p (a t) -> p a t", a=PAIRS)[:, :, 0:m], ACT.Copy)\
           .then_inc(self.rounded.h, 1)

    def tensor(self, pe, n, t):
        T = self.T
        lo = 0 if t < PT else NS
        pe.wait_ge(self.gated.h, n + 1)
        if n >= 2:
            pe.wait_ge(self.rested.h, n - 1)
        for p in range(PAIRS):
            mm = pe.transpose(T.ps[:, 6 + n % 2, p * P:p * P + P - lo], self.gate[lo:P, p * P:(p + 1) * P],
                              T.ident[lo:P, lo:P])
        mm.then_inc(self.turned.h, 1)


def phase_retain_prompt(T, M, keep_in, power_in, state_out):
    nc = T.nc
    inner, masked, kept, copied, outed, loaded, stored = (
        Count(T.ctx, nc, "rp_" + n) for n in ("inner", "masked", "kept", "copied", "outed", "loaded", "stored"))
    with ExitStack() as ctx:
        def sb(name, shape, dt=F32):
            return ctx.enter_context(nc.sbuf_tensor(name, shape, dt))

        keep = sb("keep", [P, P])
        power = sb("power", [P, PAIRS])
        weight = sb("weight", [P, 2, HEADS // 2, P])
        state = sb("state", [P, PAIRS, P])
        final = sb("final", [P, PAIRS, HD])
        gn = GroupNorm(T, M, ctx, "rp_gn_")
        block = ctx.enter_context(nc.Block())
        half = [slice(0, HD), slice(HD, P)]
        sums = T.ps[:, 4, :].rearrange("p (a e) -> p a e", a=PAIRS)

        @block.sync
        def _(sp):
            sp.dma_start(keep[:, :], keep_in).then_inc(loaded.h, 16)
            sp.dma_start(power[:, :], power_in).then_inc(loaded.h, 16)
            sp.wait_ge(copied.h, PT + 1)
            for s in range(2):
                sp.dma_start(state_out.rearrange("(a s) d e -> s d a e", s=2)[s], final[half[s], :, :])\
                  .then_inc(stored.h, 16)
            sp.wait_ge(stored.h, 32)

        @block.tensor
        def _(pe):
            for i in range(PT):
                cols = slice(i * P, (i + 1) * P)
                for g in range(2):
                    if i:
                        pe.wait_ge(masked.h, 2 * i + g - 1)
                    for j in range(HEADS // 2):
                        h = 2 * j + g
                        rows = half[g]
                        mm = pe.matmul(T.ps[:, g, j * P:(j + 1) * P], M.kbT[rows, h // 2, cols],
                                       M.qbT[rows, h // 2, cols], start=True, stop=True)
                    mm.then_inc(inner.h, 1)
                if i >= 2:
                    pe.wait_ge(gn.gated.h, i - 1)
                out = T.ps[:, 2 + i % 2, :]
                if i:
                    pe.wait_ge(copied.h, i + 1)
                    for p in range(PAIRS):
                        pe.matmul(out[:, p * P:(p + 1) * P], M.qbT[:, p, cols], state[:, p, :],
                                  start=(p == 0), stop=False, skip_group_check=True)
                pe.wait_ge(masked.h, 2 * i + 2)
                for h in range(HEADS):
                    mm = pe.matmul(out[:, h * HD:(h + 1) * HD], weight[:, h % 2, h // 2, :],
                                   M.vb[:, i, h * HD:(h + 1) * HD], start=(i == 0 and h == 0),
                                   stop=(h == HEADS - 1), skip_group_check=True)
                mm.then_inc(outed.h, 1)
                for p in range(PAIRS):
                    mm = pe.matmul(sums[:, p, :], M.kb[:, i, p * P:(p + 1) * P], M.vb[:, i, p * P:(p + 1) * P],
                                   start=(i == 0 and p == 0), stop=(i == PT - 1 and p == PAIRS - 1),
                                   skip_group_check=True)
                mm.then_inc(kept.h, 1)
                if i:
                    gn.tensor(pe, i - 1, i - 1)
            gn.tensor(pe, PT - 1, PT - 1)

        @block.vector
        def _(dve):
            dve.memset(state[:, :, :], 0.0).then_inc(copied.h, 1)
            dve.wait_ge(copied.h, 1)
            dve.wait_ge(loaded.h, 32)
            for i in range(PT):
                for g in range(2):
                    dve.wait_ge(inner.h, 2 * i + g + 1)
                    if i:
                        dve.wait_ge(outed.h, i)
                    dve.tensor_tensor(weight[:, g], T.ps[:, g, :].rearrange("p (h t) -> p h t", h=HEADS // 2),
                                      keep[:, :].unsqueeze(1).to_broadcast([P, HEADS // 2, P]), ALU.mult)\
                       .then_inc(masked.h, 1)
                dve.wait_ge(kept.h, i + 1)
                for s in range(2):
                    if i < PT - 1:
                        last = dve.tensor_copy(state[half[s], :, half[s]], sums[half[s], :, half[s]])
                    else:
                        last = dve.tensor_tensor(final[half[s], :, :], sums[half[s], :, half[s]],
                                                 power[half[s], :].unsqueeze(2).to_broadcast([HD, PAIRS, HD]),
                                                 ALU.mult)
                last.then_inc(copied.h, 1)
                gn.vector(dve, i, T.ps[:, 2 + i % 2, :], i)
                if i:
                    gn.rest(dve, i - 1, i - 1)
            gn.rest(dve, PT - 1, PT - 1)

        @block.scalar
        def _(act):
            for i in range(PT):
                gn.scalar(act, i, i)
                if i:
                    gn.round(act, i - 1, i - 1)
            gn.round(act, PT - 1, PT - 1)


def phase_retain_samples(T, M, state_in, keep_in, select_in, power_in, state_out):
    nc = T.nc
    B = DEC_BATCH
    names = ("loaded", "zeroed", "spread", "inner", "masked", "outed", "picked", "updated", "added", "stored")
    loaded, zeroed, spread, inner, masked, outed, picked, updated, added, stored = (
        Count(T.ctx, nc, "rs_" + n) for n in names)
    with ExitStack() as ctx:
        def sb(name, shape, dt=F32):
            return ctx.enter_context(nc.sbuf_tensor(name, shape, dt))

        keep = sb("keep_s", [P, NS])
        select = sb("select", [P, B])
        power = sb("power_s", [P, PAIRS])
        state = sb("state_s", [P, B * PAIRS, P])
        q_of = sb("q_of", [P, PAIRS, B, NS])
        weight = sb("weight_s", [P, 2, PAIRS, NS])
        v_of = sb("v_of", [P, 2, MIX])
        gn = GroupNorm(T, M, ctx, "rs_gn_")
        block = ctx.enter_context(nc.Block())
        half = [slice(0, HD), slice(HD, P)]
        tok = slice(NS, P)

        @block.sync
        def _(sp):
            sp.dma_start(keep[tok, :], keep_in).then_inc(loaded.h, 16)
            sp.dma_start(select[tok, :], select_in).then_inc(loaded.h, 16)
            sp.dma_start(power[:, :], power_in).then_inc(loaded.h, 16)
            sp.wait_ge(zeroed.h, 1)
            for s in range(2):
                sp.dma_start(state[half[s], :, half[s]],
                             state_in.rearrange("b (a s) d e -> s d (b a) e", s=2)[s]).then_inc(loaded.h, 16)
            sp.wait_ge(added.h, B)
            for s in range(2):
                sp.dma_start(state_out.rearrange("b (a s) d e -> s d (b a) e", s=2)[s],
                             state[half[s], :, half[s]]).then_inc(stored.h, 16)
            sp.wait_ge(stored.h, 32)

        @block.tensor
        def _(pe):
            for h in range(HEADS):
                rows = half[h % 2]
                mm = pe.matmul(T.ps[tok, (0, 4)[h % 2], h // 2 * NS:(h // 2 + 1) * NS], M.kbT[rows, h // 2, SEQ:NT],
                               M.qbT[rows, h // 2, SEQ:NT], start=True, stop=True)
            mm.then_inc(inner.h, 1)
            pe.wait_ge(spread.h, B)
            pe.wait_ge(loaded.h, 5 * 16)
            for p in range(PAIRS):
                for b in range(B):
                    pe.matmul(T.ps[tok, 1, p * P:(p + 1) * P], q_of[:, p, b, :], state[:, PAIRS * b + p, :],
                              start=(p == 0 and b == 0), stop=False, skip_group_check=True)
            pe.wait_ge(masked.h, 1)
            for h in range(HEADS):
                mm = pe.matmul(T.ps[tok, 1, h * HD:(h + 1) * HD], weight[tok, h % 2, h // 2, :],
                               M.vb[tok, PT, h * HD:(h + 1) * HD], start=False, stop=(h == HEADS - 1),
                               skip_group_check=True)
            mm.then_inc(outed.h, 1)
            for b in range(B):
                pe.wait_ge(picked.h, b + 1)
                if b >= 2:
                    pe.wait_ge(added.h, b - 1)
                for p in range(PAIRS):
                    mm = pe.matmul(T.ps[:, 2 + b % 2, p * P:(p + 1) * P], M.kb[tok, PT, p * P:(p + 1) * P],
                                   v_of[tok, b % 2, p * P:(p + 1) * P], start=True, stop=True)
                mm.then_inc(updated.h, 1)
            gn.tensor(pe, 0, PT)

        @block.vector
        def _(dve):
            dve.memset(state[:, :, :], 0.0).then_inc(zeroed.h, 1)
            dve.memset(q_of[:, :, :, :], 0.0).then_inc(zeroed.h, 1)
            dve.wait_ge(zeroed.h, 2)
            for b in range(B):
                cols = slice(b * DEC_SEQ, (b + 1) * DEC_SEQ)
                dve.tensor_copy(q_of[:, :, b, cols], M.qbT[:, :, SEQ + cols.start:SEQ + cols.stop])\
                   .then_inc(spread.h, 1)
            dve.wait_ge(loaded.h, 5 * 16)
            dve.wait_ge(inner.h, 1)
            for s in range(2):
                last = dve.tensor_tensor(weight[tok, s], T.ps[tok, (0, 4)[s], 0:PAIRS * NS]
                                         .rearrange("p (a t) -> p a t", a=PAIRS),
                                         keep[tok, :].unsqueeze(1).to_broadcast([NS, PAIRS, NS]), ALU.mult)
            last.then_inc(masked.h, 1)

            def pick(b):
                if b >= 2:
                    dve.wait_ge(updated.h, b - 1)
                dve.tensor_scalar(v_of[tok, b % 2, :], M.vb[tok, PT, :], select[tok, b:b + 1], None, ALU.mult)\
                   .then_inc(picked.h, 1)

            pick(0)
            for b in range(B):
                if b + 1 < B:
                    pick(b + 1)
                dve.wait_ge(outed.h, 1)
                dve.wait_ge(updated.h, b + 1)
                ps = T.ps[:, 2 + b % 2, :].rearrange("p (a e) -> p a e", a=PAIRS)
                mine = slice(PAIRS * b, PAIRS * (b + 1))
                for s in range(2):
                    at = state[half[s], mine, half[s]]
                    T.dve_chain(dve, dve.tensor_tensor(at, at, ps[half[s], :, half[s]], ALU.add))
                    last = dve.tensor_tensor(at, at, power[half[s], :].unsqueeze(2).to_broadcast([HD, PAIRS, HD]),
                                             ALU.mult)
                last.then_inc(added.h, 1)
            gn.vector(dve, 0, T.ps[:, 1, :], PT)
            gn.rest(dve, 0, PT)

        @block.scalar
        def _(act):
            gn.scalar(act, 0, PT)
            gn.round(act, 0, PT)



BP = DEC_BATCH // 2
PAGES = PAST_LEN // PAGE
BLOCKS = PAST_LEN // 256
GP = PAGES // 2


def linker(eng, sem, base):
    made = [0]

    def link(ins):
        made[0] += 1
        ins.then_inc(sem.h, 1)
        eng.wait_ge(sem.h, base + made[0])
    return link


def phase_attend_samples(T, M, k_pool, v_pool, table, past_mask, block_no, n_pool):
    nc = T.nc
    k_pages = k_pool.rearrange("n t h d -> n t (h d)")
    v_pages = v_pool.rearrange("n t h d -> n t (h d)")
    SOFT, NORM = 12, 2

    def count(name):
        return Count(T.ctx, nc, "sa_" + name)

    k_loaded, v_loaded, v_used = ([count(n + str(i)) for i in range(2)] for n in ("k_loaded", "v_loaded", "v_used"))
    k_turned, k_moved = ([count(n + str(i)) for i in range(2)] for n in ("k_turned", "k_moved"))
    loaded, zeroed, q_ready, scored, shifted, expd, normed = map(
        count, ("loaded", "zeroed", "q_ready", "scored", "shifted", "expd", "normed"))
    p_turned, p_moved0, p_moved1, valued, rounded, rested, soft_link, norm_link = map(
        count, ("p_turned", "p_moved0", "p_moved1", "valued", "rounded", "rested", "soft_link", "norm_link"))
    with ExitStack() as ctx:
        def sb(name, shape, dt=F32):
            return ctx.enter_context(nc.sbuf_tensor(name, shape, dt))

        k_ring, v_ring = sb("k_ring", [P, PAGES, MIX]), sb("v_ring", [P, PAGES, MIX])
        keys = sb("keys", [P, 2, PAIRS, PAST_LEN])
        q_of = sb("q_of_s", [P, 2, PAIRS * (HD + 16)])
        prob = sb("prob_s", [P, PAST_LEN + NS])
        prob_t = sb("prob_ts", [P, PAGES + 1, P])
        mask, new = sb("mask_s", [P, BP, NS]), sb("new_s", [P, NS])
        pages = sb("pages", [1, DEC_BATCH * PAGES], I32)
        number = sb("number", [P, BLOCKS])
        gate, worst, same, last_same = sb("gate_s", [P, BLOCKS]), sb("worst", [P, 1]), sb("same", [P, BLOCKS]), sb("last_same", [P, 1])
        out_of, block_top, top = sb("out_of", [P, BLOCKS]), sb("block_top", [P, BLOCKS + 1]), sb("top_s", [P, 1])
        shift, totals, total = sb("shift_s", [P, BLOCKS + 1]), sb("totals_s", [P, BLOCKS + 1]), sb("total_s", [P, 1])
        credit = sb("credit_s", [P, 4])
        block = ctx.enter_context(nc.Block())
        half = [slice(0, HD), slice(HD, P)]
        past = T.ps[:, 0:2, :].rearrange("p b (c t) -> p (b c) t", c=2)
        tok = slice(NS, P)

        @block.sync
        def _(sp):
            def load(pool, ring, arrived, bp, b2, g, free, value):
                srcs = []
                for i in range(GP):
                    at = bp * (2 * PAGES) + (b2 * PAGES + g * GP + i)
                    page = sp.value_load(pages[0:1, bass.ds(at, 1)], min_val=0, max_val=n_pool - 1)
                    srcs.append(pool[bass.ds(page, 1)].rearrange("a t c -> (a t) c"))
                if free is not None:
                    sp.wait_ge(free.h, value)
                for i in range(GP):
                    sp.dma_start(ring[:, g * GP + i], srcs[i]).then_inc(arrived[g].h, 16)

            def load_k(bp, b2, first=False):
                for g in range(2):
                    value = bp * 8 + (4 * b2 - 2 + 2 * g)
                    load(k_pages, k_ring, k_loaded, bp, b2, g, None if first else k_turned[1], value)

            def load_v(bp):
                for b2 in range(2):
                    for g in range(2):
                        load(v_pages, v_ring, v_loaded, bp, b2, g, v_used[g], bp * 2 + (b2 + 1))

            sp.dma_start(pages[:, :], table.rearrange("b n -> (b n)").unsqueeze(0)).then_inc(loaded.h, 16)
            sp.dma_start(mask[:, :, :], past_mask).then_inc(loaded.h, 16)
            sp.dma_start(number[:, :], block_no).then_inc(loaded.h, 16)
            sp.wait_ge(loaded.h, 48)
            load_k(0, 0, True)
            load_k(0, 1)
            with sp.Fori(0, BP - 1) as bp:
                load_k(bp + 1, 0)
                load_v(bp)
                load_k(bp + 1, 1)
            load_v(BP - 1)

        @block.tensor
        def _(pe):
            def turn_keys(bp, b2, first=False):
                for j in range(PAGES):
                    if j % GP == 0:
                        pe.wait_ge(k_loaded[j // GP].h, bp * 128 + (64 * b2 + 64))
                    if not (first and j < 2):
                        pe.wait_ge(k_moved[j % 2].h, bp * 8 + (4 * b2 + j // 2))
                    for p in range(PAIRS):
                        mm = pe.transpose(T.ps[:, 3 + j % 2, p * P:(p + 1) * P], k_ring[:, j, p * P:(p + 1) * P],
                                          T.ident[:, :])
                    mm.then_inc(k_turned[j % 2].h, 1)

            def score(bp, b2, first=False):
                for s in range(2):
                    pe.wait_ge(k_moved[s].h, bp * 8 + (4 * b2 + 4))
                pe.wait_ge(q_ready.h, bp + 1)
                if b2 == 0 and not first:
                    pe.wait_ge(expd.h, bp)
                rows = half[b2]
                for n in range(3):
                    for p in range(PAIRS):
                        src = keys[:, b2, p, n * 512:(n + 1) * 512] if n < 2 else M.kaT[:, p, SEQ:NT]
                        mm = pe.matmul(T.ps[rows, n, 0:src.shape[1]], q_of[:, b2, p * HD:(p + 1) * HD], src,
                                       start=(p == 0), stop=(p == PAIRS - 1))
                mm.then_inc(scored.h, 1)

            def values(bp):
                pe.wait_ge(normed.h, bp + 1)
                for g in range(2):
                    for i in range(GP):
                        j = GP * g + i
                        mm = pe.transpose(T.ps[:, 5 + g, i * P:(i + 1) * P], prob[:, j * P:(j + 1) * P], T.ident[:, :])
                    mm.then_inc(p_turned.h, 1)
                pe.transpose(T.ps[0:NS, 2, 0:P], prob[:, PAST_LEN:PAST_LEN + NS], T.ident[:, :])\
                  .then_inc(p_turned.h, 1)
                pe.wait_ge(p_moved0.h, bp * 2 + 2)
                pe.wait_ge(p_moved1.h, bp + 1)
                pe.wait_ge(rested.h, bp + 1)
                for b2 in range(2):
                    for j in range(PAGES):
                        if j % GP == 0:
                            pe.wait_ge(v_loaded[j // GP].h, bp * 128 + (64 * b2 + 64))
                        for p in range(PAIRS):
                            col = (b2 * PAIRS + p) * 16
                            mm = pe.matmul(T.ps[:, 7, col:col + 16], v_ring[:, j, p * P:(p + 1) * P],
                                           prob_t[:, j, b2 * HD + p * 16:b2 * HD + p * 16 + 16],
                                           start=(b2 == 0 and j == 0 and p == 0), stop=False, skip_group_check=True)
                        if j % GP == GP - 1:
                            mm.then_inc(v_used[j // GP].h, 1)
                for b2 in range(2):
                    for p in range(PAIRS):
                        col = (b2 * PAIRS + p) * 16
                        mm = pe.matmul(T.ps[:, 7, col:col + 16], M.va[tok, PT, p * P:(p + 1) * P],
                                       prob_t[tok, PAGES, b2 * HD + p * 16:b2 * HD + p * 16 + 16],
                                       start=False, stop=(b2 == 1 and p == PAIRS - 1), skip_group_check=True)
                mm.then_inc(valued.h, 1)

            turn_keys(0, 0, True)
            score(0, 0, True)
            turn_keys(0, 1)
            score(0, 1)
            with pe.Fori(0, BP - 1) as bp:
                turn_keys(bp + 1, 0)
                values(bp)
                score(bp + 1, 0)
                turn_keys(bp + 1, 1)
                score(bp + 1, 1)
            values(BP - 1)

        def keys_at(b2, j):
            return keys[:, b2, :, j * P:(j + 1) * P]

        def keys_ps(j):
            return T.ps[:, 3 + j % 2, :].rearrange("p (a t) -> p a t", a=PAIRS)

        def outputs_at(s, bp, buf):
            at = buf[half[s], 0:PAIRS, bass.ds(bp * (2 * DEC_SEQ) + SEQ, 2 * DEC_SEQ)]
            return at.rearrange("p a (b q) -> p a b q", b=2)

        def outputs_ps(s):
            return T.ps[half[s], 7, 0:P].rearrange("p (b a c) -> p a b c", b=2, c=16)[:, :, :, s * 8:(s + 1) * 8]

        @block.vector
        def _(dve):
            def move_keys(bp, b2):
                for j in range(1, PAGES, 2):
                    dve.wait_ge(k_turned[1].h, bp * 8 + (4 * b2 + j // 2 + 1))
                    dve.tensor_copy(keys_at(b2, j), keys_ps(j)).then_inc(k_moved[1].h, 1)

            def spread_q(bp):
                for s in range(2):
                    dst = q_of[half[s], :, :].rearrange("p b (a c) -> p b a c", a=PAIRS)[:, :, :, s * 8:(s + 1) * 8]
                    src = M.qaT[half[s], :, bass.ds(bp * (2 * DEC_SEQ) + SEQ, 2 * DEC_SEQ)]\
                        .rearrange("p a (b q) -> p b a q", b=2)
                    for b2 in range(2):
                        last = dve.tensor_copy(dst[:, b2], src[:, b2])
                last.then_inc(q_ready.h, 1)

            def soft(bp):
                dve.wait_ge(scored.h, bp * 2 + 2)
                link = linker(dve, soft_link, bp * SOFT)
                dve.tensor_reduce(gate[:, :], past, AX_X, ALU.add)
                dve.tensor_reduce(block_top[:, 0:BLOCKS], past, AX_X, ALU.max)
                link(dve.tensor_tensor(new[:, :], T.ps[:, 2, 0:NS],
                                       mask[:, bass.ds(bp, 1), :].rearrange("p a t -> p (a t)"), ALU.add))
                link(dve.reduce_max(block_top[:, BLOCKS:BLOCKS + 1], new[:, :], AX_X))
                link(dve.tensor_reduce(worst[:, :], gate[:, :], AX_X, ALU.min))
                link(dve.tensor_scalar(same[:, :], gate[:, :], worst[:, 0:1], None, ALU.is_equal))
                link(dve.tensor_tensor(same[:, :], same[:, :], number[:, :], ALU.mult))
                link(dve.reduce_max(last_same[:, :], same[:, :], AX_X))
                link(dve.tensor_scalar(out_of[:, :], number[:, :], last_same[:, 0:1], NEG, ALU.is_equal, ALU.mult))
                link(dve.tensor_tensor(block_top[:, 0:BLOCKS], block_top[:, 0:BLOCKS], out_of[:, :], ALU.add))
                link(dve.reduce_max(top[:, :], block_top[:, :], AX_X))
                link(dve.tensor_scalar(shift[:, BLOCKS:BLOCKS + 1], top[:, :], -HD ** -0.5, None, ALU.mult))
                link(dve.tensor_scalar(shift[:, 0:BLOCKS], out_of[:, :], shift[:, BLOCKS:BLOCKS + 1], None, ALU.add))
                link(dve.memset(credit[:, 3:4], 0.0))
                dve.memset(credit[:, 2:3], 0.0).then_inc(shifted.h, 1)

            def norm(bp):
                dve.wait_ge(expd.h, bp + 1)
                link = linker(dve, norm_link, bp * NORM)
                link(dve.tensor_reduce(total[:, :], totals[:, :], AX_X, ALU.add))
                link(dve.reciprocal(total[:, :], total[:, :]))
                dve.tensor_scalar(prob[:, :], prob[:, :], total[:, 0:1], None, ALU.mult).then_inc(normed.h, 1)

            def finish(bp):
                dve.wait_ge(p_turned.h, bp * 3 + 2)
                dve.tensor_copy(prob_t[:, GP:PAGES, :], T.ps[:, 6, :].rearrange("p (j t) -> p j t", j=GP))\
                   .then_inc(p_moved1.h, 1)
                dve.wait_ge(rounded.h, bp + 1)
                for s in range(2):
                    hi, lo, ps = outputs_at(s, bp, T.x_hi), outputs_at(s, bp, T.x_lo), outputs_ps(s)
                    last = dve.tensor_tensor(lo, ps, hi.bitcast(F32), ALU.subtract)
                last.then_inc(rested.h, 1)

            for i, c in enumerate((v_used[0], v_used[1], rested)):
                dve.memset(credit[:, i:i + 1], 0.0).then_inc(c.h, 1)
            dve.memset(q_of[:, :, :], 0.0).then_inc(zeroed.h, 1)
            dve.wait_ge(zeroed.h, 1)
            dve.wait_ge(loaded.h, 48)
            spread_q(0)
            move_keys(0, 0)
            move_keys(0, 1)
            soft(0)
            with dve.Fori(0, BP - 1) as bp:
                spread_q(bp + 1)
                move_keys(bp + 1, 0)
                norm(bp)
                finish(bp)
                move_keys(bp + 1, 1)
                soft(bp + 1)
            norm(BP - 1)
            finish(BP - 1)

        @block.scalar
        def _(act):
            def move_keys(bp, b2):
                for j in range(0, PAGES, 2):
                    act.wait_ge(k_turned[0].h, bp * 8 + (4 * b2 + j // 2 + 1))
                    act.activation(keys_at(b2, j), keys_ps(j), ACT.Copy).then_inc(k_moved[0].h, 1)

            def exps(bp):
                act.wait_ge(shifted.h, bp + 1)
                for c in range(BLOCKS):
                    act.activation(prob[:, c * 256:(c + 1) * 256], past[:, c], ACT.Exp, bias=shift[:, c:c + 1],
                                   scale=HD ** -0.5, accum_out=totals[:, c:c + 1])
                act.activation(prob[:, PAST_LEN:PAST_LEN + NS], new[:, :], ACT.Exp, bias=shift[:, BLOCKS:BLOCKS + 1],
                               scale=HD ** -0.5, accum_out=totals[:, BLOCKS:BLOCKS + 1]).then_inc(expd.h, 1)

            def finish(bp):
                act.wait_ge(p_turned.h, bp * 3 + 1)
                act.activation(prob_t[:, 0:GP, :], T.ps[:, 5, :].rearrange("p (j t) -> p j t", j=GP), ACT.Copy)\
                   .then_inc(p_moved0.h, 1)
                act.wait_ge(p_turned.h, bp * 3 + 3)
                act.activation(prob_t[tok, PAGES, :], T.ps[0:NS, 2, 0:P], ACT.Copy).then_inc(p_moved0.h, 1)
                act.wait_ge(valued.h, bp + 1)
                for s in range(2):
                    last = act.activation(outputs_at(s, bp, T.x_hi), outputs_ps(s), ACT.Copy)
                last.then_inc(rounded.h, 1)

            move_keys(0, 0)
            move_keys(0, 1)
            exps(0)
            with act.Fori(0, BP - 1) as bp:
                move_keys(bp + 1, 0)
                finish(bp)
                move_keys(bp + 1, 1)
                exps(bp + 1)
            finish(BP - 1)



def out_piece(w, d):
    return w.rearrange("(k p) d -> p k d", p=P)[:, :, bass.ds(d * P, P)]


def phase_out(T, w_out, w_gate, row, nxt):
    nc = T.nc
    U = T.pieces
    G = KT * P
    gated = w_gate is not None
    used = KT if gated else KT // 2
    res0, silu0 = T.res_done.n, T.silu_done.n
    with ExitStack() as ctx:
        def sb(name, shape, dt=F32):
            return ctx.enter_context(nc.sbuf_tensor(f"{name}_{row}", shape, dt))

        gate, work = sb("gate", [P, 2, NT]), sb("work", [P, 2, NT])
        acc, rstd = sb("acc", [P, NT]), sb("rstd", [P, NT])
        norm = Norm(T, row, 1.0, acc, KT + 1, gate, rstd)
        acc0 = T.acc_added.n
        block = ctx.enter_context(nc.Block())

        def pieces():
            for d in range(KT):
                if gated:
                    yield d, 0, d, w_out
                    yield d, 1, d, w_gate
                else:
                    yield d, d % 2, d // 2, w_out

        @block.sync
        def _(sp):
            for d, slot, u, w in list(pieces())[2:]:
                load_piece(T, sp, slot, U + u, out_piece(w, d))
            for slot in range(2):
                load_piece(T, sp, slot, U + used, nxt[slot])

        @block.tensor
        def _(pe):
            for d, slot, u, w in pieces():
                j = d % 2
                if w is w_out:
                    pe.wait_ge(T.res_done.h, res0 + d - 1)
                pe.wait_ge(T.w_split[slot].h, U + u + 2)
                for n in range(2):
                    for k in range(KT):
                        cols = slice(n * NH, (n + 1) * NH)
                        mm = product3(pe, T.ps[:, 4 * j + (0 if w is w_out else 2) + n, 0:NH],
                                      T.w_hi[:, slot, k * P:(k + 1) * P], T.w_lo[:, slot, k * P:(k + 1) * P],
                                      T.x_hi[:, k, cols], T.x_lo[:, k, cols], k == 0, k == KT - 1)
                mm.then_inc(T.w_used[slot].h, 1)
            norm.tensor(pe)

        @block.scalar
        def _(act):
            order = list(pieces())
            for slot in range(2):
                round_piece(T, act, slot, U, G)
            for d in range(KT):
                for dd, slot, u, w in order:
                    if dd == d + (1 if gated else 2):
                        round_piece(T, act, slot, U + u, G)
                if gated:
                    act.wait_ge(T.w_used[1].h, U + d + 2)
                    act.activation(halves(gate[:, d % 2]), T.ps[:, 4 * (d % 2) + 2:4 * (d % 2) + 4, 0:NH],
                                   ACT.Sigmoid).then_inc(T.silu_done.h, 1)
            norm.scalar(act)

        @block.vector
        def _(dve):
            order = list(pieces())
            dve.memset(acc[:, :], 0.0).then_inc(T.acc_added.h, 1)
            for slot in range(2):
                rest_piece(T, dve, slot, U, G)
            for d in range(KT):
                j = d % 2
                for dd, slot, u, w in order:
                    if dd == d + (1 if gated else 2):
                        rest_piece(T, dve, slot, U + u, G)
                y = T.ps[:, 4 * j:4 * j + 2, 0:NH]
                if gated:
                    dve.wait_ge(T.silu_done.h, silu0 + d + 1)
                    T.dve_chain(dve, dve.tensor_tensor(halves(work[:, j]), halves(gate[:, j]), y, ALU.mult))
                    y = halves(work[:, j])
                else:
                    dve.wait_ge(T.w_used[j].h, U + d // 2 + 2)
                dve.scalar_tensor_tensor(halves(T.x[:, d]), halves(T.x[:, d]), ALPHA, y, ALU.mult, ALU.add)\
                   .then_inc(T.res_done.h, 1)
                dve.wait_ge(T.res_done.h, res0 + d + 1)
                dve.wait_ge(T.acc_added.h, acc0 + d + 1)
                dve.tensor_tensor(acc[:, :], acc[:, :], T.x[:, d], ALU.add).then_inc(T.acc_added.h, 1)
            norm.vector(dve)

        @block.gpsimd
        def _(pool):
            norm.gpsimd(pool)
    T.res_done.close(KT)
    T.silu_done.close(KT if gated else 0)
    T.pieces += used
    norm.close()



GROUPS, GH, STATES = 64, 16, 64
GPAIRS = GROUPS // 2
CL = 8
PC = SEQ // CL
NC_ = NT // CL
GT = P // GH
LN2 = math.log(2.0)
LN2_HI = 0.693359375
TWO_PI_HI = 6.28125
TWO_PI_MID = float(np.float32(2 * math.pi - TWO_PI_HI))
TWO_PI_LO = 2 * math.pi - TWO_PI_HI - TWO_PI_MID
TO_INT = 12582912.0


class S5:
    pass


def open_s5(ctx, nc):
    S = S5()

    def sb(name, shape, dt=F32):
        return ctx.enter_context(nc.sbuf_tensor("s5_" + name, shape, dt))

    S.powers = sb("powers", [P, 2, CL + 1, GPAIRS])
    S.b_bar = sb("b_bar", [P, 2, GPAIRS, GH])
    S.c_t = sb("c_t", [P, 2, GPAIRS, GH])
    S.u = sb("u", [P, GROUPS, NC_])
    S.start = sb("start", [P, 2, GPAIRS, NC_])
    S.skip = sb("skip", [GH, GROUPS])
    return S


def phase_s5_constants(T, S, I):
    nc = T.nc
    loaded, rows_done, turned, state_moved, done, placed = (
        Count(T.ctx, nc, "s5c_" + n) for n in ("loaded", "rows_done", "turned", "state_moved", "done", "placed"))
    with ExitStack() as ctx:
        def sb(name, shape, dt=F32):
            return ctx.enter_context(nc.sbuf_tensor("s5c_" + name, shape, dt))

        shape = [GPAIRS, P]
        l_re, l_im, dt, work, k, e_re, theta, s_, c_, z2, inv, poly, tmp = (
            sb(n, shape) for n in ("l_re", "l_im", "dt", "work", "k", "e_re", "theta", "s", "c", "z2", "inv", "poly", "tmp"))
        k_int = sb("k_int", shape, I32)
        log_dt = sb("log_dt", [GPAIRS, 2])
        results = sb("results", [GPAIRS, 4, P])
        cols = sb("cols", [P, 4, GPAIRS])
        c_rows = sb("c_rows", [P, GT, 2, STATES])
        s_rows = sb("s_rows", [P, 2, 2, P])
        b_raw = sb("b_raw", [P, 2, GPAIRS, GH])
        m1, m2 = sb("m1", [P, GPAIRS * GH]), sb("m2", [P, GPAIRS * GH])
        block = ctx.enter_context(nc.Block())

        @block.sync
        def _(sp):
            pairs = lambda a: a.rearrange("(a s) p -> a (s p)", s=2)
            sp.dma_start(l_re[:, :], pairs(I["s5_lam_re"][0])).then_inc(loaded.h, 16)
            sp.dma_start(l_im[:, :], pairs(I["s5_lam_im"][0])).then_inc(loaded.h, 16)
            sp.dma_start(log_dt[:, :], I["s5_log_dt"][0].rearrange("(a s) -> a s", s=2)).then_inc(loaded.h, 16)
            for r, part in enumerate(("re", "im")):
                sp.dma_start(c_rows[:, :, r, :],
                             I["s5_c_" + part][0].rearrange("(k q) h p -> (q h) k p", q=GT)).then_inc(loaded.h, 16)
                sp.dma_start(s_rows[:, r, :, :],
                             I["state_s5_" + part][0].rearrange("(j b) (a s) p -> (b a) j (s p)", j=2, s=2))\
                  .then_inc(loaded.h, 16)
                sp.dma_start(b_raw[:, r], I["s5_b_" + part][0].rearrange("(a s) p h -> (s p) a h", s=2))\
                  .then_inc(loaded.h, 16)
            with nc.allow_non_contiguous_dma(reason="1024 skip weights by channel"):
                sp.dma_start(S.skip[:, :], I["s5_d"][0].rearrange("(g h) -> h g", h=GH)).then_inc(loaded.h, 16)

        @block.tensor
        def _(pe):
            pe.wait_ge(loaded.h, 10 * 16)
            for t in range(GT):
                mm = pe.transpose(T.ps[:, t // 4, (t % 4) * P:(t % 4 + 1) * P],
                                  c_rows[:, t].rearrange("p r s -> p (r s)"), T.ident[:, :])
            mm.then_inc(turned.h, 1)
            for r in range(2):
                for j in range(2):
                    mm = pe.transpose(T.ps[:, 2, (2 * r + j) * P:(2 * r + j + 1) * P], s_rows[:, r, j, :], T.ident[:, :])
            mm.then_inc(turned.h, 1)
            pe.wait_ge(rows_done.h, 1)
            for n in range(4):
                mm = pe.transpose(T.ps[:, 3, n * GPAIRS:(n + 1) * GPAIRS], results[:, n, :],
                                  T.ident[0:GPAIRS, 0:GPAIRS])
            mm.then_inc(turned.h, 1)

        @block.scalar
        def _(act):
            act.wait_ge(turned.h, 1)
            src = T.ps[:, 0:2, :].rearrange("p b (k q s h) -> p (b k) q s h", k=4, s=2, h=GH)
            for r in range(2):
                for s in range(2):
                    for kk in range(2):
                        sl = slice(4 * kk, 4 * kk + 4)
                        act.activation(S.c_t[s * HD:(s + 1) * HD, r, 16 * kk:16 * kk + 16, :]
                                       .rearrange("p (k q) h -> p k q h", q=4),
                                       src[r * HD:(r + 1) * HD, sl, :, s, :], ACT.Copy).then_inc(placed.h, 1)
            act.wait_ge(turned.h, 2)
            for r in range(2):
                act.activation(S.start[:, r, :, PC:NC_],
                               T.ps[:, 2, r * 256:(r + 1) * 256].rearrange("p (b a) -> p a b", b=DEC_BATCH),
                               ACT.Copy).then_inc(placed.h, 1)

        @block.vector
        def _(dve):
            def op(ins):
                T.dve_chain(dve, ins)

            def ts(out, a, s1, s2, op0, op1=None):
                op(dve.tensor_scalar(out[:, :], a[:, :], s1, s2, op0, op1) if op1 is not None else
                   dve.tensor_scalar(out[:, :], a[:, :], s1, None, op0))

            def tt(out, a, b, o):
                op(dve.tensor_tensor(out[:, :], a[:, :], b[:, :], o))

            def stt(out, a, s, b, op0, op1):
                op(dve.scalar_tensor_tensor(out[:, :], a[:, :], s, b[:, :], op0, op1))

            def horner(out, z, coefs):
                ts(out, z, coefs[-1], None, ALU.mult)
                for c in coefs[-2::-1]:
                    stt(out, out, c, z, ALU.add, ALU.mult)

            def exp(out, x):
                ts(work, x, -87.0, 88.0, ALU.max, ALU.min)
                ts(k, work, 1.0 / LN2, TO_INT, ALU.mult, ALU.add)
                ts(k, k, -TO_INT, None, ALU.add)
                stt(work, k, -LN2_HI, work, ALU.mult, ALU.add)
                stt(work, k, LN2_HI - LN2, work, ALU.mult, ALU.add)
                horner(poly, work, [1.0 / math.factorial(n) for n in range(1, 9)])
                ts(k, k, 127.0, 8388608.0, ALU.add, ALU.mult)
                op(dve.tensor_copy(k_int[:, :], k[:, :]))
                op(dve.scalar_tensor_tensor(out[:, :], poly[:, :], 1.0, k_int[:, :].bitcast(F32), ALU.add, ALU.mult))

            dve.wait_ge(loaded.h, 10 * 16)
            op(dve.tensor_copy(tmp[:, :].rearrange("a (s p) -> a s p", s=2),
                               log_dt[:, :].unsqueeze(2).to_broadcast([GPAIRS, 2, STATES])))
            exp(dt, tmp)
            tt(tmp, l_re, dt, ALU.mult)
            exp(e_re, tmp)
            tt(theta, l_im, dt, ALU.mult)
            ts(k, theta, 1.0 / (2 * math.pi), TO_INT, ALU.mult, ALU.add)
            ts(k, k, -TO_INT, None, ALU.add)
            for part in (TWO_PI_HI, TWO_PI_MID, TWO_PI_LO):
                stt(theta, k, -part, theta, ALU.mult, ALU.add)
            ts(theta, theta, 0.5, None, ALU.mult)
            tt(z2, theta, theta, ALU.mult)
            horner(s_, z2, [(-1) ** n / math.factorial(2 * n + 1) for n in range(1, 7)])
            stt(s_, s_, 1.0, theta, ALU.add, ALU.mult)
            horner(c_, z2, [(-1) ** n / math.factorial(2 * n) for n in range(1, 8)])
            ts(c_, c_, 1.0, None, ALU.add)
            tt(c_, s_, c_, ALU.mult)
            tt(s_, s_, s_, ALU.mult)
            ts(s_, s_, -2.0, 1.0, ALU.mult, ALU.add)
            lam_re, lam_im, co_re, co_im = (results[:, n, :] for n in range(4))
            op(dve.tensor_tensor(lam_re, e_re[:, :], s_[:, :], ALU.mult))
            op(dve.scalar_tensor_tensor(lam_im, c_[:, :], 2.0, e_re[:, :], ALU.mult, ALU.mult))
            tt(inv, l_re, l_re, ALU.mult)
            tt(tmp, l_im, l_im, ALU.mult)
            tt(inv, inv, tmp, ALU.add)
            op(dve.reciprocal(inv[:, :], inv[:, :]))
            op(dve.tensor_scalar(work[:, :], lam_re, -1.0, None, ALU.add))
            tt(tmp, work, l_re, ALU.mult)
            op(dve.tensor_tensor(k[:, :], lam_im, l_im[:, :], ALU.mult))
            tt(tmp, tmp, k, ALU.add)
            op(dve.tensor_tensor(co_re, tmp[:, :], inv[:, :], ALU.mult))
            op(dve.tensor_tensor(tmp[:, :], lam_im, l_re[:, :], ALU.mult))
            tt(k, work, l_im, ALU.mult)
            tt(tmp, tmp, k, ALU.subtract)
            dve.tensor_tensor(co_im, tmp[:, :], inv[:, :], ALU.mult).then_inc(rows_done.h, 1)

            dve.wait_ge(turned.h, 3)
            op(dve.tensor_copy(cols[:, :, :], T.ps[:, 3, 0:4 * GPAIRS].rearrange("p (n a) -> p n a", n=4)))
            op(dve.memset(S.powers[:, 0, 0], 1.0))
            op(dve.memset(S.powers[:, 1, 0], 0.0))
            op(dve.tensor_copy(S.powers[:, :, 1], cols[:, 0:2]))

            def times(out_re, out_im, a_re, a_im, b_re, b_im, view):
                for out, x, y, z, w, o in ((out_re, a_re, b_re, a_im, b_im, ALU.subtract),
                                           (out_im, a_re, b_im, a_im, b_re, ALU.add)):
                    dve.tensor_tensor(view(m1), x, y, ALU.mult)
                    op(dve.tensor_tensor(view(m2), z, w, ALU.mult))
                    op(dve.tensor_tensor(out, view(m1), view(m2), o))

            n = 1
            while n < CL:
                pw = S.powers
                by = [pw[:, r, n:n + 1].to_broadcast([P, n, GPAIRS]) for r in range(2)]
                times(pw[:, 0, n + 1:2 * n + 1], pw[:, 1, n + 1:2 * n + 1], pw[:, 0, 1:n + 1], pw[:, 1, 1:n + 1],
                      by[0], by[1], lambda m: m[:, 0:n * GPAIRS].rearrange("p (n a) -> p n a", n=n))
                n *= 2
            co = [cols[:, 2 + r].unsqueeze(2).to_broadcast([P, GPAIRS, GH]) for r in range(2)]
            times(S.b_bar[:, 0], S.b_bar[:, 1], b_raw[:, 0], b_raw[:, 1], co[0], co[1],
                  lambda m: m[:, :].rearrange("p (a h) -> p a h", h=GH))


def phase_s5_inputs(T, S):
    nc = T.nc
    turned, moved = Count(T.ctx, nc, "s5i_turned"), [Count(T.ctx, nc, f"s5i_moved{i}") for i in range(2)]
    with ExitStack() as ctx:
        chunked = ctx.enter_context(nc.sbuf_tensor("s5_chunked", [P, GROUPS, CL, GH], F32))
        block = ctx.enter_context(nc.Block())
        N1 = CL * 2
        N2 = GROUPS // 4

        @block.tensor
        def _(pe):
            for n in range(N1 + N2):
                if n == N1:
                    for i in range(2):
                        pe.wait_ge(moved[i].h, N1 // 2)
                elif n >= 8:
                    pe.wait_ge(moved[n % 2].h, (n - 8) // 2 + 1)
                for i in range(4):
                    if n < N1:
                        t, k = n // 2, 4 * (n % 2) + i
                        mm = pe.transpose(T.ps[0:NC_, n % 8, i * P:(i + 1) * P], T.x[:, k, t:NT:CL], T.ident[:, :])
                    else:
                        g = 4 * (n - N1) + i
                        mm = pe.transpose(T.ps[:, n % 8, i * NC_:(i + 1) * NC_],
                                          chunked[0:NC_, g].rearrange("p t h -> p (t h)"), T.ident[0:NC_, 0:NC_])
                mm.then_inc(turned.h, 1)

        def move(eng, copy, i):
            for n in range(i, N1 + N2, 2):
                eng.wait_ge(turned.h, n + 1)
                if n < N1:
                    t, k = n // 2, 4 * (n % 2)
                    out = chunked[0:NC_, k * GT:(k + 4) * GT, t, :]
                    src = T.ps[0:NC_, n % 8, :].rearrange("p (g h) -> p g h", h=GH)
                else:
                    g = 4 * (n - N1)
                    out = S.u[:, g:g + 4, :]
                    src = T.ps[:, n % 8, 0:4 * NC_].rearrange("p (g c) -> p g c", g=4)
                copy(out, src).then_inc(moved[i].h, 1)

        @block.vector
        def _(dve):
            move(dve, dve.tensor_copy, 0)

        @block.scalar
        def _(act):
            move(act, lambda out, src: act.activation(out, src, ACT.Copy), 1)


def phase_s5_scan(T, S, c_pow, O):
    nc = T.nc
    Q = 4
    STEPS = GPAIRS // Q
    formed, b_turned, b_moved, added, moved, stepped, turned, out_moved, stored, c_done, zeroed = (
        Count(T.ctx, nc, "s5s_" + n) for n in ("formed", "b_turned", "b_moved", "added", "moved", "stepped",
                                               "turned", "out_moved", "stored", "c_done", "zeroed"))
    with ExitStack() as ctx:
        def sb(name, shape, dt=F32):
            return ctx.enter_context(nc.sbuf_tensor("s5s_" + name, shape, dt))

        incr = sb("incr", [P, 2, GPAIRS, NC_])
        falling = sb("falling", [P, 2, CL, GPAIRS])
        by_re, by_im = sb("by_re", [P, 2, GPAIRS]), sb("by_im", [P, 2, GPAIRS])
        t1, t2 = sb("t1", [P, 2, GPAIRS]), sb("t2", [P, 2, GPAIRS])
        inner = ExitStack()
        b_pow = inner.enter_context(nc.sbuf_tensor("s5s_b_pow", [P, 2, Q, CL, GH], F32))
        b_rows = inner.enter_context(nc.sbuf_tensor("s5s_b_rows", [P, 2, Q, P], F32))
        m1 = inner.enter_context(nc.sbuf_tensor("s5s_m1", [P, Q, CL, GH], F32))
        half = [slice(0, HD), slice(HD, P)]
        with inner:
            block = inner.enter_context(nc.Block())

            @block.vector
            def _(dve):
                def op(ins):
                    T.dve_chain(dve, ins)

                for t in range(CL):
                    last = dve.tensor_copy(falling[:, :, t], S.powers[:, :, CL - 1 - t])
                op(last)
                for q in range(STEPS):
                    a = slice(Q * q, Q * (q + 1))
                    wide = [P, Q, CL, GH]
                    b = [S.b_bar[:, r, a, :].unsqueeze(2).to_broadcast(wide) for r in range(2)]
                    f = [falling[:, r, :, a].rearrange("p t a -> p a t").unsqueeze(3).to_broadcast(wide)
                         for r in range(2)]
                    if q:
                        dve.wait_ge(b_turned.h, q)
                    for r, (x, y, o) in enumerate(((f[0], f[1], ALU.subtract), (f[1], f[0], ALU.add))):
                        dve.tensor_tensor(b_pow[:, r], b[0], x, ALU.mult)
                        op(dve.tensor_tensor(m1[:, :, :, :], b[1], y, ALU.mult))
                        last = dve.tensor_tensor(b_pow[:, r], b_pow[:, r], m1[:, :, :, :], o)
                        if r == 0:
                            op(last)
                    last.then_inc(formed.h, 1)
                    dve.wait_ge(formed.h, q + 1)
                    if q:
                        dve.wait_ge(added.h, q)
                        prev = slice(Q * (q - 1), Q * q)
                        for r in range(2):
                            last = dve.tensor_copy(incr[:, r, prev, :],
                                                   T.ps[:, 2 + 2 * ((q - 1) % 2) + r, 0:Q * NC_]
                                                   .rearrange("p (a c) -> p a c", a=Q))
                        last.then_inc(moved.h, 1)
                dve.wait_ge(added.h, STEPS)
                for r in range(2):
                    last = dve.tensor_copy(incr[:, r, GPAIRS - Q:GPAIRS, :],
                                           T.ps[:, 2 + 2 * ((STEPS - 1) % 2) + r, 0:Q * NC_]
                                           .rearrange("p (a c) -> p a c", a=Q))
                last.then_inc(moved.h, 1)

            @block.scalar
            def _(act):
                for q in range(STEPS):
                    act.wait_ge(b_turned.h, q + 1)
                    if q:
                        act.wait_ge(added.h, q)
                    for r in range(2):
                        last = act.activation(b_rows[:, r], T.ps[:, r, :].rearrange("p (a s) -> p a s", a=Q), ACT.Copy)
                    last.then_inc(b_moved.h, 1)

            @block.tensor
            def _(pe):
                def increments(q):
                    pe.wait_ge(b_moved.h, q + 1)
                    if q >= 2:
                        pe.wait_ge(moved.h, q - 1)
                    for a in range(Q):
                        for s in range(2):
                            for r in range(2):
                                mm = pe.matmul(T.ps[half[s], 2 + 2 * (q % 2) + r, a * NC_:(a + 1) * NC_],
                                               b_rows[:, r, a, half[s]], S.u[:, 2 * (Q * q + a) + s, :],
                                               start=True, stop=True)
                    mm.then_inc(added.h, 1)

                for q in range(STEPS):
                    pe.wait_ge(formed.h, q + 1)
                    if q:
                        pe.wait_ge(b_moved.h, q)
                    for r in range(2):
                        for a in range(Q):
                            mm = pe.transpose(T.ps[:, r, a * P:(a + 1) * P],
                                              b_pow[:, r, a].rearrange("p t h -> p (t h)"), T.ident[:, :])
                    mm.then_inc(b_turned.h, 1)
                    increments(q)

        ends = ctx.enter_context(nc.sbuf_tensor("s5s_ends", [P, 2, DEC_BATCH, GPAIRS], F32))
        end = ctx.enter_context(nc.sbuf_tensor("s5s_end", [P, 2, GPAIRS], F32))
        out_rows = ctx.enter_context(nc.sbuf_tensor("s5s_out_rows", [P, 5, P], F32))
        m2 = ctx.enter_context(nc.sbuf_tensor("s5s_m2", [P, 4, CL + 1, GH], F32))
        m3 = ctx.enter_context(nc.sbuf_tensor("s5s_m3", [P, 4, CL + 1, GH], F32))
        block = ctx.enter_context(nc.Block())
        LINKS = 2

        @block.vector
        def _(dve):
            def op(ins):
                T.dve_chain(dve, ins)

            op(dve.memset(S.start[:, :, :, 0:1], 0.0))
            for r in range(2):
                last = dve.tensor_copy(by_re[:, r], S.powers[:, 0, CL])
            op(last)
            op(dve.tensor_copy(by_im[:, 1], S.powers[:, 1, CL]))
            op(dve.tensor_scalar(by_im[:, 0], S.powers[:, 1, CL], -1.0, None, ALU.mult))

            def step(c, base, out):
                link = linker(dve, stepped, base)

                def at(buf, r):
                    return buf[:, r, :, bass.ds(c, 1)].rearrange("p a c -> p (a c)")

                dve.tensor_tensor(t1[:, :, :], S.start[:, :, :, bass.ds(c, 1)].rearrange("p r a c -> p r (a c)"),
                                  by_re[:, :, :], ALU.mult)
                dve.tensor_tensor(t2[:, 0], at(S.start, 1), by_im[:, 0], ALU.mult)
                link(dve.tensor_tensor(t2[:, 1], at(S.start, 0), by_im[:, 1], ALU.mult))
                link(dve.tensor_tensor(t2[:, :, :], t2[:, :, :],
                                       incr[:, :, :, bass.ds(c, 1)].rearrange("p r a c -> p r (a c)"), ALU.add))
                link(dve.tensor_tensor(out, t1[:, :, :], t2[:, :, :], ALU.add))

            with dve.Fori(0, PC - 1) as c:
                step(c, c * 3, S.start[:, :, :, bass.ds(c + 1, 1)].rearrange("p r a c -> p r (a c)"))
            step(PC - 1, 3 * (PC - 1), end[:, :, :])
            for b in range(DEC_BATCH):
                step(PC + b, 3 * (PC + b), ends[:, :, b])
            for n in range(5):
                dve.wait_ge(turned.h, n + 1)
                m = P if n < 4 else 2 * GPAIRS
                dve.tensor_copy(out_rows[0:m, n, :], T.ps[0:m, n, 0:P]).then_inc(out_moved.h, 1)

        @block.tensor
        def _(pe):
            pe.wait_ge(stepped.h, 3 * NC_)
            for r in range(2):
                for j in range(2):
                    pe.transpose(T.ps[:, 2 * r + j, 0:P],
                                 ends[:, r, 4 * j:4 * j + 4, :].rearrange("p b a -> p (b a)"), T.ident[:, :])\
                      .then_inc(turned.h, 1)
            pe.transpose(T.ps[0:2 * GPAIRS, 4, 0:P], end[:, :, :].rearrange("p r a -> p (r a)"), T.ident[:, :]).then_inc(turned.h, 1)

        @block.sync
        def _(sp):
            for r, part in enumerate(("re", "im")):
                for j in range(2):
                    sp.wait_ge(out_moved.h, 2 * r + j + 1)
                    sp.dma_start(O[f"s5_{part}_sample"].rearrange("(j b) (a s) p -> j (b a) (s p)", j=2, s=2)[j],
                                 out_rows[:, 2 * r + j, :]).then_inc(stored.h, 16)
            sp.wait_ge(out_moved.h, 5)
            for r, part in enumerate(("re", "im")):
                sp.dma_start(O[f"s5_{part}_prompt"].rearrange("(a s) p -> a (s p)", s=2),
                             out_rows[r * GPAIRS:(r + 1) * GPAIRS, 4, :]).then_inc(stored.h, 16)
            sp.wait_ge(stored.h, 6 * 16)

        @block.gpsimd
        def _(pool):
            def op(ins):
                T.pool_chain(pool, ins)

            for q in range(GPAIRS // 4):
                a = slice(4 * q, 4 * q + 4)
                wide = [P, 4, CL + 1, GH]
                c = [S.c_t[:, r, a, :].unsqueeze(2).to_broadcast(wide) for r in range(2)]
                f = [S.powers[:, r, :, a].rearrange("p k a -> p a k").unsqueeze(3).to_broadcast(wide)
                     for r in range(2)]
                out = c_pow[:, 0, a]
                pool.tensor_tensor(m2[:, :, :, :], c[0], f[0], ALU.mult)
                op(pool.tensor_tensor(m3[:, :, :, :], c[1], f[1], ALU.mult))
                op(pool.tensor_tensor(out, m2[:, :, :, :], m3[:, :, :, :], ALU.subtract))
                out = c_pow[:, 1, a]
                pool.tensor_tensor(m2[:, :, :, :], c[0], f[1], ALU.mult)
                op(pool.tensor_tensor(m3[:, :, :, :], c[1], f[0], ALU.mult))
                op(pool.tensor_tensor(m2[:, :, :, :], m2[:, :, :, :], m3[:, :, :, :], ALU.add))
                op(pool.tensor_scalar(out, m2[:, :, :, :], -1.0, None, ALU.mult))


def phase_s5_outputs(T, S, c_pow):
    nc = T.nc
    names = ("kernels", "placed", "mixed", "gelued", "turned", "rounded", "rested")
    kernels, placed, mixed, gelued, turned, rounded, rested = (Count(T.ctx, nc, "s5o_" + n) for n in names)
    zeroed = Count(T.ctx, nc, "s5o_zeroed")
    spread = [Count(T.ctx, nc, f"s5o_spread{i}") for i in range(2)]
    A = GT // 2
    with ExitStack() as ctx:
        def sb(name, shape, dt=F32):
            return ctx.enter_context(nc.sbuf_tensor("s5o_" + name, shape, dt))

        kernel_of = sb("kernel", [GH, 2, 2 * A, 2 * P])
        toeplitz = sb("toeplitz", [P, 2, 2 * A, P])
        diag = sb("diag", [GH, 2 * A, GH])
        gel = sb("gel", [P, CL, A, 2, GH])
        block = ctx.enter_context(nc.Block())
        half = [slice(0, HD), slice(HD, P)]

        @block.tensor
        def _(pe):
            def make_kernels(e):
                if e:
                    pe.wait_ge(placed.h, e)
                for s in range(2):
                    for a in range(A):
                        gp = A * e + a
                        for r in range(2):
                            mm = pe.matmul(T.ps[0:GH, s, a * P:(a + 1) * P], S.b_bar[half[s], r, gp, :],
                                           c_pow[half[s], r, gp, 0:CL, :].rearrange("p k h -> p (k h)"),
                                           start=(r == 0), stop=(r == 1))
                mm.then_inc(kernels.h, 1)

            def outputs(e):
                pe.wait_ge(spread[e % 2].h, (e // 2 + 1) * CL * 16)
                if e:
                    pe.wait_ge(gelued.h, 2 * e)
                for s in range(2):
                    for a in range(A):
                        gp = A * e + a
                        out = T.ps[0:NC_, 2 + s, a * P:(a + 1) * P]
                        pe.matmul(out, S.u[:, 2 * gp + s, :], toeplitz[:, e % 2, s * A + a, :], start=True, stop=False)
                        for r in range(2):
                            mm = pe.matmul(out, S.start[half[s], r, gp, :],
                                           c_pow[half[s], r, gp, 1:CL + 1, :].rearrange("p k h -> p (k h)"),
                                           start=False, stop=(r == 1))
                mm.then_inc(mixed.h, 1)

            def turn(e):
                pe.wait_ge(gelued.h, 2 * e + 2)
                if e:
                    pe.wait_ge(rested.h, e)
                for t in range(CL):
                    mm = pe.transpose(T.ps[:, 4 + t // 4, (t % 4) * NC_:(t % 4 + 1) * NC_],
                                      gel[0:NC_, t].rearrange("p a s h -> p (a s h)"), T.ident[0:NC_, 0:NC_])
                mm.then_inc(turned.h, 1)

            make_kernels(0)
            for e in range(KT):
                if e + 1 < KT:
                    make_kernels(e + 1)
                outputs(e)
                turn(e)

        @block.vector
        def _(dve):
            def place(e):
                dve.wait_ge(kernels.h, e + 1)
                if e >= 2:
                    dve.wait_ge(spread[e % 2].h, (e // 2) * CL * 16)
                dst = kernel_of[:, e % 2, :, P:2 * P]
                T.dve_chain(dve, dve.tensor_copy(dst.rearrange("p (s a) k -> p s a k", s=2),
                                                 T.ps[0:GH, 0:2, :].rearrange("p s (a k) -> p s a k", a=A)))
                skip = S.skip[:, GT * e:GT * (e + 1)].rearrange("p (a s) -> p s a", s=2)
                for s in range(2):
                    last = dve.tensor_tensor(diag[:, s * A:(s + 1) * A, :],
                                             T.ident[0:GH, 0:GH].unsqueeze(1).to_broadcast([GH, A, GH]),
                                             skip[:, s].unsqueeze(2).to_broadcast([GH, A, GH]), ALU.mult)
                T.dve_chain(dve, last)
                dve.tensor_tensor(dst[:, :, 0:GH], dst[:, :, 0:GH], diag[:, :, :], ALU.add).then_inc(placed.h, 1)
                dve.wait_ge(placed.h, e + 1)

            def rest(e):
                dve.wait_ge(rounded.h, e + 1)
                dve.tensor_tensor(T.x_lo[:, e].rearrange("p (c b t) -> p b t c", b=2, t=4),
                                  T.ps[:, 4:6, 0:4 * NC_].rearrange("p b (t c) -> p b t c", t=4),
                                  T.x_hi[:, e].rearrange("p (c b t) -> p b t c", b=2, t=4).bitcast(F32),
                                  ALU.subtract).then_inc(rested.h, 1)

            dve.memset(kernel_of[:, :, :, 0:P], 0.0).then_inc(zeroed.h, 1)
            dve.wait_ge(zeroed.h, 1)
            place(0)
            for e in range(KT):
                if e + 1 < KT:
                    place(e + 1)
                rest(e)

        @block.scalar
        def _(act):
            for e in range(KT):
                act.wait_ge(mixed.h, e + 1)
                if e:
                    act.wait_ge(turned.h, e)
                for s in range(2):
                    act.activation(gel[0:NC_, :, :, s, :].rearrange("p t a h -> p a t h"),
                                   T.ps[0:NC_, 2 + s, :].rearrange("p (a t h) -> p a t h", a=A, h=GH),
                                   ACT.Gelu_apprx_tanh).then_inc(gelued.h, 1)
                act.wait_ge(turned.h, e + 1)
                act.activation(T.x_hi[:, e].rearrange("p (c b t) -> p b t c", b=2, t=4),
                               T.ps[:, 4:6, 0:4 * NC_].rearrange("p b (t c) -> p b t c", t=4), ACT.Copy)\
                   .then_inc(rounded.h, 1)

        @block.sync
        def _(sp):
            for e in range(KT):
                sp.wait_ge(placed.h, e + 1)
                if e >= 2:
                    sp.wait_ge(mixed.h, e - 1)
                for t in range(CL):
                    sp.dma_start(toeplitz[t * GH:(t + 1) * GH, e % 2],
                                 kernel_of[:, e % 2, :, P - t * GH:2 * P - t * GH]).then_inc(spread[e % 2].h, 16)


def host_tables():
    half = HD // 2
    inv = (10000.0 ** (-np.arange(half) / half)).astype(np.float32)
    pos = np.zeros((P, TT), np.float32)
    step = np.zeros((P, TT), np.float64)
    for t in range(PT):
        pos[:, t] = t * P + np.arange(P)
        step[:, t] = pos[:, t]
    pos[NS:, PT] = PAST_LEN + np.arange(NS) % DEC_SEQ
    step[NS:, PT] = np.arange(NS) % DEC_SEQ
    ang = (pos[:, :, None] * inv).astype(np.float64)
    log_g = np.log1p(-np.exp2(-5.0 - np.arange(HEADS)))
    f = lambda a: np.ascontiguousarray(a, np.float32)
    at = np.arange(P)
    causal = np.where(at[None, :] <= at[:, None], 0.0, NEG)
    keep = at[None, :] >= at[:, None]
    s = np.arange(NS)
    keep_s = (s[None, :] >= s[:, None]) & (s[None, :] // DEC_SEQ == s[:, None] // DEC_SEQ)
    select = s[:, None] // DEC_SEQ == np.arange(DEC_BATCH)
    of_row = log_g.reshape(PAIRS, 2)[:, np.arange(P) // HD].T
    row_b, row_q = at // HD, at % DEC_SEQ
    past_mask = np.full((P, BP, NS), NEG)
    for bp in range(BP):
        seen = (s // DEC_SEQ == 2 * bp + row_b[:, None]) & (s % DEC_SEQ <= row_q[:, None])
        past_mask[:, bp][seen] = 0.0
    return {"past_mask": f(past_mask), "block_no": f(np.tile(np.arange(BLOCKS) + 1.0, (P, 1))), "causal": f(causal), "keep": f(keep), "keep_s": f(keep_s), "select": f(select),
            "power": f(np.exp(of_row * SEQ)), "power_s": f(np.exp(of_row * DEC_SEQ)), "ident": np.eye(P, dtype=np.float32), "rope_cos": f(np.cos(ang)),
            "rope_sin": f(np.stack([-np.sin(ang), np.sin(ang)], 2)),
            "decay_q": f(np.exp(log_g * (step[:, :, None] + 1))),
            "decay_k": f(np.exp(-log_g * (step[:, :, None] + 1)) * HD ** -0.5)}


def program(nc, I, O):
    rows = lambda a: a.rearrange("b s d -> (b s) d")
    ffn = [[(I[f"ffn{n}_w_gate"][layer], I[f"ffn{n}_w_up"][layer], I[f"ffn{n}_w_down"][layer]) for n in (1, 2)]
           for layer in range(DEPTH)]
    first = lambda w: [gate_piece(w[0], 0), gate_piece(w[1], 0)]
    w_in, w_out = I["w_in_ab"][0], I["w_out_ab"][0]
    s5_out, s5_gate = I["s5_w_out"][0], I["s5_w_gate"][0]
    with ExitStack() as ctx:
        T = open_trunk(ctx, nc)
        phase_load(T, rows(I["x_prompt"]), rows(I["x_sample"]), rows(I["ln_g"]), rows(I["ln_b"]), I["ident"],
                   first(ffn[0][0]))
        phase_ffn(T, *ffn[0][0], 0, [in_piece(w_in, 0), in_piece(w_in, 1)])
        M = Trunk()
        with ExitStack() as actx:
            open_mix(actx, nc, M, "attention")
            with ExitStack() as rctx:
                open_mix(rctx, nc, M, "retention")
                phase_project(T, M, w_in, I["rope_cos"], I["rope_sin"], I["decay_q"], I["decay_k"], O,
                              [out_piece(w_out, 0), out_piece(w_out, 1)])
                phase_attend_prompt(T, M, I["causal"])
                phase_retain_prompt(T, M, I["keep"], I["power"], O["state_prompt"])
                phase_retain_samples(T, M, I["state_ret"][0], I["keep_s"], I["select"], I["power_s"],
                                     O["state_sample"])
            phase_attend_samples(T, M, I["cache_k"][0], I["cache_v"][0], I["page_table"], I["past_mask"],
                                 I["block_no"], I["cache_k"].shape[1])
        phase_out(T, w_out, None, 1, first(ffn[0][1]))
        phase_ffn(T, *ffn[0][1], 2, first(ffn[1][0]))
        phase_ffn(T, *ffn[1][0], 3, [out_piece(s5_out, 0), out_piece(s5_gate, 0)])
        with ExitStack() as sctx:
            S = open_s5(sctx, nc)
            phase_s5_constants(T, S, I)
            phase_s5_inputs(T, S)
            c_pow = sctx.enter_context(nc.sbuf_tensor("s5_c_pow", [P, 2, GPAIRS, CL + 1, GH], F32))
            phase_s5_scan(T, S, c_pow, O)
            phase_s5_outputs(T, S, c_pow)
        phase_out(T, s5_out, s5_gate, 4, first(ffn[1][1]))
        phase_ffn(T, *ffn[1][1], 5, None)
        phase_store(T, O["y_prompt"], O["y_sample"])


OUTPUTS = (
    ("y_prompt", (SEQ, D_MODEL), (1, SEQ, D_MODEL)),
    ("y_sample", (NS, D_MODEL), (DEC_BATCH, DEC_SEQ, D_MODEL)),
    ("k_prompt", (SEQ, MIX), (1, 1, PT, PAGE, HEADS, HD)),
    ("v_prompt", (SEQ, MIX), (1, 1, PT, PAGE, HEADS, HD)),
    ("k_sample", (NS, MIX), (1, DEC_BATCH, DEC_SEQ, HEADS, HD)),
    ("v_sample", (NS, MIX), (1, DEC_BATCH, DEC_SEQ, HEADS, HD)),
    ("state_prompt", (HEADS, HD, HD), (1, 1, HEADS, HD, HD)),
    ("state_sample", (DEC_BATCH, HEADS, HD, HD), (1, DEC_BATCH, HEADS, HD, HD)),
    ("s5_re_prompt", (GROUPS, STATES), (1, 1, GROUPS, STATES)),
    ("s5_im_prompt", (GROUPS, STATES), (1, 1, GROUPS, STATES)),
    ("s5_re_sample", (DEC_BATCH, GROUPS, STATES), (1, DEC_BATCH, GROUPS, STATES)),
    ("s5_im_sample", (DEC_BATCH, GROUPS, STATES), (1, DEC_BATCH, GROUPS, STATES)),
)


def kernel(**inputs):
    import concourse.bacc as bacc
    from concourse.bass_utils import run_bass_kernel_spmd

    nc = bacc.Bacc("TRN2", target_bir_lowering=False, num_devices=1)
    arrays = {name: np.ascontiguousarray(a) for name, a in inputs.items()}
    arrays.update(host_tables())
    I = {name: nc.dram_tensor(f"in_{name}", a.shape, mybir.dt.from_np(a.dtype), kind="ExternalInput").ap()
         for name, a in arrays.items()}
    O = {name: nc.dram_tensor(f"out_{name}", shape, F32, kind="ExternalOutput").ap() for name, shape, _ in OUTPUTS}
    program(nc, I, O)
    r = run_bass_kernel_spmd(nc, [{f"in_{name}": a for name, a in arrays.items()}], core_ids=[0])
    return tuple(np.reshape(r.results[0][f"out_{name}"], shape) for name, _, shape in OUTPUTS)
```

```python
import math
from contextlib import ExitStack

import concourse.bass as bass
import numpy as np
from concourse import mybir
from concourse.alu_op_type import AluOpType as ALU

F32 = mybir.dt.float32
F32R = mybir.dt.float32r
I32 = mybir.dt.int32
ACT = mybir.ActivationFunctionType
AX_X = mybir.AxisListType.X

P = 128
D_MODEL, SEQ, DEC_BATCH, DEC_SEQ, PAST_LEN, PAGE = 1024, 512, 8, 8, 1024, 128
NS = DEC_BATCH * DEC_SEQ
NT = SEQ + NS
NH = NT // 2
KT = D_MODEL // P
D_FF = ((8 * D_MODEL // 3 + 127) // 128) * 128
FT = D_FF // P
HF = FT // 2
DEPTH = 2
ALPHA = (2 * DEPTH) ** 0.25
LN_EPS = 1e-5
GN_EPS = 1e-6
NEG = -1e30
PT = SEQ // P
HD = 64
HEADS = 8
PAIRS = HEADS // 2
MIX = HEADS * HD


class Count:

    def __init__(self, ctx, nc, name):
        self.h = ctx.enter_context(nc.semaphore(name))
        self.n = 0

    def done(self, k):
        return self.n + k

    def close(self, k):
        self.n += k


class Chain:

    def __init__(self, ctx, nc, name):
        self.h = ctx.enter_context(nc.semaphore(name))
        self.n = 0

    def __call__(self, eng, ins):
        self.n += 1
        ins.then_inc(self.h, 1)
        eng.wait_ge(self.h, self.n)


class Trunk:
    pass


def halves(ap):
    return ap.rearrange("p (n t) -> p n t", n=2)


def open_trunk(ctx, nc):
    T = Trunk()
    T.ctx, T.nc = ctx, nc

    def sb(name, shape, dt=F32):
        return ctx.enter_context(nc.sbuf_tensor(name, shape, dt))

    def count(name):
        return Count(ctx, nc, name)

    T.x = sb("x", [P, KT, NT])
    T.x_hi = sb("x_hi", [P, KT, NT], F32R)
    T.x_lo = sb("x_lo", [P, KT, NT], F32R)
    T.w_raw = sb("w_raw", [P, 2, HF * P])
    T.w_hi = sb("w_hi", [P, 2, HF * P], F32R)
    T.w_lo = sb("w_lo", [P, 2, HF * P], F32R)
    T.ident = sb("ident", [P, P])
    T.ones = sb("ones", [P, P])
    T.ln_gain = sb("ln_gain", [P, DEPTH * 3, KT])
    T.ln_bias = sb("ln_bias", [P, DEPTH * 3, KT])
    T.eps = sb("eps", [P, 2])
    T.ps = ctx.enter_context(nc.psum_tensor("ps", [P, 8, 512], F32))
    T.w_loaded = [count("w_loaded0"), count("w_loaded1")]
    T.w_hi_ready = [count("w_hi_ready0"), count("w_hi_ready1")]
    T.w_split = [count("w_split0"), count("w_split1")]
    T.w_used = [count("w_used0"), count("w_used1")]
    T.pieces = 0
    T.const_ready, T.const_loaded = count("const_ready"), count("const_loaded")
    T.silu_done, T.glu_done, T.h_rounded, T.h_done = map(count, ("silu_done", "glu_done", "h_rounded", "h_done"))
    T.res_done, T.acc_added, T.sum_done, T.centred = map(count, ("res_done", "acc_added", "sum_done", "centred"))
    T.squared, T.var_done, T.rstd_ready, T.normed = map(count, ("squared", "var_done", "rstd_ready", "normed"))
    T.affine_done, T.x_rounded, T.x_ready = map(count, ("affine_done", "x_rounded", "x_ready"))
    T.pe_done, T.dve_done, T.act_done, T.pool_done = map(count, ("pe_done", "dve_done", "act_done", "pool_done"))
    T.stored = count("stored")
    T.act_chain = Chain(ctx, nc, "act_chain")
    T.dve_chain = Chain(ctx, nc, "dve_chain")
    T.pool_chain = Chain(ctx, nc, "pool_chain")
    return T



def load_piece(T, sp, slot, u, src, shape=None):
    n = src.shape[1] * src.shape[2]
    dst = T.w_raw[:, slot, 0:n].rearrange("p (a b) -> p a b", a=src.shape[1])
    sp.wait_ge(T.w_split[slot].h, u + 1)
    sp.dma_start(dst, src).then_inc(T.w_loaded[slot].h, 16)


def round_piece(T, act, slot, u, n):
    act.wait_ge(T.w_loaded[slot].h, (u + 1) * 16)
    act.wait_ge(T.w_used[slot].h, u + 1)
    act.activation(T.w_hi[:, slot, 0:n], T.w_raw[:, slot, 0:n], ACT.Copy).then_inc(T.w_hi_ready[slot].h, 1)


def rest_piece(T, dve, slot, u, n):
    dve.wait_ge(T.w_hi_ready[slot].h, u + 1)
    dve.tensor_tensor(T.w_lo[:, slot, 0:n], T.w_raw[:, slot, 0:n], T.w_hi[:, slot, 0:n].bitcast(F32),
                      ALU.subtract).then_inc(T.w_split[slot].h, 1)


def product3(pe, out, w_hi, w_lo, m_hi, m_lo, first, last):
    pe.matmul(out, w_hi, m_hi, start=first, stop=False)
    pe.matmul(out, w_hi, m_lo, start=False, stop=False)
    return pe.matmul(out, w_lo, m_hi, start=False, stop=last)



class Norm:

    def __init__(self, T, row, scale, acc, acc_steps, squares, rstd, pieces, products):
        self.acc_steps, self.pieces, self.products = acc_steps, pieces, products
        self.T, self.row, self.acc, self.squares, self.rstd = T, row, acc, squares, rstd
        self.eps = T.eps[:, int(scale) - 1:int(scale)]
        self.mean_ps = T.ps[:, 4:6, 0:NH]
        self.var_ps = T.ps[:, 6:8, 0:NH]

    def tensor(self, pe):
        T = self.T
        pe.wait_ge(T.acc_added.h, T.acc_added.done(self.acc_steps))
        for n in range(2):
            mm = pe.matmul(self.mean_ps[:, n], T.ones[:, :], self.acc[:, n * NH:(n + 1) * NH],
                           start=True, stop=True)
        mm.then_inc(T.sum_done.h, 1)
        for k in range(KT):
            pe.wait_ge(T.squared.h, T.squared.done(k + 1))
            for n in range(2):
                mm = pe.matmul(self.var_ps[:, n], T.ones[:, :], self.squares[:, k % 2, n * NH:(n + 1) * NH],
                               start=(k == 0), stop=(k == KT - 1))
            mm.then_inc(T.var_done.h, 1)

    def scalar(self, act):
        T = self.T
        if self.pieces is not None:
            for slot in range(2):
                round_piece(T, act, slot, self.pieces, KT * P)
        for k in range(KT):
            act.wait_ge(T.centred.h, T.centred.done(k + 1))
            if k >= 2:
                act.wait_ge(T.var_done.h, T.var_done.done(k - 1))
            act.activation(self.squares[:, k % 2], T.x[:, k], ACT.Square).then_inc(T.squared.h, 1)
        act.wait_ge(T.var_done.h, T.var_done.done(KT))
        act.activation(halves(self.rstd[:, :]), self.var_ps, ACT.Sqrt, bias=self.eps).then_inc(T.rstd_ready.h, 1)
        for k in range(KT):
            act.wait_ge(T.normed.h, T.normed.done(k + 1))
            if self.products:
                act.activation(T.x_hi[:, k], T.x[:, k], ACT.Identity, bias=self.bias(k)).then_inc(T.x_rounded.h, 1)
            else:
                act.activation(T.x[:, k], T.x[:, k], ACT.Identity, bias=self.bias(k)).then_inc(T.affine_done.h, 1)
        if self.products:
            for k in range(KT - self.ON_POOL):
                act.wait_ge(T.x_ready.h, T.x_ready.done(k + 1))
                act.activation(T.x[:, k], T.x[:, k], ACT.Identity, bias=self.bias(k)).then_inc(T.affine_done.h, 1)

    ON_POOL = 2

    def bias(self, k):
        return self.T.ln_bias[:, self.row, k:k + 1]

    def vector(self, dve):
        T = self.T
        dve.wait_ge(T.sum_done.h, T.sum_done.done(1))
        for k in range(KT):
            dve.scalar_tensor_tensor(halves(T.x[:, k]), self.mean_ps, -1.0 / D_MODEL, halves(T.x[:, k]),
                                     ALU.mult, ALU.add).then_inc(T.centred.h, 1)
        if self.pieces is not None:
            for slot in range(2):
                rest_piece(T, dve, slot, self.pieces, KT * P)
        dve.wait_ge(T.rstd_ready.h, T.rstd_ready.done(1))
        dve.reciprocal(self.rstd[:, :], self.rstd[:, :]).then_inc(T.rstd_ready.h, 1)
        dve.wait_ge(T.rstd_ready.h, T.rstd_ready.done(2))

        def rest(k):
            dve.wait_ge(T.x_rounded.h, T.x_rounded.done(k + 1))
            dve.scalar_tensor_tensor(T.x_lo[:, k], T.x[:, k], self.bias(k), T.x_hi[:, k].bitcast(F32),
                                     ALU.add, ALU.subtract).then_inc(T.x_ready.h, 1)

        for k in range(KT):
            dve.scalar_tensor_tensor(T.x[:, k], T.x[:, k], T.ln_gain[:, self.row, k:k + 1], self.rstd[:, :],
                                     ALU.mult, ALU.mult).then_inc(T.normed.h, 1)
            if self.products and k >= 2:
                rest(k - 2)
        if self.products:
            for k in range(KT - 2, KT):
                rest(k)

    def gpsimd(self, pool):
        T = self.T
        if self.products:
            for k in range(KT - self.ON_POOL, KT):
                pool.wait_ge(T.x_ready.h, T.x_ready.done(k + 1))
                pool.tensor_scalar(T.x[:, k], T.x[:, k], self.bias(k), None, ALU.add).then_inc(T.affine_done.h, 1)

    def close(self):
        T = self.T
        split = KT if self.products else 0
        for c, k in ((T.acc_added, self.acc_steps), (T.sum_done, 1), (T.squared, KT), (T.var_done, KT), (T.centred, KT),
                     (T.normed, KT), (T.affine_done, KT), (T.rstd_ready, 2), (T.x_rounded, split), (T.x_ready, split)):
            c.close(k)



def phase_load(T, x_prompt, x_sample, ln_g, ln_b, ident, first):
    nc = T.nc
    with ExitStack() as ctx:
        rows = ctx.enter_context(nc.sbuf_tensor("x_rows", [P, PT + 1, D_MODEL], F32))
        credit = ctx.enter_context(nc.sbuf_tensor("credit", [P, 8], F32))
        block = ctx.enter_context(nc.Block())
        loaded = T.const_loaded

        @block.sync
        def _(sp):
            sp.dma_start(T.ident[:, :], ident).then_inc(loaded.h, 16)
            for t in range(PT):
                sp.dma_start(rows[:, t], x_prompt[t * P:(t + 1) * P, :]).then_inc(loaded.h, 16)
            sp.dma_start(rows[NS:P, PT], x_sample).then_inc(loaded.h, 16)
            with nc.allow_non_contiguous_dma(reason="layer norm gains and biases, feature-major"):
                sp.dma_start(T.ln_gain[:, :, :], ln_g.rearrange("r (k p) -> p r k", p=P)).then_inc(loaded.h, 16)
                sp.dma_start(T.ln_bias[:, :, :], ln_b.rearrange("r (k p) -> p r k", p=P)).then_inc(loaded.h, 16)
            for slot in range(2):
                load_piece(T, sp, slot, T.pieces, first[slot])

        @block.tensor
        def _(pe):
            pe.wait_ge(loaded.h, (PT + 4) * 16)
            for k in range(KT):
                b = 2 * (k % 4)
                if k >= 4:
                    pe.wait_ge(T.dve_done.h, T.dve_done.done(k - 3))
                for t in range(PT):
                    pe.transpose(T.ps[:, b, t * P:(t + 1) * P], rows[:, t, k * P:(k + 1) * P], T.ident[:, :])
                pe.transpose(T.ps[:, b + 1, 0:NS], rows[NS:P, PT, k * P:(k + 1) * P], T.ident[NS:P, NS:P])\
                  .then_inc(T.pe_done.h, 1)

        @block.vector
        def _(dve):
            dve.memset(T.ones[:, :], 1.0).then_inc(T.const_ready.h, 1)
            for scale in (1, 2):
                dve.memset(T.eps[:, scale - 1:scale], LN_EPS * D_MODEL * scale * scale).then_inc(T.const_ready.h, 1)
            for slot in range(2):
                dve.memset(credit[:, slot:slot + 1], 0.0).then_inc(T.w_split[slot].h, 1)
                dve.memset(credit[:, 2 + slot:3 + slot], 0.0).then_inc(T.w_used[slot].h, 1)
                dve.memset(credit[:, 4 + slot:5 + slot], 0.0).then_inc(T.glu_done.h, 1)
                dve.memset(credit[:, 6 + slot:7 + slot], 0.0).then_inc(T.res_done.h, 1)
            dve.wait_ge(loaded.h, (PT + 4) * 16)
            dve.tensor_scalar(T.ln_gain[:, :, :], T.ln_gain[:, :, :], math.sqrt(D_MODEL), None, ALU.mult)\
               .then_inc(T.const_ready.h, 1)
            for k in range(KT):
                b = 2 * (k % 4)
                dve.wait_ge(T.pe_done.h, T.pe_done.done(k + 1))
                T.dve_chain(dve, dve.tensor_copy(T.x[:, k, 0:SEQ], T.ps[:, b, 0:SEQ]))
                T.dve_chain(dve, dve.tensor_copy(T.x[:, k, SEQ:NT], T.ps[:, b + 1, 0:NS]))
                T.dve_chain(dve, dve.tensor_copy(T.x_hi[:, k], T.x[:, k]))
                dve.tensor_tensor(T.x_lo[:, k], T.x[:, k], T.x_hi[:, k].bitcast(F32), ALU.subtract)\
                   .then_inc(T.dve_done.h, 1)
            for slot in range(2):
                rest_piece(T, dve, slot, T.pieces, KT * P)

        @block.scalar
        def _(act):
            for slot in range(2):
                round_piece(T, act, slot, T.pieces, KT * P)
    T.const_loaded.close((PT + 4) * 16)
    T.pe_done.close(KT)
    T.dve_done.close(KT)
    T.glu_done.close(2)
    T.res_done.close(2)


def gate_piece(w, ft):
    return w.rearrange("(k p) f -> p k f", p=P)[:, :, bass.ds(ft * P, P)]


def down_piece(w, half, d):
    return w[half * HF * P:(half + 1) * HF * P, :].rearrange("(f p) d -> p f d", p=P)[:, :, bass.ds(d * P, P)]


def phase_ffn(T, w_gate, w_up, w_down, row, nxt, products=True, beside=None):
    nc = T.nc
    U = T.pieces
    G = KT * P
    D = HF * P
    LOOPED = FT - 2
    DLOOPED = KT - 2
    with ExitStack() as ctx:
        def sb(name, shape, dt=F32):
            return ctx.enter_context(nc.sbuf_tensor(f"{name}_{row}", shape, dt))

        h_hi = sb("h_hi", [P, FT, NT], F32R)
        h_lo = sb("h_lo", [P, FT, NT], F32R)
        gate = sb("gate", [P, 2, NT])
        prod = sb("prod", [P, 2, NT])
        acc, rstd, squares = prod[:, 0], prod[:, 1], gate
        norm = Norm(T, row, 2.0, acc, KT + 1, squares, rstd, U + FT + KT if nxt else None, products)
        silu0, glu0, hr0, h0 = T.silu_done.n, T.glu_done.n, T.h_rounded.n, T.h_done.n
        res0, acc0 = T.res_done.n, T.acc_added.n
        if beside:
            beside.open(ctx)
        block = ctx.enter_context(nc.Block())

        @block.sync
        def _(sp):
            with sp.Fori(1, FT) as ft:
                for slot, w in ((0, w_gate), (1, w_up)):
                    src = gate_piece(w, ft)
                    load_piece(T, sp, slot, U + ft, src)
            with sp.Fori(0, KT) as d:
                for slot in range(2):
                    src = down_piece(w_down, slot, d)
                    load_piece(T, sp, slot, U + FT + d, src)
            for slot in range(2):
                if nxt:
                    load_piece(T, sp, slot, U + FT + KT, nxt[slot])

        @block.tensor
        def _(pe):
            def gate_up(ft, j):
                pe.wait_ge(T.glu_done.h, ft + (glu0 - 1))
                for slot in range(2):
                    pe.wait_ge(T.w_split[slot].h, ft + (U + 2))
                    for n in range(2):
                        for k in range(KT):
                            cols = slice(n * NH, (n + 1) * NH)
                            mm = product3(pe, T.ps[:, 4 * j + 2 * slot + n, 0:NH],
                                          T.w_hi[:, slot, k * P:(k + 1) * P], T.w_lo[:, slot, k * P:(k + 1) * P],
                                          T.x_hi[:, k, cols], T.x_lo[:, k, cols], k == 0, k == KT - 1)
                    mm.then_inc(T.w_used[slot].h, 1)

            def down(d, j):
                pe.wait_ge(T.res_done.h, d + (res0 - 1))
                for slot in range(2):
                    pe.wait_ge(T.h_done.h, h0 + FT - 1 + slot)
                    pe.wait_ge(T.w_split[slot].h, d + (U + FT + 2))
                    for n in range(2):
                        for f in range(HF):
                            cols = slice(n * NH, (n + 1) * NH)
                            ft = slot * HF + f
                            mm = product3(pe, T.ps[:, 2 * j + n, 0:NH],
                                          T.w_hi[:, slot, f * P:(f + 1) * P], T.w_lo[:, slot, f * P:(f + 1) * P],
                                          h_hi[:, ft, cols], h_lo[:, ft, cols], ft == 0, ft == FT - 1)
                    mm.then_inc(T.w_used[slot].h, 1)

            with pe.Fori(0, FT, 2) as ft:
                for j in range(2):
                    gate_up(ft + j, j)
            with pe.Fori(0, KT, 2) as d:
                for j in range(2):
                    down(d + j, j)
            norm.tensor(pe)

        @block.scalar
        def _(act):
            def step(ft, j, n):
                for slot in range(2):
                    round_piece(T, act, slot, ft + (U + 1), n)
                act.wait_ge(T.w_used[1].h, ft + (U + 2))
                act.activation(halves(gate[:, j]), T.ps[:, 4 * j:4 * j + 2, 0:NH], ACT.Silu)\
                   .then_inc(T.silu_done.h, 1)

            with act.Fori(0, LOOPED, 2) as ft:
                for j in range(2):
                    step(ft + j, j, G)
            step(FT - 2, 0, G)
            step(FT - 1, 1, D)
            with act.Fori(1, KT) as d:
                for slot in range(2):
                    round_piece(T, act, slot, d + (U + FT), D)
            norm.scalar(act)

        @block.vector
        def _(dve):
            def step(ft, j, n):
                for slot in range(2):
                    rest_piece(T, dve, slot, ft + (U + 1), n)
                dve.wait_ge(T.silu_done.h, ft + (silu0 + 1))
                dve.tensor_tensor(halves(prod[:, j]), halves(gate[:, j]), T.ps[:, 4 * j + 2:4 * j + 4, 0:NH],
                                  ALU.mult).then_inc(T.glu_done.h, 1)
                dve.wait_ge(T.glu_done.h, ft + (glu0 + 1))
                hi = h_hi[:, bass.ds(ft, 1), :].rearrange("p a t -> p (a t)")
                lo = h_lo[:, bass.ds(ft, 1), :].rearrange("p a t -> p (a t)")
                dve.tensor_copy(hi, prod[:, j]).then_inc(T.h_rounded.h, 1)
                dve.wait_ge(T.h_rounded.h, ft + (hr0 + 1))
                dve.tensor_tensor(lo, prod[:, j], hi.bitcast(F32), ALU.subtract).then_inc(T.h_done.h, 1)

            with dve.Fori(0, LOOPED, 2) as ft:
                for j in range(2):
                    step(ft + j, j, G)
            step(FT - 2, 0, G)
            step(FT - 1, 1, D)
            dve.wait_ge(T.h_done.h, h0 + FT)
            dve.memset(acc, 0.0).then_inc(T.acc_added.h, 1)

            def add(d, j):
                dve.wait_ge(T.w_used[1].h, d + (U + FT + 2))
                xd = T.x[:, bass.ds(d, 1), :].rearrange("p a t -> p (a t)")
                dve.scalar_tensor_tensor(halves(xd), halves(xd), 2.0 * ALPHA, T.ps[:, 2 * j:2 * j + 2, 0:NH],
                                         ALU.mult, ALU.add).then_inc(T.res_done.h, 1)
                dve.wait_ge(T.res_done.h, d + (res0 + 1))
                dve.wait_ge(T.acc_added.h, d + (acc0 + 1))
                dve.tensor_tensor(acc, acc, xd, ALU.add).then_inc(T.acc_added.h, 1)

            with dve.Fori(0, DLOOPED, 2) as d:
                for j in range(2):
                    for slot in range(2):
                        rest_piece(T, dve, slot, d + (j + U + FT + 1), D)
                    add(d + j, j)
            for slot in range(2):
                rest_piece(T, dve, slot, U + FT + KT - 1, D)
            add(KT - 2, 0)
            add(KT - 1, 1)
            norm.vector(dve)

        @block.gpsimd
        def _(pool):
            if beside:
                beside.gpsimd(pool)
            norm.gpsimd(pool)
    for c, k in ((T.silu_done, FT), (T.glu_done, FT), (T.h_rounded, FT), (T.h_done, FT), (T.res_done, KT)):
        c.close(k)
    T.pieces += FT + KT
    norm.close()


def phase_store(T, y_prompt, y_sample):
    nc = T.nc
    with ExitStack() as ctx:
        rows = ctx.enter_context(nc.sbuf_tensor("y_rows", [P, PT + 1, D_MODEL], F32))
        block = ctx.enter_context(nc.Block())
        banks = [(t, q) for t in range(PT + 1) for q in range(2)]

        @block.tensor
        def _(pe):
            for i, (t, q) in enumerate(banks):
                m = P if t < PT else NS
                if i >= 8:
                    pe.wait_ge(T.dve_done.h, T.dve_done.done(i - 7))
                for k in range(4):
                    mm = pe.transpose(T.ps[0:m, i % 8, k * P:(k + 1) * P],
                                      T.x[:, 4 * q + k, t * P:t * P + m], T.ident[:, :])
                mm.then_inc(T.pe_done.h, 1)

        @block.vector
        def _(dve):
            for i, (t, q) in enumerate(banks):
                m = P if t < PT else NS
                dve.wait_ge(T.pe_done.h, T.pe_done.done(i + 1))
                dve.tensor_copy(rows[0:m, t, q * 512:(q + 1) * 512], T.ps[0:m, i % 8, 0:512])\
                   .then_inc(T.dve_done.h, 1)

        @block.sync
        def _(sp):
            for t in range(PT + 1):
                sp.wait_ge(T.dve_done.h, T.dve_done.done(2 * t + 2))
                if t < PT:
                    sp.dma_start(y_prompt[t * P:(t + 1) * P, :], rows[:, t]).then_inc(T.stored.h, 16)
                else:
                    sp.dma_start(y_sample, rows[0:NS, t]).then_inc(T.stored.h, 16)
            sp.wait_ge(T.stored.h, T.stored.done((PT + 1) * 16))
    T.pe_done.close(len(banks))
    T.dve_done.close(len(banks))
    T.stored.close((PT + 1) * 16)



SECTIONS = 7
Q_A, K_A, V_A, Q_B, K_B, V_B, G_B = range(SECTIONS)
ROPED = (Q_A, K_A, Q_B, K_B)
TT = PT + 1
KPP = 2
SECTION_PIECES = KT // KPP


def tile_cols(t):
    return slice(t * P, (t + 1) * P) if t < PT else slice(NT - P, NT)


def in_piece(w_in, g):
    s, q = divmod(g, SECTION_PIECES)
    return w_in.rearrange("(k p) c -> p k c", p=P)[:, q * KPP:(q + 1) * KPP, s * MIX:(s + 1) * MIX]


def open_mix(ctx, nc, M, part):

    def sb(name, shape, dt=F32):
        return ctx.enter_context(nc.sbuf_tensor(name, shape, dt))

    if part == "attention":
        M.qaT, M.kaT = sb("qaT", [P, PAIRS, NT]), sb("kaT", [P, PAIRS, NT])
        M.va = sb("va", [P, TT, MIX])
    else:
        M.qbT, M.kbT = sb("qbT", [P, PAIRS, NT]), sb("kbT", [P, PAIRS, NT])
        M.kb, M.vb, M.gb = (sb(n, [P, TT, MIX]) for n in ("kb", "vb", "gb"))


def phase_project(T, M, w_in, rope_cos, rope_sin, decay_q, decay_k, O, nxt):
    nc = T.nc
    U = T.pieces
    NP = SECTIONS * SECTION_PIECES
    N = KPP * MIX
    staged, roped, turned, moved, k_stored, v_stored, tables = (
        Count(T.ctx, nc, n) for n in ("staged", "roped", "turned", "moved", "k_stored", "v_stored", "tables_loaded"))
    with ExitStack() as ctx:
        def sb(name, shape, dt=F32):
            return ctx.enter_context(nc.sbuf_tensor(name, shape, dt))

        stage, rot = sb("stage", [P, TT, MIX]), sb("rot", [P, TT, MIX])
        by_cos, by_sin = sb("by_cos", [P, MIX]), sb("by_sin", [P, MIX])
        cos, sin = sb("cos", [P, TT, HD // 2]), sb("sin", [P, TT, 2, HD // 2])
        dq, dk = sb("dq", [P, TT, HEADS]), sb("dk", [P, TT, HEADS])
        block = ctx.enter_context(nc.Block())

        def bank(s, t):
            return (TT * s + t) % 6

        @block.sync
        def _(sp):
            sp.dma_start(cos[:, :, :], rope_cos).then_inc(tables.h, 16)
            sp.dma_start(sin[:, :, :, :], rope_sin).then_inc(tables.h, 16)
            sp.dma_start(dq[:, :, :], decay_q).then_inc(tables.h, 16)
            sp.dma_start(dk[:, :, :], decay_k).then_inc(tables.h, 16)
            for g in range(2, NP):
                load_piece(T, sp, g % 2, U + g // 2, in_piece(w_in, g))
            for slot in range(2):
                load_piece(T, sp, slot, U + NP // 2, nxt[slot])

        @block.tensor
        def _(pe):
            def turn(r):
                src = M.kb if ROPED[r] == K_B else rot
                for t in range(TT):
                    pe.wait_ge(roped.h, TT * r + t + 1)
                    if TT * r + t >= 2:
                        pe.wait_ge(moved.h, TT * r + t - 1)
                    for p in range(PAIRS):
                        lo = 0 if t < PT else NS
                        mm = pe.transpose(T.ps[:, 6 + t % 2, p * P:p * P + P - lo],
                                          src[lo:P, t, p * P:(p + 1) * P], T.ident[lo:P, lo:P])
                    mm.then_inc(turned.h, 1)

            for g in range(NP):
                s, q = divmod(g, SECTION_PIECES)
                slot = g % 2
                pe.wait_ge(T.w_split[slot].h, U + g // 2 + 2)
                for t in range(TT):
                    if q == 0 and TT * s + t >= 6:
                        pe.wait_ge(staged.h, TT * s + t - 5)
                    for k in range(KPP):
                        cols = slice(k * MIX, (k + 1) * MIX)
                        kk = q * KPP + k
                        x_hi, x_lo = T.x_hi[:, kk, tile_cols(t)], T.x_lo[:, kk, tile_cols(t)]
                        w_hi, w_lo = T.w_hi[:, slot, cols], T.w_lo[:, slot, cols]
                        out = T.ps[:, bank(s, t), 0:MIX]
                        pe.matmul(out, x_hi, w_hi, start=(kk == 0), stop=False)
                        pe.matmul(out, x_hi, w_lo, start=False, stop=False)
                        mm = pe.matmul(out, x_lo, w_hi, start=False, stop=(kk == KT - 1))
                mm.then_inc(T.w_used[slot].h, 1)
                if q == 2 and s - 1 in ROPED:
                    turn(ROPED.index(s - 1))

        @block.scalar
        def _(act):
            def empty(s):
                act.wait_ge(T.w_used[1].h, U + (4 * s + 3) // 2 + 2)
                dst = {V_A: M.va, V_B: M.vb, G_B: M.gb}.get(s, stage)
                for t in range(TT):
                    if s in ROPED and s > 0:
                        act.wait_ge(roped.h, TT * (ROPED.index(s) - 1) + t + 1)
                    act.activation(dst[:, t], T.ps[:, bank(s, t), 0:MIX], ACT.Silu if s == G_B else ACT.Copy)\
                       .then_inc(staged.h, 1)

            def move(r):
                dst = (M.qaT, M.kaT, M.qbT, M.kbT)[r]
                for t in range(TT):
                    m = P if t < PT else NS
                    act.wait_ge(turned.h, TT * r + t + 1)
                    act.activation(dst[:, :, t * P:t * P + m],
                                   T.ps[:, 6 + t % 2, :].rearrange("p (a t) -> p a t", a=PAIRS)[:, :, 0:m],
                                   ACT.Copy).then_inc(moved.h, 1)

            for g in range(NP):
                if 2 <= g + 1 < NP:
                    round_piece(T, act, (g + 1) % 2, U + (g + 1) // 2, N)
                s, q = divmod(g, SECTION_PIECES)
                if q == 2 and s - 1 in ROPED:
                    move(ROPED.index(s - 1))
                if q == 3:
                    empty(s)
            for slot in range(2):
                round_piece(T, act, slot, U + NP // 2, KT * P)

        @block.vector
        def _(dve):
            def rotate(s, t):
                r = ROPED.index(s)
                dve.wait_ge(staged.h, TT * s + t + 1)
                heads = stage[:, t].rearrange("p (h j d) -> p h j d", h=HEADS, j=2)
                sums = by_sin[:, :].rearrange("p (h j d) -> p h j d", h=HEADS, j=2)
                flat = [P, HEADS * 2, HD // 2]
                dve.tensor_tensor(by_cos[:, :].rearrange("p (h d) -> p h d", d=HD // 2),
                                  stage[:, t].rearrange("p (h d) -> p h d", d=HD // 2),
                                  cos[:, t:t + 1, :].to_broadcast(flat), ALU.mult)
                for j in range(2):
                    last = dve.tensor_tensor(sums[:, :, j], heads[:, :, 1 - j],
                                             sin[:, t, j:j + 1, :].to_broadcast([P, HEADS, HD // 2]), ALU.mult)
                T.dve_chain(dve, last)
                dst = M.kb if s == K_B else rot
                if r and dst is rot:
                    dve.wait_ge(turned.h, TT * (r - 1) + t + 1)
                    if s == Q_B:
                        dve.wait_ge(k_stored.h, 16 * TT)
                last = dve.tensor_tensor(dst[:, t], by_cos[:, :], by_sin[:, :], ALU.add)
                if s in (Q_B, K_B):
                    T.dve_chain(dve, last)
                    d = (dq if s == Q_B else dk)[:, t, :].unsqueeze(2).to_broadcast([P, HEADS, HD])
                    last = dve.tensor_tensor(dst[:, t].rearrange("p (h d) -> p h d", h=HEADS),
                                             dst[:, t].rearrange("p (h d) -> p h d", h=HEADS), d, ALU.mult)
                last.then_inc(roped.h, 1)
                dve.wait_ge(roped.h, TT * r + t + 1)

            dve.wait_ge(tables.h, 64)
            for g in range(NP):
                if 2 <= g + 1 < NP:
                    rest_piece(T, dve, (g + 1) % 2, U + (g + 1) // 2, N)
                s, q = divmod(g, SECTION_PIECES)
                if s - 1 in ROPED and q < 2:
                    for t in (0, 1) if q == 0 else (2, 3, 4):
                        rotate(s - 1, t)
            for slot in range(2):
                rest_piece(T, dve, slot, U + NP // 2, KT * P)

        @block.gpsimd
        def _(pool):
            for stored, src, wait, of_prompt, of_sample in (
                    (k_stored, rot, lambda t: (roped.h, TT + t + 1), O["k_prompt"], O["k_sample"]),
                    (v_stored, M.va, lambda t: (staged.h, TT * V_A + t + 1), O["v_prompt"], O["v_sample"])):
                for t in range(TT):
                    pool.wait_ge(*wait(t))
                    if t < PT:
                        pool.dma_start(of_prompt[t * P:(t + 1) * P, :], src[:, t]).then_inc(stored.h, 16)
                    else:
                        pool.dma_start(of_sample, src[NS:P, t]).then_inc(stored.h, 16)
            pool.wait_ge(k_stored.h, TT * 16)
            pool.wait_ge(v_stored.h, TT * 16)
    T.pieces += NP // 2



def phase_attend_prompt(T, M, causal_in):
    nc = T.nc
    N = PT * HEADS
    scored, maxed, expd, turned, moved, valued, normed, oturned, rounded, rested, loaded, shifted = (
        Count(T.ctx, nc, "pa_" + n) for n in (
            "scored", "maxed", "expd", "turned", "moved", "valued", "normed", "oturned", "rounded", "rested",
            "loaded", "shifted"))
    with ExitStack() as ctx:
        def sb(name, shape, dt=F32):
            return ctx.enter_context(nc.sbuf_tensor(name, shape, dt))

        prob, prob_t = sb("prob", [P, 2, SEQ]), sb("prob_t", [P, 2, SEQ])
        out = sb("attn_out", [P, 2, MIX])
        causal = sb("causal", [P, P])
        top, shift, total, inv = (sb(n, [P, N]) for n in ("top", "shift", "total", "inv"))
        block = ctx.enter_context(nc.Block())
        jobs = [(i, h) for i in range(PT) for h in range(HEADS)]
        half = [slice(0, HD), slice(HD, P)]

        @block.sync
        def _(sp):
            sp.dma_start(causal[:, :], causal_in).then_inc(loaded.h, 16)

        @block.tensor
        def _(pe):
            def score(n):
                i, h = jobs[n]
                if n >= 2:
                    pe.wait_ge(expd.h, n - 1)
                rows = half[h % 2]
                pe.matmul(T.ps[:, n % 2, 0:(i + 1) * P], M.qaT[rows, h // 2, i * P:(i + 1) * P],
                          M.kaT[rows, h // 2, 0:(i + 1) * P], start=True, stop=True).then_inc(scored.h, 1)

            def turn(n):
                i, h = jobs[n]
                pe.wait_ge(expd.h, n + 1)
                if n >= 2:
                    pe.wait_ge(moved.h, n - 1)
                for j in range(i + 1):
                    mm = pe.transpose(T.ps[:, 2 + n % 2, j * P:(j + 1) * P], prob[:, n % 2, j * P:(j + 1) * P],
                                      T.ident[:, :])
                mm.then_inc(turned.h, 1)

            def value(n):
                i, h = jobs[n]
                pe.wait_ge(moved.h, n + 1)
                if h == 0 and i >= 2:
                    pe.wait_ge(normed.h, i - 1)
                for j in range(i + 1):
                    mm = pe.matmul(T.ps[:, 4 + i % 2, h * HD:(h + 1) * HD], prob_t[:, n % 2, j * P:(j + 1) * P],
                                   M.va[:, j, h * HD:(h + 1) * HD], start=(h == 0 and j == 0),
                                   stop=(h == HEADS - 1 and j == i), skip_group_check=True)
                mm.then_inc(valued.h, 1)

            def turn_out(i):
                pe.wait_ge(normed.h, i + 1)
                if i >= 2:
                    pe.wait_ge(rested.h, i - 1)
                for p in range(PAIRS):
                    mm = pe.transpose(T.ps[:, 6 + i % 2, p * P:(p + 1) * P], out[:, i % 2, p * P:(p + 1) * P],
                                      T.ident[:, :])
                mm.then_inc(oturned.h, 1)

            for n in range(N + 2):
                if n < N:
                    score(n)
                if 1 <= n <= N:
                    turn(n - 1)
                if n >= 2:
                    value(n - 2)
                if n >= HEADS + 4 and (n - 4) % HEADS == 0:
                    turn_out((n - 4) // HEADS - 1)
            turn_out(PT - 1)

        @block.vector
        def _(dve):
            dve.wait_ge(loaded.h, 16)

            def rest(i):
                dve.wait_ge(rounded.h, i + 1)
                cols = slice(i * P, (i + 1) * P)
                dve.tensor_tensor(T.x_lo[:, 0:PAIRS, cols],
                                  T.ps[:, 6 + i % 2, :].rearrange("p (a t) -> p a t", a=PAIRS),
                                  T.x_hi[:, 0:PAIRS, cols].bitcast(F32), ALU.subtract).then_inc(rested.h, 1)

            def norm(i):
                dve.wait_ge(valued.h, HEADS * (i + 1))
                cols = slice(HEADS * i, HEADS * (i + 1))
                T.dve_chain(dve, dve.reciprocal(inv[:, cols], total[:, cols]))
                if i >= 2:
                    dve.wait_ge(oturned.h, i - 1)
                dve.tensor_tensor(out[:, i % 2].rearrange("p (h d) -> p h d", h=HEADS),
                                  T.ps[:, 4 + i % 2, :].rearrange("p (h d) -> p h d", h=HEADS),
                                  inv[:, cols].unsqueeze(2).to_broadcast([P, HEADS, HD]), ALU.mult)\
                   .then_inc(normed.h, 1)

            for n in range(N):
                i, h = jobs[n]
                dve.wait_ge(scored.h, n + 1)
                diag = T.ps[:, n % 2, i * P:(i + 1) * P]
                T.dve_chain(dve, dve.tensor_tensor(diag, diag, causal[:, :], ALU.add))
                T.dve_chain(dve, dve.reduce_max(top[:, n:n + 1], T.ps[:, n % 2, 0:(i + 1) * P], AX_X))
                dve.tensor_scalar(shift[:, n:n + 1], top[:, n:n + 1], -HD ** -0.5, None, ALU.mult)\
                   .then_inc(maxed.h, 1)
                if i and h == 2:
                    norm(i - 1)
                if i and h == 5:
                    rest(i - 1)
            norm(PT - 1)
            rest(PT - 1)

        @block.scalar
        def _(act):
            def move(n):
                i, h = jobs[n]
                act.wait_ge(turned.h, n + 1)
                if n >= 2:
                    act.wait_ge(valued.h, n - 1)
                act.activation(prob_t[:, n % 2, 0:(i + 1) * P], T.ps[:, 2 + n % 2, 0:(i + 1) * P], ACT.Copy)\
                   .then_inc(moved.h, 1)

            def round_out(i):
                act.wait_ge(oturned.h, i + 1)
                act.activation(T.x_hi[:, 0:PAIRS, i * P:(i + 1) * P],
                               T.ps[:, 6 + i % 2, :].rearrange("p (a t) -> p a t", a=PAIRS), ACT.Copy)\
                   .then_inc(rounded.h, 1)

            for n in range(N):
                i, h = jobs[n]
                act.wait_ge(maxed.h, n + 1)
                if n >= 2:
                    act.wait_ge(turned.h, n - 1)
                act.activation(prob[:, n % 2, 0:(i + 1) * P], T.ps[:, n % 2, 0:(i + 1) * P], ACT.Exp,
                               bias=shift[:, n:n + 1], scale=HD ** -0.5, accum_out=total[:, n:n + 1])\
                   .then_inc(expd.h, 1)
                if n >= 1:
                    move(n - 1)
                if i and h == 5:
                    round_out(i - 1)
            move(N - 1)
            round_out(PT - 1)



class GroupNorm:

    def __init__(self, T, M, ctx, name):
        def sb(part, shape):
            return ctx.enter_context(T.nc.sbuf_tensor(name + part, shape, F32))

        self.T, self.M = T, M
        self.ready, self.rooted, self.gated, self.turned, self.rounded, self.rested = (
            Count(T.ctx, T.nc, name + n) for n in ("ready", "rooted", "gated", "turned", "rounded", "rested"))
        self.centred, self.squares, self.gate = (sb(n, [P, MIX]) for n in ("centred", "squares", "gate"))
        self.mean, self.var = sb("mean", [P, HEADS]), sb("var", [P, HEADS])

    def vector(self, dve, n, ps, t):
        T, M = self.T, self.M
        r = slice(0 if t < PT else NS, P)
        rows = P - r.start
        wide = [rows, HEADS, HD]

        def heads(ap):
            return ap.rearrange("p (h d) -> p h d", h=HEADS)

        def each(ap):
            return ap.unsqueeze(2).to_broadcast(wide)

        mean, var, centred, squares = self.mean[r, :], self.var[r, :], self.centred[r, :], self.squares[r, :]
        T.dve_chain(dve, dve.tensor_reduce(mean, heads(ps[r, :]), AX_X, ALU.add))
        T.dve_chain(dve, dve.tensor_scalar(mean, mean, -1.0 / HD, None, ALU.mult))
        T.dve_chain(dve, dve.tensor_tensor(heads(centred), heads(ps[r, :]), each(mean), ALU.add))
        T.dve_chain(dve, dve.tensor_tensor(squares, centred, centred, ALU.mult))
        T.dve_chain(dve, dve.tensor_reduce(var, heads(squares), AX_X, ALU.add))
        dve.tensor_scalar(var, var, 1.0 / HD, GN_EPS, ALU.mult, ALU.add).then_inc(self.ready.h, 1)
        dve.wait_ge(self.rooted.h, n + 1)
        T.dve_chain(dve, dve.reciprocal(var, var))
        T.dve_chain(dve, dve.tensor_tensor(heads(centred), heads(centred), each(var), ALU.mult))
        if n >= 1:
            dve.wait_ge(self.turned.h, n)
        dve.tensor_tensor(self.gate[r, :], centred, M.gb[r, t], ALU.mult).then_inc(self.gated.h, 1)

    def rest(self, dve, n, t):
        T = self.T
        m = P if t < PT else NS
        dve.wait_ge(self.rounded.h, n + 1)
        cols = slice(t * P, t * P + m)
        dve.tensor_tensor(T.x_lo[:, PAIRS:KT, cols],
                          T.ps[:, 6 + n % 2, :].rearrange("p (a t) -> p a t", a=PAIRS)[:, :, 0:m],
                          T.x_hi[:, PAIRS:KT, cols].bitcast(F32), ALU.subtract).then_inc(self.rested.h, 1)

    def scalar(self, act, n, t):
        T = self.T
        r = slice(0 if t < PT else NS, P)
        act.wait_ge(self.ready.h, n + 1)
        act.activation(self.var[r, :], self.var[r, :], ACT.Sqrt).then_inc(self.rooted.h, 1)

    def round(self, act, n, t):
        T = self.T
        m = P if t < PT else NS
        act.wait_ge(self.turned.h, n + 1)
        act.activation(T.x_hi[:, PAIRS:KT, t * P:t * P + m],
                       T.ps[:, 6 + n % 2, :].rearrange("p (a t) -> p a t", a=PAIRS)[:, :, 0:m], ACT.Copy)\
           .then_inc(self.rounded.h, 1)

    def tensor(self, pe, n, t):
        T = self.T
        lo = 0 if t < PT else NS
        pe.wait_ge(self.gated.h, n + 1)
        if n >= 2:
            pe.wait_ge(self.rested.h, n - 1)
        for p in range(PAIRS):
            mm = pe.transpose(T.ps[:, 6 + n % 2, p * P:p * P + P - lo], self.gate[lo:P, p * P:(p + 1) * P],
                              T.ident[lo:P, lo:P])
        mm.then_inc(self.turned.h, 1)


def phase_retain_prompt(T, M, keep_in, power_in, state_out):
    nc = T.nc
    inner, masked, kept, copied, outed, loaded, stored = (
        Count(T.ctx, nc, "rp_" + n) for n in ("inner", "masked", "kept", "copied", "outed", "loaded", "stored"))
    with ExitStack() as ctx:
        def sb(name, shape, dt=F32):
            return ctx.enter_context(nc.sbuf_tensor(name, shape, dt))

        keep = sb("keep", [P, P])
        power = sb("power", [P, PAIRS])
        weight = sb("weight", [P, 2, HEADS // 2, P])
        state = sb("state", [P, PAIRS, P])
        final = sb("final", [P, PAIRS, HD])
        gn = GroupNorm(T, M, ctx, "rp_gn_")
        block = ctx.enter_context(nc.Block())
        half = [slice(0, HD), slice(HD, P)]
        sums = T.ps[:, 4, :].rearrange("p (a e) -> p a e", a=PAIRS)

        @block.sync
        def _(sp):
            sp.dma_start(keep[:, :], keep_in).then_inc(loaded.h, 16)
            sp.dma_start(power[:, :], power_in).then_inc(loaded.h, 16)
            sp.wait_ge(copied.h, PT + 1)
            for s in range(2):
                sp.dma_start(state_out.rearrange("(a s) d e -> s d a e", s=2)[s], final[half[s], :, :])\
                  .then_inc(stored.h, 16)
            sp.wait_ge(stored.h, 32)

        @block.tensor
        def _(pe):
            for i in range(PT):
                cols = slice(i * P, (i + 1) * P)
                for g in range(2):
                    if i:
                        pe.wait_ge(masked.h, 2 * i + g - 1)
                    for j in range(HEADS // 2):
                        h = 2 * j + g
                        rows = half[g]
                        mm = pe.matmul(T.ps[:, g, j * P:(j + 1) * P], M.kbT[rows, h // 2, cols],
                                       M.qbT[rows, h // 2, cols], start=True, stop=True)
                    mm.then_inc(inner.h, 1)
                if i >= 2:
                    pe.wait_ge(gn.gated.h, i - 1)
                out = T.ps[:, 2 + i % 2, :]
                if i:
                    pe.wait_ge(copied.h, i + 1)
                    for p in range(PAIRS):
                        pe.matmul(out[:, p * P:(p + 1) * P], M.qbT[:, p, cols], state[:, p, :],
                                  start=(p == 0), stop=False, skip_group_check=True)
                pe.wait_ge(masked.h, 2 * i + 2)
                for h in range(HEADS):
                    mm = pe.matmul(out[:, h * HD:(h + 1) * HD], weight[:, h % 2, h // 2, :],
                                   M.vb[:, i, h * HD:(h + 1) * HD], start=(i == 0 and h == 0),
                                   stop=(h == HEADS - 1), skip_group_check=True)
                mm.then_inc(outed.h, 1)
                for p in range(PAIRS):
                    mm = pe.matmul(sums[:, p, :], M.kb[:, i, p * P:(p + 1) * P], M.vb[:, i, p * P:(p + 1) * P],
                                   start=(i == 0 and p == 0), stop=(i == PT - 1 and p == PAIRS - 1),
                                   skip_group_check=True)
                mm.then_inc(kept.h, 1)
                if i:
                    gn.tensor(pe, i - 1, i - 1)
            gn.tensor(pe, PT - 1, PT - 1)

        @block.vector
        def _(dve):
            dve.memset(state[:, :, :], 0.0).then_inc(copied.h, 1)
            dve.wait_ge(copied.h, 1)
            dve.wait_ge(loaded.h, 32)
            for i in range(PT):
                for g in range(2):
                    dve.wait_ge(inner.h, 2 * i + g + 1)
                    if i:
                        dve.wait_ge(outed.h, i)
                    dve.tensor_tensor(weight[:, g], T.ps[:, g, :].rearrange("p (h t) -> p h t", h=HEADS // 2),
                                      keep[:, :].unsqueeze(1).to_broadcast([P, HEADS // 2, P]), ALU.mult)\
                       .then_inc(masked.h, 1)
                dve.wait_ge(kept.h, i + 1)
                for s in range(2):
                    if i < PT - 1:
                        last = dve.tensor_copy(state[half[s], :, half[s]], sums[half[s], :, half[s]])
                    else:
                        last = dve.tensor_tensor(final[half[s], :, :], sums[half[s], :, half[s]],
                                                 power[half[s], :].unsqueeze(2).to_broadcast([HD, PAIRS, HD]),
                                                 ALU.mult)
                last.then_inc(copied.h, 1)
                gn.vector(dve, i, T.ps[:, 2 + i % 2, :], i)
                if i:
                    gn.rest(dve, i - 1, i - 1)
            gn.rest(dve, PT - 1, PT - 1)

        @block.scalar
        def _(act):
            for i in range(PT):
                gn.scalar(act, i, i)
                if i:
                    gn.round(act, i - 1, i - 1)
            gn.round(act, PT - 1, PT - 1)


def phase_retain_samples(T, M, state_in, keep_in, select_in, power_in, state_out):
    nc = T.nc
    B = DEC_BATCH
    names = ("loaded", "zeroed", "spread", "inner", "masked", "outed", "picked", "updated", "added", "stored")
    loaded, zeroed, spread, inner, masked, outed, picked, updated, added, stored = (
        Count(T.ctx, nc, "rs_" + n) for n in names)
    with ExitStack() as ctx:
        def sb(name, shape, dt=F32):
            return ctx.enter_context(nc.sbuf_tensor(name, shape, dt))

        keep = sb("keep_s", [P, NS])
        select = sb("select", [P, B])
        power = sb("power_s", [P, PAIRS])
        state = sb("state_s", [P, B * PAIRS, P])
        q_of = sb("q_of", [P, PAIRS, B, NS])
        weight = sb("weight_s", [P, 2, PAIRS, NS])
        v_of = sb("v_of", [P, 2, MIX])
        gn = GroupNorm(T, M, ctx, "rs_gn_")
        block = ctx.enter_context(nc.Block())
        half = [slice(0, HD), slice(HD, P)]
        tok = slice(NS, P)

        @block.sync
        def _(sp):
            sp.dma_start(keep[tok, :], keep_in).then_inc(loaded.h, 16)
            sp.dma_start(select[tok, :], select_in).then_inc(loaded.h, 16)
            sp.dma_start(power[:, :], power_in).then_inc(loaded.h, 16)
            sp.wait_ge(zeroed.h, 1)
            for s in range(2):
                sp.dma_start(state[half[s], :, half[s]],
                             state_in.rearrange("b (a s) d e -> s d (b a) e", s=2)[s]).then_inc(loaded.h, 16)
            sp.wait_ge(added.h, B)
            for s in range(2):
                sp.dma_start(state_out.rearrange("b (a s) d e -> s d (b a) e", s=2)[s],
                             state[half[s], :, half[s]]).then_inc(stored.h, 16)
            sp.wait_ge(stored.h, 32)

        @block.tensor
        def _(pe):
            for h in range(HEADS):
                rows = half[h % 2]
                mm = pe.matmul(T.ps[tok, (0, 4)[h % 2], h // 2 * NS:(h // 2 + 1) * NS], M.kbT[rows, h // 2, SEQ:NT],
                               M.qbT[rows, h // 2, SEQ:NT], start=True, stop=True)
            mm.then_inc(inner.h, 1)
            pe.wait_ge(spread.h, B)
            pe.wait_ge(loaded.h, 5 * 16)
            for p in range(PAIRS):
                for b in range(B):
                    pe.matmul(T.ps[tok, 1, p * P:(p + 1) * P], q_of[:, p, b, :], state[:, PAIRS * b + p, :],
                              start=(p == 0 and b == 0), stop=False, skip_group_check=True)
            pe.wait_ge(masked.h, 1)
            for h in range(HEADS):
                mm = pe.matmul(T.ps[tok, 1, h * HD:(h + 1) * HD], weight[tok, h % 2, h // 2, :],
                               M.vb[tok, PT, h * HD:(h + 1) * HD], start=False, stop=(h == HEADS - 1),
                               skip_group_check=True)
            mm.then_inc(outed.h, 1)
            for b in range(B):
                pe.wait_ge(picked.h, b + 1)
                if b >= 2:
                    pe.wait_ge(added.h, b - 1)
                for p in range(PAIRS):
                    mm = pe.matmul(T.ps[:, 2 + b % 2, p * P:(p + 1) * P], M.kb[tok, PT, p * P:(p + 1) * P],
                                   v_of[tok, b % 2, p * P:(p + 1) * P], start=True, stop=True)
                mm.then_inc(updated.h, 1)
            gn.tensor(pe, 0, PT)

        @block.vector
        def _(dve):
            dve.memset(state[:, :, :], 0.0).then_inc(zeroed.h, 1)
            dve.memset(q_of[:, :, :, :], 0.0).then_inc(zeroed.h, 1)
            dve.wait_ge(zeroed.h, 2)
            for b in range(B):
                cols = slice(b * DEC_SEQ, (b + 1) * DEC_SEQ)
                dve.tensor_copy(q_of[:, :, b, cols], M.qbT[:, :, SEQ + cols.start:SEQ + cols.stop])\
                   .then_inc(spread.h, 1)
            dve.wait_ge(loaded.h, 5 * 16)
            dve.wait_ge(inner.h, 1)
            for s in range(2):
                last = dve.tensor_tensor(weight[tok, s], T.ps[tok, (0, 4)[s], 0:PAIRS * NS]
                                         .rearrange("p (a t) -> p a t", a=PAIRS),
                                         keep[tok, :].unsqueeze(1).to_broadcast([NS, PAIRS, NS]), ALU.mult)
            last.then_inc(masked.h, 1)

            def pick(b):
                if b >= 2:
                    dve.wait_ge(updated.h, b - 1)
                dve.tensor_scalar(v_of[tok, b % 2, :], M.vb[tok, PT, :], select[tok, b:b + 1], None, ALU.mult)\
                   .then_inc(picked.h, 1)

            pick(0)
            for b in range(B):
                if b + 1 < B:
                    pick(b + 1)
                dve.wait_ge(outed.h, 1)
                dve.wait_ge(updated.h, b + 1)
                ps = T.ps[:, 2 + b % 2, :].rearrange("p (a e) -> p a e", a=PAIRS)
                mine = slice(PAIRS * b, PAIRS * (b + 1))
                for s in range(2):
                    at = state[half[s], mine, half[s]]
                    T.dve_chain(dve, dve.tensor_tensor(at, at, ps[half[s], :, half[s]], ALU.add))
                    last = dve.tensor_tensor(at, at, power[half[s], :].unsqueeze(2).to_broadcast([HD, PAIRS, HD]),
                                             ALU.mult)
                last.then_inc(added.h, 1)
            gn.vector(dve, 0, T.ps[:, 1, :], PT)
            gn.rest(dve, 0, PT)

        @block.scalar
        def _(act):
            gn.scalar(act, 0, PT)
            gn.round(act, 0, PT)



BP = DEC_BATCH // 2
PAGES = PAST_LEN // PAGE
BLOCKS = PAST_LEN // 256
GP = PAGES // 2


def linker(eng, sem, base):
    made = [0]

    def link(ins):
        made[0] += 1
        ins.then_inc(sem.h, 1)
        eng.wait_ge(sem.h, base + made[0])
    return link


def phase_attend_samples(T, M, k_pool, v_pool, table, past_mask, block_no, n_pool):
    nc = T.nc
    k_pages = k_pool.rearrange("n t h d -> n t (h d)")
    v_pages = v_pool.rearrange("n t h d -> n t (h d)")
    SOFT, NORM = 12, 2

    def count(name):
        return Count(T.ctx, nc, "sa_" + name)

    k_loaded = [count(f"k_loaded{i}") for i in range(2)]
    k_turned, k_moved = ([count(n + str(i)) for i in range(2)] for n in ("k_turned", "k_moved"))
    v_loaded, v_used = ([count(n + str(i)) for i in range(4)] for n in ("v_loaded", "v_used"))
    table_loaded, loaded, zeroed, q_ready, scored, shifted, expd, normed = map(
        count, ("table_loaded", "loaded", "zeroed", "q_ready", "scored", "shifted", "expd", "normed"))
    p_turned, p_moved0, p_moved1, valued, rounded, rested, soft_link, norm_link = map(
        count, ("p_turned", "p_moved0", "p_moved1", "valued", "rounded", "rested", "soft_link", "norm_link"))
    with ExitStack() as ctx:
        def sb(name, shape, dt=F32):
            return ctx.enter_context(nc.sbuf_tensor(name, shape, dt))

        k_ring = sb("k_ring", [P, PAGES, MIX])
        v_ring = sb("v_ring", [P, 2 * PAGES, MIX])
        keys = sb("keys", [P, PAIRS, PAST_LEN])
        q_of = sb("q_of_s", [P, 2, PAIRS * (HD + 16)])
        prob = sb("prob_s", [P, PAST_LEN + NS])
        prob_t = sb("prob_ts", [P, PAGES + 1, P])
        mask, new = sb("mask_s", [P, BP, NS]), sb("new_s", [P, NS])
        pages = sb("pages", [1, DEC_BATCH * PAGES], I32)
        number = sb("number", [P, BLOCKS])
        gate, worst, same, last_same = sb("gate_s", [P, BLOCKS]), sb("worst", [P, 1]), sb("same", [P, BLOCKS]), sb("last_same", [P, 1])
        out_of, block_top, top = sb("out_of", [P, BLOCKS]), sb("block_top", [P, BLOCKS + 1]), sb("top_s", [P, 1])
        shift, totals, total = sb("shift_s", [P, BLOCKS + 1]), sb("totals_s", [P, BLOCKS + 1]), sb("total_s", [P, 1])
        credit = sb("credit_s", [P, 7])
        block = ctx.enter_context(nc.Block())
        half = [slice(0, HD), slice(HD, P)]
        past = T.ps[:, 0:2, :].rearrange("p b (c t) -> p (b c) t", c=2)
        tok = slice(NS, P)

        def load(q, pool, ring, at0, arrived, bp, b2, g, free, value):
            srcs = []
            for i in range(GP):
                at = bp * (2 * PAGES) + (b2 * PAGES + g * GP + i)
                page = q.value_load(pages[0:1, bass.ds(at, 1)], min_val=0, max_val=n_pool - 1)
                srcs.append(pool[bass.ds(page, 1)].rearrange("a t c -> (a t) c"))
            if free is not None:
                q.wait_ge(free.h, value)
            for i in range(GP):
                q.dma_start(ring[:, at0 + i], srcs[i]).then_inc(arrived.h, 16)

        @block.sync
        def _(sp):
            def load_k(bp, b2, free_value):
                for g in range(2):
                    load(sp, k_pages, k_ring, GP * g, k_loaded[g], bp, b2, g, k_turned[1 - b2],
                         free_value + GP * (g + 1))

            sp.dma_start(pages[:, :], table.rearrange("b n -> (b n)").unsqueeze(0)).then_inc(table_loaded.h, 16)
            sp.dma_start(number[:, :], block_no).then_inc(loaded.h, 16)
            sp.dma_start(mask[:, :, :], past_mask).then_inc(loaded.h, 16)
            sp.wait_ge(table_loaded.h, 16)
            for g in range(2):
                load(sp, k_pages, k_ring, GP * g, k_loaded[g], 0, 0, g, None, 0)
            load_k(0, 1, 0)
            with sp.Fori(0, BP - 1) as bp:
                load_k(bp + 1, 0, bp * PAGES)
                load_k(bp + 1, 1, bp * PAGES + PAGES)

        @block.gpsimd
        def _(pool):
            pool.wait_ge(table_loaded.h, 16)
            with pool.Fori(0, BP) as bp:
                for b2 in range(2):
                    for g in range(2):
                        part = 2 * b2 + g
                        load(pool, v_pages, v_ring, GP * part, v_loaded[part], bp, b2, g, v_used[part], bp + 1)

        @block.tensor
        def _(pe):
            def turn_keys(bp, b2):
                for j in range(PAGES):
                    if j % GP == 0:
                        pe.wait_ge(k_loaded[j // GP].h, bp * 128 + (64 * b2 + 64))
                    if j >= 2:
                        pe.wait_ge(k_moved[b2].h, bp * PAGES + (j - 1))
                    for p in range(PAIRS):
                        mm = pe.transpose(T.ps[:, 3 + j % 2, p * P:(p + 1) * P], k_ring[:, j, p * P:(p + 1) * P],
                                          T.ident[:, :])
                    mm.then_inc(k_turned[b2].h, 1)

            def score(bp, b2, first=False):
                pe.wait_ge(k_moved[b2].h, bp * PAGES + PAGES)
                pe.wait_ge(q_ready.h, bp + 1)
                if b2 == 0 and not first:
                    pe.wait_ge(expd.h, bp)
                rows = half[b2]
                for n in range(3):
                    for p in range(PAIRS):
                        src = keys[:, p, n * 512:(n + 1) * 512] if n < 2 else M.kaT[:, p, SEQ:NT]
                        mm = pe.matmul(T.ps[rows, n, 0:src.shape[1]], q_of[:, b2, p * HD:(p + 1) * HD], src,
                                       start=(p == 0), stop=(p == PAIRS - 1))
                mm.then_inc(scored.h, 1)

            def values(bp):
                pe.wait_ge(rested.h, bp + 1)
                pe.wait_ge(normed.h, bp + 1)
                for g in range(2):
                    for i in range(GP):
                        j = GP * g + i
                        mm = pe.transpose(T.ps[:, 5 + g, i * P:(i + 1) * P], prob[:, j * P:(j + 1) * P], T.ident[:, :])
                    mm.then_inc(p_turned.h, 1)
                pe.transpose(T.ps[0:NS, 7, P:2 * P], prob[:, PAST_LEN:PAST_LEN + NS], T.ident[:, :])\
                  .then_inc(p_turned.h, 1)
                pe.wait_ge(p_moved0.h, bp * 2 + 2)
                pe.wait_ge(p_moved1.h, bp + 1)
                for b2 in range(2):
                    for j in range(PAGES):
                        part = 2 * b2 + j // GP
                        if j % GP == 0:
                            pe.wait_ge(v_loaded[part].h, bp * 64 + 64)
                        for p in range(PAIRS):
                            col = (b2 * PAIRS + p) * 16
                            mm = pe.matmul(T.ps[:, 7, col:col + 16], v_ring[:, PAGES * b2 + j, p * P:(p + 1) * P],
                                           prob_t[:, j, b2 * HD + p * 16:b2 * HD + p * 16 + 16],
                                           start=(b2 == 0 and j == 0 and p == 0), stop=False, skip_group_check=True)
                        if j % GP == GP - 1:
                            mm.then_inc(v_used[part].h, 1)
                for b2 in range(2):
                    for p in range(PAIRS):
                        col = (b2 * PAIRS + p) * 16
                        mm = pe.matmul(T.ps[:, 7, col:col + 16], M.va[tok, PT, p * P:(p + 1) * P],
                                       prob_t[tok, PAGES, b2 * HD + p * 16:b2 * HD + p * 16 + 16],
                                       start=False, stop=(b2 == 1 and p == PAIRS - 1), skip_group_check=True)
                mm.then_inc(valued.h, 1)

            turn_keys(0, 0)
            score(0, 0, True)
            turn_keys(0, 1)
            score(0, 1)
            with pe.Fori(0, BP - 1) as bp:
                turn_keys(bp + 1, 0)
                score(bp + 1, 0)
                values(bp)
                turn_keys(bp + 1, 1)
                score(bp + 1, 1)
            values(BP - 1)

        def move_keys(eng, copy, bp, b2, scores, first=False):
            if not first:
                eng.wait_ge(scored.h, scores)
            for j in range(PAGES):
                eng.wait_ge(k_turned[b2].h, bp * PAGES + (j + 1))
                copy(keys[:, :, j * P:(j + 1) * P], T.ps[:, 3 + j % 2, :].rearrange("p (a t) -> p a t", a=PAIRS))\
                    .then_inc(k_moved[b2].h, 1)

        def outputs_at(s, bp, buf):
            at = buf[half[s], 0:PAIRS, bass.ds(bp * (2 * DEC_SEQ) + SEQ, 2 * DEC_SEQ)]
            return at.rearrange("p a (b q) -> p a b q", b=2)

        def outputs_ps(s):
            return T.ps[half[s], 7, 0:P].rearrange("p (b a c) -> p a b c", b=2, c=16)[:, :, :, s * 8:(s + 1) * 8]

        @block.vector
        def _(dve):
            def spread_q(bp):
                for s in range(2):
                    dst = q_of[half[s], :, :].rearrange("p b (a c) -> p b a c", a=PAIRS)[:, :, :, s * 8:(s + 1) * 8]
                    src = M.qaT[half[s], :, bass.ds(bp * (2 * DEC_SEQ) + SEQ, 2 * DEC_SEQ)]\
                        .rearrange("p a (b q) -> p b a q", b=2)
                    for b2 in range(2):
                        last = dve.tensor_copy(dst[:, b2], src[:, b2])
                last.then_inc(q_ready.h, 1)

            def soft(bp):
                dve.wait_ge(scored.h, bp * 2 + 2)
                link = linker(dve, soft_link, bp * SOFT)
                dve.tensor_reduce(gate[:, :], past, AX_X, ALU.add)
                dve.tensor_reduce(block_top[:, 0:BLOCKS], past, AX_X, ALU.max)
                link(dve.tensor_tensor(new[:, :], T.ps[:, 2, 0:NS],
                                       mask[:, bass.ds(bp, 1), :].rearrange("p a t -> p (a t)"), ALU.add))
                link(dve.reduce_max(block_top[:, BLOCKS:BLOCKS + 1], new[:, :], AX_X))
                link(dve.tensor_reduce(worst[:, :], gate[:, :], AX_X, ALU.min))
                link(dve.tensor_scalar(same[:, :], gate[:, :], worst[:, 0:1], None, ALU.is_equal))
                link(dve.tensor_tensor(same[:, :], same[:, :], number[:, :], ALU.mult))
                link(dve.reduce_max(last_same[:, :], same[:, :], AX_X))
                link(dve.tensor_scalar(out_of[:, :], number[:, :], last_same[:, 0:1], NEG, ALU.is_equal, ALU.mult))
                link(dve.tensor_tensor(block_top[:, 0:BLOCKS], block_top[:, 0:BLOCKS], out_of[:, :], ALU.add))
                link(dve.reduce_max(top[:, :], block_top[:, :], AX_X))
                link(dve.tensor_scalar(shift[:, BLOCKS:BLOCKS + 1], top[:, :], -HD ** -0.5, None, ALU.mult))
                link(dve.tensor_scalar(shift[:, 0:BLOCKS], out_of[:, :], shift[:, BLOCKS:BLOCKS + 1], None, ALU.add))
                link(dve.memset(credit[:, 6:7], 0.0))
                dve.memset(credit[:, 5:6], 0.0).then_inc(shifted.h, 1)

            def norm(bp):
                dve.wait_ge(expd.h, bp + 1)
                link = linker(dve, norm_link, bp * NORM)
                link(dve.tensor_reduce(total[:, :], totals[:, :], AX_X, ALU.add))
                link(dve.reciprocal(total[:, :], total[:, :]))
                dve.tensor_scalar(prob[:, :], prob[:, :], total[:, 0:1], None, ALU.mult).then_inc(normed.h, 1)

            def move_prob(bp):
                dve.wait_ge(p_turned.h, bp * 3 + 2)
                dve.tensor_copy(prob_t[:, GP:PAGES, :], T.ps[:, 6, :].rearrange("p (j t) -> p j t", j=GP))\
                   .then_inc(p_moved1.h, 1)

            def rest(bp):
                dve.wait_ge(rounded.h, bp + 1)
                for s in range(2):
                    hi, lo, ps = outputs_at(s, bp, T.x_hi), outputs_at(s, bp, T.x_lo), outputs_ps(s)
                    last = dve.tensor_tensor(lo, ps, hi.bitcast(F32), ALU.subtract)
                last.then_inc(rested.h, 1)

            for i, c in enumerate((*v_used, rested)):
                dve.memset(credit[:, i:i + 1], 0.0).then_inc(c.h, 1)
            dve.memset(q_of[:, :, :], 0.0).then_inc(zeroed.h, 1)
            dve.wait_ge(zeroed.h, 1)
            spread_q(0)
            move_keys(dve, dve.tensor_copy, 0, 1, 1)
            dve.wait_ge(loaded.h, 32)
            with dve.Fori(0, BP - 1) as bp:
                soft(bp)
                spread_q(bp + 1)
                norm(bp)
                move_prob(bp)
                move_keys(dve, dve.tensor_copy, bp + 1, 1, bp * 2 + 3)
                rest(bp)
            soft(BP - 1)
            norm(BP - 1)
            move_prob(BP - 1)
            rest(BP - 1)

        @block.scalar
        def _(act):
            def copy(out, src):
                return act.activation(out, src, ACT.Copy)

            def exps(bp):
                act.wait_ge(shifted.h, bp + 1)
                for c in range(BLOCKS):
                    act.activation(prob[:, c * 256:(c + 1) * 256], past[:, c], ACT.Exp, bias=shift[:, c:c + 1],
                                   scale=HD ** -0.5, accum_out=totals[:, c:c + 1])
                act.activation(prob[:, PAST_LEN:PAST_LEN + NS], new[:, :], ACT.Exp, bias=shift[:, BLOCKS:BLOCKS + 1],
                               scale=HD ** -0.5, accum_out=totals[:, BLOCKS:BLOCKS + 1]).then_inc(expd.h, 1)

            def finish(bp):
                act.wait_ge(p_turned.h, bp * 3 + 1)
                act.activation(prob_t[:, 0:GP, :], T.ps[:, 5, :].rearrange("p (j t) -> p j t", j=GP), ACT.Copy)\
                   .then_inc(p_moved0.h, 1)
                act.wait_ge(p_turned.h, bp * 3 + 3)
                act.activation(prob_t[tok, PAGES, :], T.ps[0:NS, 7, P:2 * P], ACT.Copy).then_inc(p_moved0.h, 1)
                act.wait_ge(valued.h, bp + 1)
                for s in range(2):
                    last = act.activation(outputs_at(s, bp, T.x_hi), outputs_ps(s), ACT.Copy)
                last.then_inc(rounded.h, 1)

            move_keys(act, copy, 0, 0, 0, True)
            with act.Fori(0, BP - 1) as bp:
                move_keys(act, copy, bp + 1, 0, bp * 2 + 2)
                exps(bp)
                finish(bp)
            exps(BP - 1)
            finish(BP - 1)



def out_piece(w, d):
    return w.rearrange("(k p) d -> p k d", p=P)[:, :, bass.ds(d * P, P)]


def phase_out(T, w_out, w_gate, row, nxt):
    nc = T.nc
    U = T.pieces
    G = KT * P
    gated = w_gate is not None
    used = KT if gated else KT // 2
    res0, silu0 = T.res_done.n, T.silu_done.n
    with ExitStack() as ctx:
        def sb(name, shape, dt=F32):
            return ctx.enter_context(nc.sbuf_tensor(f"{name}_{row}", shape, dt))

        gate, work = sb("gate", [P, 2, NT]), sb("work", [P, 2, NT])
        acc, rstd = sb("acc", [P, NT]), sb("rstd", [P, NT])
        norm = Norm(T, row, 1.0, acc, KT + 1, gate, rstd, U + used, True)
        acc0 = T.acc_added.n
        block = ctx.enter_context(nc.Block())

        def pieces():
            for d in range(KT):
                if gated:
                    yield d, 0, d, w_out
                    yield d, 1, d, w_gate
                else:
                    yield d, d % 2, d // 2, w_out

        @block.sync
        def _(sp):
            for d, slot, u, w in list(pieces())[2:]:
                load_piece(T, sp, slot, U + u, out_piece(w, d))
            for slot in range(2):
                load_piece(T, sp, slot, U + used, nxt[slot])

        @block.tensor
        def _(pe):
            for d, slot, u, w in pieces():
                j = d % 2
                if w is w_out:
                    pe.wait_ge(T.res_done.h, res0 + d - 1)
                pe.wait_ge(T.w_split[slot].h, U + u + 2)
                for n in range(2):
                    for k in range(KT):
                        cols = slice(n * NH, (n + 1) * NH)
                        mm = product3(pe, T.ps[:, 4 * j + (0 if w is w_out else 2) + n, 0:NH],
                                      T.w_hi[:, slot, k * P:(k + 1) * P], T.w_lo[:, slot, k * P:(k + 1) * P],
                                      T.x_hi[:, k, cols], T.x_lo[:, k, cols], k == 0, k == KT - 1)
                mm.then_inc(T.w_used[slot].h, 1)
            norm.tensor(pe)

        @block.scalar
        def _(act):
            order = list(pieces())
            for d in range(KT):
                for dd, slot, u, w in order:
                    if dd == d + (1 if gated else 2):
                        round_piece(T, act, slot, U + u, G)
                if gated:
                    act.wait_ge(T.w_used[1].h, U + d + 2)
                    act.activation(halves(gate[:, d % 2]), T.ps[:, 4 * (d % 2) + 2:4 * (d % 2) + 4, 0:NH],
                                   ACT.Sigmoid).then_inc(T.silu_done.h, 1)
            norm.scalar(act)

        @block.vector
        def _(dve):
            order = list(pieces())
            dve.memset(acc[:, :], 0.0).then_inc(T.acc_added.h, 1)
            for d in range(KT):
                j = d % 2
                for dd, slot, u, w in order:
                    if dd == d + (1 if gated else 2):
                        rest_piece(T, dve, slot, U + u, G)
                y = T.ps[:, 4 * j:4 * j + 2, 0:NH]
                if gated:
                    dve.wait_ge(T.silu_done.h, silu0 + d + 1)
                    T.dve_chain(dve, dve.tensor_tensor(halves(work[:, j]), halves(gate[:, j]), y, ALU.mult))
                    y = halves(work[:, j])
                else:
                    dve.wait_ge(T.w_used[j].h, U + d // 2 + 2)
                dve.scalar_tensor_tensor(halves(T.x[:, d]), halves(T.x[:, d]), ALPHA, y, ALU.mult, ALU.add)\
                   .then_inc(T.res_done.h, 1)
                dve.wait_ge(T.res_done.h, res0 + d + 1)
                dve.wait_ge(T.acc_added.h, acc0 + d + 1)
                dve.tensor_tensor(acc[:, :], acc[:, :], T.x[:, d], ALU.add).then_inc(T.acc_added.h, 1)
            norm.vector(dve)

        @block.gpsimd
        def _(pool):
            norm.gpsimd(pool)
    T.res_done.close(KT)
    T.silu_done.close(KT if gated else 0)
    T.pieces += used
    norm.close()



GROUPS, GH, STATES = 64, 16, 64
GPAIRS = GROUPS // 2
CL = 8
PC = SEQ // CL
CHUNKS = NT // CL
GT = P // GH
LN2 = math.log(2.0)
LN2_HI = 0.693359375
TWO_PI_HI = 6.28125
TWO_PI_MID = float(np.float32(2 * math.pi - TWO_PI_HI))
TWO_PI_LO = 2 * math.pi - TWO_PI_HI - TWO_PI_MID
TO_INT = 12582912.0


class S5:
    pass


def open_s5_constants(ctx, nc):
    S = S5()

    def sb(name, shape, dt=F32):
        return ctx.enter_context(nc.sbuf_tensor("s5_" + name, shape, dt))

    S.powers = sb("powers", [P, 2, CL + 1, GPAIRS])
    S.coef = sb("coef", [P, 2, GPAIRS])
    S.size2 = sb("size2", [P, GPAIRS])
    S.skip = sb("skip", [GH, GROUPS])
    return S


def open_s5(ctx, nc, S):
    def sb(name, shape, dt=F32):
        return ctx.enter_context(nc.sbuf_tensor("s5_" + name, shape, dt))

    S.b_bar = sb("b_bar", [P, 2, GPAIRS, GH])
    S.c_t = sb("c_t", [P, 2, GPAIRS, GH])
    S.u = sb("u", [P, GROUPS, CHUNKS])
    S.start = sb("start", [P, 2, GPAIRS, CHUNKS])


class S5Constants:

    def __init__(self, T, S, I):
        self.T, self.S, self.I = T, S, I
        self.loaded = Count(T.ctx, T.nc, "s5c_loaded")

    def open(self, ctx):
        def sb(name, shape, dt=F32):
            return ctx.enter_context(self.T.nc.sbuf_tensor("s5c_" + name, shape, dt))

        self.bufs = [sb(n, [P, GPAIRS]) for n in ("l_re", "l_im", "log_dt", "dt", "work", "k", "e_re", "theta", "s", "c",
                                                  "z2", "poly", "tmp")]
        self.k_int = sb("k_int", [P, GPAIRS], I32)
        self.m1, self.m2 = sb("m1", [P, CL // 2, GPAIRS]), sb("m2", [P, CL // 2, GPAIRS])

    def gpsimd(self, pool):
        T, S, I, loaded = self.T, self.S, self.I, self.loaded
        l_re, l_im, log_dt, dt, work, k, e_re, theta, s_, c_, z2, poly, tmp = (b[:, :] for b in self.bufs)
        k_int, m1, m2 = self.k_int[:, :], self.m1, self.m2

        def op(ins):
            T.pool_chain(pool, ins)

        def ts(out, a, s1, s2, op0, op1=None):
            op(pool.tensor_scalar(out, a, s1, s2, op0, op1) if op1 is not None else
               pool.tensor_scalar(out, a, s1, None, op0))

        def tt(out, a, b, o):
            op(pool.tensor_tensor(out, a, b, o))

        def horner(out, z, coefs):
            ts(out, z, coefs[-1], None, ALU.mult)
            for c in coefs[-2::-1]:
                ts(out, out, c, None, ALU.add)
                tt(out, out, z, ALU.mult)

        def less(out, times, part):
            ts(poly, times, -part, None, ALU.mult)
            tt(out, out, poly, ALU.add)

        def exp(out, x):
            ts(work, x, -87.0, 88.0, ALU.max, ALU.min)
            ts(k, work, 1.0 / LN2, TO_INT, ALU.mult, ALU.add)
            ts(k, k, -TO_INT, None, ALU.add)
            less(work, k, LN2_HI)
            less(work, k, LN2 - LN2_HI)
            horner(poly, work, [1.0 / math.factorial(n) for n in range(1, 9)])
            ts(k, k, 127.0, 8388608.0, ALU.add, ALU.mult)
            op(pool.tensor_copy(k_int, k))
            ts(poly, poly, 1.0, None, ALU.add)
            tt(out, poly, k_int.bitcast(F32), ALU.mult)

        with T.nc.allow_non_contiguous_dma(reason="4096 state constants and 1024 skip weights by state and channel"):
            for dst, name in ((l_re, "s5_lam_re"), (l_im, "s5_lam_im")):
                for s in range(2):
                    pool.dma_start(dst[s * STATES:(s + 1) * STATES],
                                   I[name][0].rearrange("(a s) p -> s p a", s=2)[s]).then_inc(loaded.h, 16)
            for s in range(2):
                pool.dma_start(log_dt[s * STATES:(s + 1) * STATES],
                               I["s5_log_dt"][0].rearrange("(a s) -> s a", s=2)[s:s + 1]
                               .to_broadcast([STATES, GPAIRS])).then_inc(loaded.h, 16)
            pool.dma_start(S.skip[:, :], I["s5_d"][0].rearrange("(g h) -> h g", h=GH)).then_inc(loaded.h, 16)
        pool.wait_ge(loaded.h, 7 * 16)
        exp(dt, log_dt)
        tt(tmp, l_re, dt, ALU.mult)
        exp(e_re, tmp)
        tt(theta, l_im, dt, ALU.mult)
        ts(k, theta, 1.0 / (2 * math.pi), TO_INT, ALU.mult, ALU.add)
        ts(k, k, -TO_INT, None, ALU.add)
        for part in (TWO_PI_HI, TWO_PI_MID, TWO_PI_LO):
            less(theta, k, part)
        ts(theta, theta, 0.5, None, ALU.mult)
        tt(z2, theta, theta, ALU.mult)
        horner(s_, z2, [(-1) ** n / math.factorial(2 * n + 1) for n in range(1, 7)])
        ts(s_, s_, 1.0, None, ALU.add)
        tt(s_, s_, theta, ALU.mult)
        horner(c_, z2, [(-1) ** n / math.factorial(2 * n) for n in range(1, 8)])
        ts(c_, c_, 1.0, None, ALU.add)
        tt(c_, s_, c_, ALU.mult)
        tt(s_, s_, s_, ALU.mult)
        ts(s_, s_, -2.0, 1.0, ALU.mult, ALU.add)
        ts(c_, c_, 2.0, None, ALU.mult)
        lam_re, lam_im = S.powers[:, 0, 1], S.powers[:, 1, 1]
        tt(lam_re, e_re, s_, ALU.mult)
        tt(lam_im, e_re, c_, ALU.mult)
        tt(k, l_re, l_re, ALU.mult)
        tt(tmp, l_im, l_im, ALU.mult)
        tt(S.size2[:, :], k, tmp, ALU.add)
        ts(work, lam_re, -1.0, None, ALU.add)
        for r, (x, y, o) in enumerate(((work, lam_im, ALU.add), (lam_im, work, ALU.subtract))):
            tt(tmp, x, l_re, ALU.mult)
            tt(k, y, l_im, ALU.mult)
            tt(S.coef[:, r], tmp, k, o)
        op(pool.memset(S.powers[:, 0, 0], 1.0))
        op(pool.memset(S.powers[:, 1, 0], 0.0))
        n = 1
        while n < CL:
            a = [S.powers[:, r, 1:n + 1] for r in range(2)]
            by = [S.powers[:, r, n:n + 1].to_broadcast([P, n, GPAIRS]) for r in range(2)]
            for r, (x, y, o) in enumerate(((by[0], by[1], ALU.subtract), (by[1], by[0], ALU.add))):
                tt(m1[:, 0:n], a[0], x, ALU.mult)
                tt(m2[:, 0:n], a[1], y, ALU.mult)
                tt(S.powers[:, r, n + 1:2 * n + 1], m1[:, 0:n], m2[:, 0:n], o)
            n *= 2


def phase_s5_inputs(T, S, I):
    nc = T.nc
    turned, moved = Count(T.ctx, nc, "s5i_turned"), [Count(T.ctx, nc, f"s5i_moved{i}") for i in range(2)]
    b_loaded, inverted, rows_loaded, rows_turned, placed = (
        Count(T.ctx, nc, "s5i_" + n) for n in ("b_loaded", "inverted", "rows_loaded", "rows_turned", "placed"))
    with ExitStack() as ctx:
        def sb(name, shape):
            return ctx.enter_context(nc.sbuf_tensor("s5i_" + name, shape, F32))

        chunked = sb("chunked", [P, GROUPS, CL, GH])
        c_rows = sb("c_rows", [P, GT, 2, STATES])
        s_rows = sb("s_rows", [P, 2, 2, P])
        b_raw = sb("b_raw", [P, 2, GPAIRS, GH])
        m1, m2 = sb("m1", [P, GPAIRS, GH]), sb("m2", [P, GPAIRS, GH])
        block = ctx.enter_context(nc.Block())
        N1 = CL * 2
        N2 = GROUPS // 4
        N = N1 + N2

        @block.sync
        def _(sp):
            for r, part in enumerate(("re", "im")):
                sp.dma_start(b_raw[:, r], I["s5_b_" + part][0].rearrange("(a s) p h -> (s p) a h", s=2))                  .then_inc(b_loaded.h, 16)
            for r, part in enumerate(("re", "im")):
                sp.dma_start(c_rows[:, :, r, :],
                             I["s5_c_" + part][0].rearrange("(k q) h p -> (q h) k p", q=GT)).then_inc(rows_loaded.h, 16)
                sp.dma_start(s_rows[:, r, :, :],
                             I["state_s5_" + part][0].rearrange("(j b) (a s) p -> (b a) j (s p)", j=2, s=2))                  .then_inc(rows_loaded.h, 16)

        @block.gpsimd
        def _(pool):
            pool.wait_ge(inverted.h, 1)
            T.pool_chain(pool, pool.tensor_tensor(S.coef[:, :, :], S.coef[:, :, :],
                                                  S.size2[:, :].unsqueeze(1).to_broadcast([P, 2, GPAIRS]), ALU.mult))
            pool.wait_ge(b_loaded.h, 32)
            co = [S.coef[:, r].unsqueeze(2).to_broadcast([P, GPAIRS, GH]) for r in range(2)]
            for r, (x, y, o) in enumerate(((co[0], co[1], ALU.subtract), (co[1], co[0], ALU.add))):
                T.pool_chain(pool, pool.tensor_tensor(m1[:, :, :], b_raw[:, 0], x, ALU.mult))
                T.pool_chain(pool, pool.tensor_tensor(m2[:, :, :], b_raw[:, 1], y, ALU.mult))
                T.pool_chain(pool, pool.tensor_tensor(S.b_bar[:, r], m1[:, :, :], m2[:, :, :], o))

        @block.tensor
        def _(pe):
            for n in range(N):
                if n == N1:
                    for i in range(2):
                        pe.wait_ge(moved[i].h, N1 // 2)
                elif n >= 8:
                    pe.wait_ge(moved[n % 2].h, (n - 8) // 2 + 1)
                for i in range(4):
                    if n < N1:
                        t, k = n // 2, 4 * (n % 2) + i
                        mm = pe.transpose(T.ps[0:CHUNKS, n % 8, i * P:(i + 1) * P], T.x[:, k, t:NT:CL], T.ident[:, :])
                    else:
                        g = 4 * (n - N1) + i
                        mm = pe.transpose(T.ps[:, n % 8, i * CHUNKS:(i + 1) * CHUNKS],
                                          chunked[0:CHUNKS, g].rearrange("p t h -> p (t h)"),
                                          T.ident[0:CHUNKS, 0:CHUNKS])
                mm.then_inc(turned.h, 1)
            pe.wait_ge(rows_loaded.h, 4 * 16)
            for i in range(2):
                pe.wait_ge(moved[i].h, N // 2 - 2)
            for t in range(GT):
                mm = pe.transpose(T.ps[:, t // 4, (t % 4) * P:(t % 4 + 1) * P],
                                  c_rows[:, t].rearrange("p r s -> p (r s)"), T.ident[:, :])
            mm.then_inc(rows_turned.h, 1)
            for r in range(2):
                for j in range(2):
                    mm = pe.transpose(T.ps[:, 2 + r, j * P:(j + 1) * P], s_rows[:, r, j, :], T.ident[:, :])
            mm.then_inc(rows_turned.h, 1)

        def move(eng, copy, i):
            for n in range(i, N, 2):
                eng.wait_ge(turned.h, n + 1)
                if n < N1:
                    t, k = n // 2, 4 * (n % 2)
                    out = chunked[0:CHUNKS, k * GT:(k + 4) * GT, t, :]
                    src = T.ps[0:CHUNKS, n % 8, :].rearrange("p (g h) -> p g h", h=GH)
                else:
                    g = 4 * (n - N1)
                    out = S.u[:, g:g + 4, :]
                    src = T.ps[:, n % 8, 0:4 * CHUNKS].rearrange("p (g c) -> p g c", g=4)
                copy(out, src).then_inc(moved[i].h, 1)
            eng.wait_ge(rows_turned.h, 1)
            src = T.ps[:, 0:2, :].rearrange("p b (k q s h) -> p (b k) q s h", k=4, s=2, h=GH)
            for s in range(2):
                for kk in range(2):
                    copy(S.c_t[s * HD:(s + 1) * HD, i, 16 * kk:16 * kk + 16, :].rearrange("p (k q) h -> p k q h", q=4),
                         src[i * HD:(i + 1) * HD, 4 * kk:4 * kk + 4, :, s, :]).then_inc(placed.h, 1)
            eng.wait_ge(rows_turned.h, 2)
            copy(S.start[:, i, :, PC:CHUNKS],
                 T.ps[:, 2 + i, 0:2 * P].rearrange("p (b a) -> p a b", b=DEC_BATCH)).then_inc(placed.h, 1)

        @block.vector
        def _(dve):
            dve.reciprocal(S.size2[:, :], S.size2[:, :]).then_inc(inverted.h, 1)
            move(dve, dve.tensor_copy, 0)

        @block.scalar
        def _(act):
            move(act, lambda out, src: act.activation(out, src, ACT.Copy), 1)


def phase_s5_scan(T, S, c_pow, O):
    nc = T.nc
    Q = 4
    STEPS = GPAIRS // Q
    RUN = 8
    RUNS = PC // RUN
    FIX = 8
    formed, b_turned, b_moved, added, moved, jumped, states_done, turned, out_moved, stored = (
        Count(T.ctx, nc, "s5s_" + n) for n in ("formed", "b_turned", "b_moved", "added", "moved", "jumped",
                                               "states_done", "turned", "out_moved", "stored"))
    with ExitStack() as ctx:
        def sb(name, shape, dt=F32):
            return ctx.enter_context(nc.sbuf_tensor("s5s_" + name, shape, dt))

        falling = sb("falling", [P, 2, CL, GPAIRS])
        b_pow, b_rows = sb("b_pow", [P, 2, Q, CL, GH]), sb("b_rows", [P, 2, Q, P])
        m1 = sb("m1", [P, Q, CL, GH])
        jump = sb("jump", [P, 2, RUN, GPAIRS])
        ends = sb("ends", [P, 2, DEC_BATCH, GPAIRS])
        end = sb("end", [P, 2, GPAIRS])
        out_rows = sb("out_rows", [P, 5, P])
        signal = sb("signal", [P, 3])
        m2, minus = sb("m2", [P, 4, CL + 1, GH]), sb("minus", [P, 2, CL + 1, GPAIRS])
        part = sb("part", [P, 4, FIX * (RUNS - 1) * (RUN - 1)])
        block = ctx.enter_context(nc.Block())
        half = [slice(0, HD), slice(HD, P)]
        runs = S.start[:, :, :, 0:PC].rearrange("p r a (b j) -> p r a b j", j=RUN)

        @block.vector
        def _(dve):
            def op(ins):
                T.dve_chain(dve, ins)

            for t in range(CL):
                last = dve.tensor_copy(falling[:, :, t], S.powers[:, :, CL - 1 - t])
            op(last)
            for q in range(STEPS):
                a = slice(Q * q, Q * (q + 1))
                wide = [P, Q, CL, GH]
                b = [S.b_bar[:, r, a, :].unsqueeze(2).to_broadcast(wide) for r in range(2)]
                f = [falling[:, r, :, a].rearrange("p t a -> p a t").unsqueeze(3).to_broadcast(wide)
                     for r in range(2)]
                if q:
                    dve.wait_ge(b_turned.h, q)
                for r, (x, y, o) in enumerate(((f[0], f[1], ALU.subtract), (f[1], f[0], ALU.add))):
                    dve.tensor_tensor(b_pow[:, r], b[0], x, ALU.mult)
                    op(dve.tensor_tensor(m1[:, :, :, :], b[1], y, ALU.mult))
                    last = dve.tensor_tensor(b_pow[:, r], b_pow[:, r], m1[:, :, :, :], o)
                    if r == 0:
                        op(last)
                last.then_inc(formed.h, 1)
                dve.wait_ge(formed.h, q + 1)

            def advance(out, src, f, shape):
                n = int(np.prod(shape[1:]))
                names = " ".join(f"d{i}" for i in range(len(shape) - 1))
                sizes = {f"d{i}": k for i, k in enumerate(shape[1:])}
                buf = [part[:, i, 0:n].rearrange(f"p ({names}) -> p {names}", **sizes) for i in range(4)]
                dve.tensor_tensor(buf[0], src[0], f[0], ALU.mult)
                dve.tensor_tensor(buf[1], src[1], f[0], ALU.mult)
                dve.tensor_tensor(buf[2], src[1], f[1], ALU.mult)
                op(dve.tensor_tensor(buf[3], src[0], f[1], ALU.mult))
                dve.tensor_tensor(out[0], out[0], buf[0], ALU.add)
                op(dve.tensor_tensor(out[1], out[1], buf[1], ALU.add))
                dve.tensor_tensor(out[0], out[0], buf[2], ALU.subtract)
                op(dve.tensor_tensor(out[1], out[1], buf[3], ALU.add))

            op(dve.memset(S.start[:, :, :, 0:1], 0.0))
            dve.wait_ge(moved.h, STEPS)
            dve.wait_ge(jumped.h, 1)

            def over(k, shape):
                f = [jump[:, r, k] for r in range(2)]
                if len(shape) == 3:
                    f = [x.unsqueeze(2).to_broadcast(shape) for x in f]
                return f

            wide = [P, GPAIRS, DEC_BATCH]
            advance([ends[:, r].rearrange("p b a -> p a b") for r in range(2)],
                    [S.start[:, r, :, PC:CHUNKS] for r in range(2)], over(0, wide), wide)
            dve.memset(signal[:, 1:2], 0.0).then_inc(states_done.h, 1)
            for j in range(1, RUN - 1):
                wide = [P, GPAIRS, RUNS]
                advance([runs[:, r, :, :, j + 1] for r in range(2)], [runs[:, r, :, :, j] for r in range(2)],
                        over(0, wide), wide)
            wide = [P, GPAIRS, RUNS - 1]
            advance([runs[:, r, :, 1:RUNS, 0] for r in range(2)],
                    [runs[:, r, :, 0:RUNS - 1, RUN - 1] for r in range(2)], over(0, wide), wide)
            flat = [P, GPAIRS]
            advance([end[:, r] for r in range(2)], [runs[:, r, :, RUNS - 1, RUN - 1] for r in range(2)],
                    over(0, flat), flat)
            for b in range(1, RUNS):
                out = [runs[:, r, :, b + 1, 0] if b + 1 < RUNS else end[:, r] for r in range(2)]
                advance(out, [runs[:, r, :, b, 0] for r in range(2)], over(RUN - 1, flat), flat)
            dve.memset(signal[:, 2:3], 0.0).then_inc(states_done.h, 1)
            for a0 in range(0, GPAIRS, FIX):
                a = slice(a0, a0 + FIX)
                wide = [P, FIX, RUNS - 1, RUN - 1]
                advance([runs[:, r, a, 1:RUNS, 1:RUN] for r in range(2)],
                        [runs[:, r, a, 1:RUNS, 0:1].to_broadcast(wide) for r in range(2)],
                        [jump[:, r, 0:RUN - 1, a].rearrange("p j a -> p a j").unsqueeze(2).to_broadcast(wide)
                         for r in range(2)], wide)

        @block.scalar
        def _(act):
            def move(q):
                a = slice(Q * q, Q * (q + 1))
                for r in range(2):
                    src = T.ps[:, 2 + 2 * (q % 2) + r, 0:Q * CHUNKS].rearrange("p (a c) -> p a c", a=Q)
                    act.activation(S.start[:, r, a, 1:PC], src[:, :, 0:PC - 1], ACT.Copy)
                    act.activation(end[:, r, a], src[:, :, PC - 1], ACT.Copy)
                    last = act.activation(ends[:, r, :, a].rearrange("p b a -> p a b"), src[:, :, PC:CHUNKS], ACT.Copy)
                last.then_inc(moved.h, 1)

            for q in range(STEPS):
                act.wait_ge(b_turned.h, q + 1)
                if q:
                    act.wait_ge(added.h, q)
                for r in range(2):
                    last = act.activation(b_rows[:, r], T.ps[:, r, :].rearrange("p (a s) -> p a s", a=Q), ACT.Copy)
                last.then_inc(b_moved.h, 1)
                if q:
                    move(q - 1)
            act.wait_ge(added.h, STEPS)
            move(STEPS - 1)
            for n in range(5):
                act.wait_ge(turned.h, n + 1)
                m = P if n < 4 else 2 * GPAIRS
                act.activation(out_rows[0:m, n, :], T.ps[0:m, n, 0:P], ACT.Copy).then_inc(out_moved.h, 1)

        @block.tensor
        def _(pe):
            def increments(q):
                pe.wait_ge(b_moved.h, q + 1)
                if q >= 2:
                    pe.wait_ge(moved.h, q - 1)
                for a in range(Q):
                    for s in range(2):
                        for r in range(2):
                            mm = pe.matmul(T.ps[half[s], 2 + 2 * (q % 2) + r, a * CHUNKS:(a + 1) * CHUNKS],
                                           b_rows[:, r, a, half[s]], S.u[:, 2 * (Q * q + a) + s, :],
                                           start=True, stop=True)
                mm.then_inc(added.h, 1)

            for q in range(STEPS):
                pe.wait_ge(formed.h, q + 1)
                if q:
                    pe.wait_ge(b_moved.h, q)
                for r in range(2):
                    for a in range(Q):
                        mm = pe.transpose(T.ps[:, r, a * P:(a + 1) * P],
                                          b_pow[:, r, a].rearrange("p t h -> p (t h)"), T.ident[:, :])
                mm.then_inc(b_turned.h, 1)
                increments(q)
            pe.wait_ge(states_done.h, 1)
            for r in range(2):
                for j in range(2):
                    pe.transpose(T.ps[:, 2 * r + j, 0:P],
                                 ends[:, r, 4 * j:4 * j + 4, :].rearrange("p b a -> p (b a)"), T.ident[:, :])\
                      .then_inc(turned.h, 1)
            pe.wait_ge(states_done.h, 2)
            pe.transpose(T.ps[0:2 * GPAIRS, 4, 0:P], end[:, :, :].rearrange("p r a -> p (r a)"), T.ident[:, :])\
              .then_inc(turned.h, 1)

        @block.sync
        def _(sp):
            for r, part_ in enumerate(("re", "im")):
                for j in range(2):
                    sp.wait_ge(out_moved.h, 2 * r + j + 1)
                    sp.dma_start(O[f"s5_{part_}_sample"].rearrange("(j b) (a s) p -> j (b a) (s p)", j=2, s=2)[j],
                                 out_rows[:, 2 * r + j, :]).then_inc(stored.h, 16)
            sp.wait_ge(out_moved.h, 5)
            for r, part_ in enumerate(("re", "im")):
                sp.dma_start(O[f"s5_{part_}_prompt"].rearrange("(a s) p -> a (s p)", s=2),
                             out_rows[r * GPAIRS:(r + 1) * GPAIRS, 4, :]).then_inc(stored.h, 16)
            sp.wait_ge(stored.h, 6 * 16)

        @block.gpsimd
        def _(pool):
            def tt(out, a, b, o):
                T.pool_chain(pool, pool.tensor_tensor(out, a, b, o))

            T.pool_chain(pool, pool.tensor_copy(jump[:, :, 0], S.powers[:, :, CL]))
            t1, t2 = (m2[:, i].rearrange("p k h -> p (k h)")[:, 0:4 * GPAIRS].rearrange("p (n a) -> p n a", n=4)
                      for i in range(2))
            n = 1
            while n < RUN:
                a = [jump[:, r, 0:n] for r in range(2)]
                by = [jump[:, r, n - 1:n].to_broadcast([P, n, GPAIRS]) for r in range(2)]
                for r, (x, y, o) in enumerate(((by[0], by[1], ALU.subtract), (by[1], by[0], ALU.add))):
                    tt(t1[:, 0:n], a[0], x, ALU.mult)
                    tt(t2[:, 0:n], a[1], y, ALU.mult)
                    tt(jump[:, r, n:2 * n], t1[:, 0:n], t2[:, 0:n], o)
                n *= 2
            T.pool_chain(pool, pool.tensor_scalar(minus[:, :, :, :], S.powers[:, :, :, :], -1.0, None, ALU.mult))
            pool.memset(signal[:, 0:1], 0.0).then_inc(jumped.h, 1)
            for q in range(GPAIRS // 4):
                a = slice(4 * q, 4 * q + 4)
                wide = [P, 4, CL + 1, GH]
                c = [S.c_t[:, r, a, :].unsqueeze(2).to_broadcast(wide) for r in range(2)]
                f, g = ([x[:, r, :, a].rearrange("p k a -> p a k").unsqueeze(3).to_broadcast(wide) for r in range(2)]
                        for x in (S.powers, minus))
                for r, (x, y) in enumerate(((f[0], g[1]), (g[1], g[0]))):
                    pool.tensor_tensor(c_pow[:, r, a], c[0], x, ALU.mult)
                    tt(m2[:, :, :, :], c[1], y, ALU.mult)
                    tt(c_pow[:, r, a], c_pow[:, r, a], m2[:, :, :, :], ALU.add)


def phase_s5_outputs(T, S, c_pow):
    nc = T.nc
    names = ("kernels", "placed", "mixed", "gelued", "turned", "rounded", "rested")
    kernels, placed, mixed, gelued, turned, rounded, rested = (Count(T.ctx, nc, "s5o_" + n) for n in names)
    zeroed = Count(T.ctx, nc, "s5o_zeroed")
    spread = [Count(T.ctx, nc, f"s5o_spread{i}") for i in range(2)]
    A = GT // 2
    with ExitStack() as ctx:
        def sb(name, shape, dt=F32):
            return ctx.enter_context(nc.sbuf_tensor("s5o_" + name, shape, dt))

        kernel_of = sb("kernel", [GH, 2, 2 * A, 2 * P])
        toeplitz = sb("toeplitz", [P, 2, 2 * A, P])
        diag = sb("diag", [GH, 2 * A, GH])
        gel = sb("gel", [P, CL, A, 2, GH])
        block = ctx.enter_context(nc.Block())
        half = [slice(0, HD), slice(HD, P)]

        @block.tensor
        def _(pe):
            def make_kernels(e):
                if e:
                    pe.wait_ge(placed.h, e)
                for s in range(2):
                    for a in range(A):
                        gp = A * e + a
                        for r in range(2):
                            mm = pe.matmul(T.ps[0:GH, s, a * P:(a + 1) * P], S.b_bar[half[s], r, gp, :],
                                           c_pow[half[s], r, gp, 0:CL, :].rearrange("p k h -> p (k h)"),
                                           start=(r == 0), stop=(r == 1))
                mm.then_inc(kernels.h, 1)

            def outputs(e):
                pe.wait_ge(spread[e % 2].h, (e // 2 + 1) * CL * 16)
                if e:
                    pe.wait_ge(gelued.h, 2 * e)
                for s in range(2):
                    for a in range(A):
                        gp = A * e + a
                        out = T.ps[0:CHUNKS, 2 + s, a * P:(a + 1) * P]
                        pe.matmul(out, S.u[:, 2 * gp + s, :], toeplitz[:, e % 2, s * A + a, :], start=True, stop=False)
                        for r in range(2):
                            mm = pe.matmul(out, S.start[half[s], r, gp, :],
                                           c_pow[half[s], r, gp, 1:CL + 1, :].rearrange("p k h -> p (k h)"),
                                           start=False, stop=(r == 1))
                mm.then_inc(mixed.h, 1)

            def turn(e):
                pe.wait_ge(gelued.h, 2 * e + 2)
                if e:
                    pe.wait_ge(rested.h, e)
                for t in range(CL):
                    mm = pe.transpose(T.ps[:, 4 + t // 4, (t % 4) * CHUNKS:(t % 4 + 1) * CHUNKS],
                                      gel[0:CHUNKS, t].rearrange("p a s h -> p (a s h)"), T.ident[0:CHUNKS, 0:CHUNKS])
                mm.then_inc(turned.h, 1)

            make_kernels(0)
            for e in range(KT):
                if e + 1 < KT:
                    make_kernels(e + 1)
                outputs(e)
                turn(e)

        @block.vector
        def _(dve):
            def place(e):
                dve.wait_ge(kernels.h, e + 1)
                if e >= 2:
                    dve.wait_ge(spread[e % 2].h, (e // 2) * CL * 16)
                dst = kernel_of[:, e % 2, :, P:2 * P]
                T.dve_chain(dve, dve.tensor_copy(dst.rearrange("p (s a) k -> p s a k", s=2),
                                                 T.ps[0:GH, 0:2, :].rearrange("p s (a k) -> p s a k", a=A)))
                skip = S.skip[:, GT * e:GT * (e + 1)].rearrange("p (a s) -> p s a", s=2)
                for s in range(2):
                    last = dve.tensor_tensor(diag[:, s * A:(s + 1) * A, :],
                                             T.ident[0:GH, 0:GH].unsqueeze(1).to_broadcast([GH, A, GH]),
                                             skip[:, s].unsqueeze(2).to_broadcast([GH, A, GH]), ALU.mult)
                T.dve_chain(dve, last)
                dve.tensor_tensor(dst[:, :, 0:GH], dst[:, :, 0:GH], diag[:, :, :], ALU.add).then_inc(placed.h, 1)
                dve.wait_ge(placed.h, e + 1)

            def rest(e):
                dve.wait_ge(rounded.h, e + 1)
                dve.tensor_tensor(T.x_lo[:, e].rearrange("p (c b t) -> p b t c", b=2, t=4),
                                  T.ps[:, 4:6, 0:4 * CHUNKS].rearrange("p b (t c) -> p b t c", t=4),
                                  T.x_hi[:, e].rearrange("p (c b t) -> p b t c", b=2, t=4).bitcast(F32),
                                  ALU.subtract).then_inc(rested.h, 1)

            dve.memset(kernel_of[:, :, :, 0:P], 0.0).then_inc(zeroed.h, 1)
            dve.wait_ge(zeroed.h, 1)
            place(0)
            for e in range(KT):
                if e + 1 < KT:
                    place(e + 1)
                rest(e)

        @block.scalar
        def _(act):
            for e in range(KT):
                act.wait_ge(mixed.h, e + 1)
                if e:
                    act.wait_ge(turned.h, e)
                for s in range(2):
                    act.activation(gel[0:CHUNKS, :, :, s, :].rearrange("p t a h -> p a t h"),
                                   T.ps[0:CHUNKS, 2 + s, :].rearrange("p (a t h) -> p a t h", a=A, h=GH),
                                   ACT.Gelu_apprx_tanh).then_inc(gelued.h, 1)
                act.wait_ge(turned.h, e + 1)
                act.activation(T.x_hi[:, e].rearrange("p (c b t) -> p b t c", b=2, t=4),
                               T.ps[:, 4:6, 0:4 * CHUNKS].rearrange("p b (t c) -> p b t c", t=4), ACT.Copy)\
                   .then_inc(rounded.h, 1)

        @block.sync
        def _(sp):
            for e in range(KT):
                sp.wait_ge(placed.h, e + 1)
                if e >= 2:
                    sp.wait_ge(mixed.h, e - 1)
                for t in range(CL):
                    sp.dma_start(toeplitz[t * GH:(t + 1) * GH, e % 2],
                                 kernel_of[:, e % 2, :, P - t * GH:2 * P - t * GH]).then_inc(spread[e % 2].h, 16)


def host_tables():
    half = HD // 2
    inv = (10000.0 ** (-np.arange(half) / half)).astype(np.float32)
    pos = np.zeros((P, TT), np.float32)
    step = np.zeros((P, TT), np.float64)
    for t in range(PT):
        pos[:, t] = t * P + np.arange(P)
        step[:, t] = pos[:, t]
    pos[NS:, PT] = PAST_LEN + np.arange(NS) % DEC_SEQ
    step[NS:, PT] = np.arange(NS) % DEC_SEQ
    ang = (pos[:, :, None] * inv).astype(np.float64)
    log_g = np.log1p(-np.exp2(-5.0 - np.arange(HEADS)))
    f = lambda a: np.ascontiguousarray(a, np.float32)
    at = np.arange(P)
    causal = np.where(at[None, :] <= at[:, None], 0.0, NEG)
    keep = at[None, :] >= at[:, None]
    s = np.arange(NS)
    keep_s = (s[None, :] >= s[:, None]) & (s[None, :] // DEC_SEQ == s[:, None] // DEC_SEQ)
    select = s[:, None] // DEC_SEQ == np.arange(DEC_BATCH)
    of_row = log_g.reshape(PAIRS, 2)[:, np.arange(P) // HD].T
    row_b, row_q = at // HD, at % DEC_SEQ
    past_mask = np.full((P, BP, NS), NEG)
    for bp in range(BP):
        seen = (s // DEC_SEQ == 2 * bp + row_b[:, None]) & (s % DEC_SEQ <= row_q[:, None])
        past_mask[:, bp][seen] = 0.0
    return {"past_mask": f(past_mask), "block_no": f(np.tile(np.arange(BLOCKS) + 1.0, (P, 1))), "causal": f(causal), "keep": f(keep), "keep_s": f(keep_s), "select": f(select),
            "power": f(np.exp(of_row * SEQ)), "power_s": f(np.exp(of_row * DEC_SEQ)), "ident": np.eye(P, dtype=np.float32), "rope_cos": f(np.cos(ang)),
            "rope_sin": f(np.stack([-np.sin(ang), np.sin(ang)], 2)),
            "decay_q": f(np.exp(log_g * (step[:, :, None] + 1))),
            "decay_k": f(np.exp(-log_g * (step[:, :, None] + 1)) * HD ** -0.5)}


def program(nc, I, O):
    rows = lambda a: a.rearrange("b s d -> (b s) d")
    ffn = [[(I[f"ffn{n}_w_gate"][layer], I[f"ffn{n}_w_up"][layer], I[f"ffn{n}_w_down"][layer]) for n in (1, 2)]
           for layer in range(DEPTH)]
    first = lambda w: [gate_piece(w[0], 0), gate_piece(w[1], 0)]
    w_in, w_out = I["w_in_ab"][0], I["w_out_ab"][0]
    s5_out, s5_gate = I["s5_w_out"][0], I["s5_w_gate"][0]
    with ExitStack() as ctx:
        T = open_trunk(ctx, nc)
        phase_load(T, rows(I["x_prompt"]), rows(I["x_sample"]), rows(I["ln_g"]), rows(I["ln_b"]), I["ident"],
                   first(ffn[0][0]))
        phase_ffn(T, *ffn[0][0], 0, [in_piece(w_in, 0), in_piece(w_in, 1)])
        M = Trunk()
        with ExitStack() as actx:
            open_mix(actx, nc, M, "attention")
            with ExitStack() as rctx:
                open_mix(rctx, nc, M, "retention")
                phase_project(T, M, w_in, I["rope_cos"], I["rope_sin"], I["decay_q"], I["decay_k"], O,
                              [out_piece(w_out, 0), out_piece(w_out, 1)])
                phase_attend_prompt(T, M, I["causal"])
                phase_retain_prompt(T, M, I["keep"], I["power"], O["state_prompt"])
                phase_retain_samples(T, M, I["state_ret"][0], I["keep_s"], I["select"], I["power_s"],
                                     O["state_sample"])
            phase_attend_samples(T, M, I["cache_k"][0], I["cache_v"][0], I["page_table"], I["past_mask"],
                                 I["block_no"], I["cache_k"].shape[1])
        phase_out(T, w_out, None, 1, first(ffn[0][1]))
        phase_ffn(T, *ffn[0][1], 2, first(ffn[1][0]))
        with ExitStack() as sctx:
            S = open_s5_constants(sctx, nc)
            phase_ffn(T, *ffn[1][0], 3, [out_piece(s5_out, 0), out_piece(s5_gate, 0)], False,
                      S5Constants(T, S, I))
            open_s5(sctx, nc, S)
            phase_s5_inputs(T, S, I)
            c_pow = sctx.enter_context(nc.sbuf_tensor("s5_c_pow", [P, 2, GPAIRS, CL + 1, GH], F32))
            phase_s5_scan(T, S, c_pow, O)
            phase_s5_outputs(T, S, c_pow)
        phase_out(T, s5_out, s5_gate, 4, first(ffn[1][1]))
        phase_ffn(T, *ffn[1][1], 5, None, False)
        phase_store(T, O["y_prompt"], O["y_sample"])


OUTPUTS = (
    ("y_prompt", (SEQ, D_MODEL), (1, SEQ, D_MODEL)),
    ("y_sample", (NS, D_MODEL), (DEC_BATCH, DEC_SEQ, D_MODEL)),
    ("k_prompt", (SEQ, MIX), (1, 1, PT, PAGE, HEADS, HD)),
    ("v_prompt", (SEQ, MIX), (1, 1, PT, PAGE, HEADS, HD)),
    ("k_sample", (NS, MIX), (1, DEC_BATCH, DEC_SEQ, HEADS, HD)),
    ("v_sample", (NS, MIX), (1, DEC_BATCH, DEC_SEQ, HEADS, HD)),
    ("state_prompt", (HEADS, HD, HD), (1, 1, HEADS, HD, HD)),
    ("state_sample", (DEC_BATCH, HEADS, HD, HD), (1, DEC_BATCH, HEADS, HD, HD)),
    ("s5_re_prompt", (GROUPS, STATES), (1, 1, GROUPS, STATES)),
    ("s5_im_prompt", (GROUPS, STATES), (1, 1, GROUPS, STATES)),
    ("s5_re_sample", (DEC_BATCH, GROUPS, STATES), (1, DEC_BATCH, GROUPS, STATES)),
    ("s5_im_sample", (DEC_BATCH, GROUPS, STATES), (1, DEC_BATCH, GROUPS, STATES)),
)


def kernel(**inputs):
    import concourse.bacc as bacc
    from concourse.bass_utils import run_bass_kernel_spmd

    nc = bacc.Bacc("TRN2", target_bir_lowering=False, num_devices=1)
    arrays = {name: np.ascontiguousarray(a) for name, a in inputs.items()}
    arrays.update(host_tables())
    I = {name: nc.dram_tensor(f"in_{name}", a.shape, mybir.dt.from_np(a.dtype), kind="ExternalInput").ap()
         for name, a in arrays.items()}
    O = {name: nc.dram_tensor(f"out_{name}", shape, F32, kind="ExternalOutput").ap() for name, shape, _ in OUTPUTS}
    program(nc, I, O)
    r = run_bass_kernel_spmd(nc, [{f"in_{name}": a for name, a in arrays.items()}], core_ids=[0])
    return tuple(np.reshape(r.results[0][f"out_{name}"], shape) for name, _, shape in OUTPUTS)
```

```python
import math
from contextlib import ExitStack

import concourse.bass as bass
import numpy as np
from concourse import mybir
from concourse.alu_op_type import AluOpType as ALU

F32 = mybir.dt.float32
F32R = mybir.dt.float32r
I32 = mybir.dt.int32
ACT = mybir.ActivationFunctionType
AX_X = mybir.AxisListType.X

P = 128
D_MODEL, SEQ, DEC_BATCH, DEC_SEQ, PAST_LEN, PAGE = 1024, 512, 8, 8, 1024, 128
NS = DEC_BATCH * DEC_SEQ
NT = SEQ + NS
NH = NT // 2
KT = D_MODEL // P
D_FF = ((8 * D_MODEL // 3 + 127) // 128) * 128
FT = D_FF // P
HF = FT // 2
DEPTH = 2
ALPHA = (2 * DEPTH) ** 0.25
LN_EPS = 1e-5
GN_EPS = 1e-6
NEG = -1e30
PT = SEQ // P
HD = 64
HEADS = 8
PAIRS = HEADS // 2
MIX = HEADS * HD


class Count:

    def __init__(self, ctx, nc, name):
        self.h = ctx.enter_context(nc.semaphore(name))
        self.n = 0

    def done(self, k):
        return self.n + k

    def close(self, k):
        self.n += k


class Chain:

    def __init__(self, ctx, nc, name):
        self.h = ctx.enter_context(nc.semaphore(name))
        self.n = 0

    def __call__(self, eng, ins):
        self.n += 1
        ins.then_inc(self.h, 1)
        eng.wait_ge(self.h, self.n)


class Trunk:
    pass


def halves(ap):
    return ap.rearrange("p (n t) -> p n t", n=2)


def open_trunk(ctx, nc):
    T = Trunk()
    T.ctx, T.nc = ctx, nc

    def sb(name, shape, dt=F32):
        return ctx.enter_context(nc.sbuf_tensor(name, shape, dt))

    def count(name):
        return Count(ctx, nc, name)

    T.x = sb("x", [P, KT, NT])
    T.x_hi = sb("x_hi", [P, KT, NT], F32R)
    T.x_lo = sb("x_lo", [P, KT, NT], F32R)
    T.w_raw = sb("w_raw", [P, 2, HF * P])
    T.w_hi = sb("w_hi", [P, 2, HF * P], F32R)
    T.w_lo = sb("w_lo", [P, 2, HF * P], F32R)
    T.ident = sb("ident", [P, P])
    T.ones = sb("ones", [P, P])
    T.ln_gain = sb("ln_gain", [P, DEPTH * 3, KT])
    T.ln_bias = sb("ln_bias", [P, DEPTH * 3, KT])
    T.eps = sb("eps", [P, 2])
    T.ps = ctx.enter_context(nc.psum_tensor("ps", [P, 8, 512], F32))
    T.w_loaded = [count("w_loaded0"), count("w_loaded1")]
    T.w_hi_ready = [count("w_hi_ready0"), count("w_hi_ready1")]
    T.w_split = [count("w_split0"), count("w_split1")]
    T.w_used = [count("w_used0"), count("w_used1")]
    T.norm_before = None
    T.pieces = 0
    T.const_ready, T.const_loaded = count("const_ready"), count("const_loaded")
    T.silu_done, T.glu_done, T.h_rounded, T.h_done = map(count, ("silu_done", "glu_done", "h_rounded", "h_done"))
    T.res_done, T.acc_added, T.sum_done, T.centred = map(count, ("res_done", "acc_added", "sum_done", "centred"))
    T.squared, T.var_done, T.rstd_ready, T.normed = map(count, ("squared", "var_done", "rstd_ready", "normed"))
    T.affine_done, T.x_rounded, T.x_ready = map(count, ("affine_done", "x_rounded", "x_ready"))
    T.pe_done, T.dve_done, T.act_done, T.pool_done = map(count, ("pe_done", "dve_done", "act_done", "pool_done"))
    T.stored = count("stored")
    T.dve_chain = Chain(ctx, nc, "dve_chain")
    T.pool_chain = Chain(ctx, nc, "pool_chain")
    return T



def load_piece(T, sp, slot, u, src):
    n = src.shape[1] * src.shape[2]
    dst = T.w_raw[:, slot, 0:n].rearrange("p (a b) -> p a b", a=src.shape[1])
    sp.wait_ge(T.w_split[slot].h, u + 1)
    sp.dma_start(dst, src).then_inc(T.w_loaded[slot].h, 16)


def round_piece(T, act, slot, u, n):
    act.wait_ge(T.w_loaded[slot].h, (u + 1) * 16)
    act.wait_ge(T.w_used[slot].h, u + 1)
    act.activation(T.w_hi[:, slot, 0:n], T.w_raw[:, slot, 0:n], ACT.Copy).then_inc(T.w_hi_ready[slot].h, 1)


def rest_piece(T, dve, slot, u, n):
    dve.wait_ge(T.w_hi_ready[slot].h, u + 1)
    dve.tensor_tensor(T.w_lo[:, slot, 0:n], T.w_raw[:, slot, 0:n], T.w_hi[:, slot, 0:n].bitcast(F32),
                      ALU.subtract).then_inc(T.w_split[slot].h, 1)


def product3(pe, out, w_hi, w_lo, m_hi, m_lo, first, last):
    pe.matmul(out, w_hi, m_hi, start=first, stop=False)
    pe.matmul(out, w_hi, m_lo, start=False, stop=False)
    return pe.matmul(out, w_lo, m_hi, start=False, stop=last)



class Norm:

    ON_POOL = 2

    def __init__(self, T, row, scale, acc_steps, pieces, products):
        self.acc_steps, self.pieces, self.products = acc_steps, pieces, products
        self.T, self.row, self.squares = T, row, T.gate
        self.acc, self.rstd = T.prod[:, 0], T.prod[:, 1]
        self.base = {c: c.n for c in self.counts()}
        self.eps = T.eps[:, int(scale) - 1:int(scale)]
        self.mean_ps = T.ps[:, 4:6, 0:NH]
        self.var_ps = T.ps[:, 6:8, 0:NH]

    def tensor(self, pe):
        T = self.T
        pe.wait_ge(T.acc_added.h, self.done(T.acc_added, self.acc_steps))
        for n in range(2):
            mm = pe.matmul(self.mean_ps[:, n], T.ones[:, :], self.acc[:, n * NH:(n + 1) * NH],
                           start=True, stop=True)
        mm.then_inc(T.sum_done.h, 1)
        for k in range(KT):
            pe.wait_ge(T.squared.h, self.done(T.squared, k + 1))
            for n in range(2):
                mm = pe.matmul(self.var_ps[:, n], T.ones[:, :], self.squares[:, k % 2, n * NH:(n + 1) * NH],
                               start=(k == 0), stop=(k == KT - 1))
            mm.then_inc(T.var_done.h, 1)

    def scalar(self, act):
        T = self.T
        if self.pieces is not None:
            for slot in range(2):
                round_piece(T, act, slot, self.pieces, KT * P)
        for k in range(KT):
            act.wait_ge(T.centred.h, self.done(T.centred, k + 1))
            if k >= 2:
                act.wait_ge(T.var_done.h, self.done(T.var_done, k - 1))
            act.activation(self.squares[:, k % 2], T.x[:, k], ACT.Square).then_inc(T.squared.h, 1)
        act.wait_ge(T.var_done.h, self.done(T.var_done, KT))
        act.activation(halves(self.rstd[:, :]), self.var_ps, ACT.Sqrt, bias=self.eps).then_inc(T.rstd_ready.h, 1)
        for k in range(KT):
            act.wait_ge(T.normed.h, self.done(T.normed, k + 1))
            if self.products:
                act.activation(T.x_hi[:, k], T.x[:, k], ACT.Identity, bias=self.bias(k)).then_inc(T.x_rounded.h, 1)
            else:
                act.activation(T.x[:, k], T.x[:, k], ACT.Identity, bias=self.bias(k)).then_inc(T.affine_done.h, 1)
        if self.products:
            for k in range(KT - self.ON_POOL):
                act.wait_ge(T.x_ready.h, self.done(T.x_ready, k + 1))
                act.activation(T.x[:, k], T.x[:, k], ACT.Identity, bias=self.bias(k)).then_inc(T.affine_done.h, 1)

    def bias(self, k):
        return self.T.ln_bias[:, self.row, k:k + 1]

    def vector(self, dve):
        T = self.T
        dve.wait_ge(T.sum_done.h, self.done(T.sum_done, 1))
        for k in range(KT):
            dve.scalar_tensor_tensor(halves(T.x[:, k]), self.mean_ps, -1.0 / D_MODEL, halves(T.x[:, k]),
                                     ALU.mult, ALU.add).then_inc(T.centred.h, 1)
        if self.pieces is not None:
            for slot in range(2):
                rest_piece(T, dve, slot, self.pieces, KT * P)
        dve.wait_ge(T.rstd_ready.h, self.done(T.rstd_ready, 1))
        dve.reciprocal(self.rstd[:, :], self.rstd[:, :]).then_inc(T.rstd_ready.h, 1)
        dve.wait_ge(T.rstd_ready.h, self.done(T.rstd_ready, 2))

        def rest(k):
            dve.wait_ge(T.x_rounded.h, self.done(T.x_rounded, k + 1))
            dve.scalar_tensor_tensor(T.x_lo[:, k], T.x[:, k], self.bias(k), T.x_hi[:, k].bitcast(F32),
                                     ALU.add, ALU.subtract).then_inc(T.x_ready.h, 1)

        for k in range(KT):
            dve.scalar_tensor_tensor(T.x[:, k], T.x[:, k], T.ln_gain[:, self.row, k:k + 1], self.rstd[:, :],
                                     ALU.mult, ALU.mult).then_inc(T.normed.h, 1)
            if self.products and k >= 2:
                rest(k - 2)
        if self.products:
            for k in range(KT - 2, KT):
                rest(k)

    def gpsimd(self, pool):
        T = self.T
        if self.products:
            for k in range(KT - self.ON_POOL, KT):
                pool.wait_ge(T.x_ready.h, self.done(T.x_ready, k + 1))
                pool.tensor_scalar(T.x[:, k], T.x[:, k], self.bias(k), None, ALU.add).then_inc(T.affine_done.h, 1)

    def counts(self):
        T = self.T
        split = KT if self.products else 0
        return {T.acc_added: self.acc_steps, T.sum_done: 1, T.squared: KT, T.var_done: KT, T.centred: KT,
                T.normed: KT, T.affine_done: KT, T.rstd_ready: 2, T.x_rounded: split, T.x_ready: split}

    def done(self, count, k):
        return self.base[count] + k

    def feature_ready(self, pe, k):
        pe.wait_ge(self.T.x_ready.h, self.done(self.T.x_ready, k + 1))

    def close(self):
        for c, k in self.counts().items():
            c.close(k)


def end_with_norm(T, norm, join):
    norm.close()
    T.norm_before = norm if join else None


def open_norm_buffers(ctx, T):
    T.gate = ctx.enter_context(T.nc.sbuf_tensor(f"gate{T.pieces}", [P, 2, NT], F32))
    T.prod = ctx.enter_context(T.nc.sbuf_tensor(f"prod{T.pieces}", [P, 2, NT], F32))



def phase_load(T, x_prompt, x_sample, ln_g, ln_b, ident, first):
    nc = T.nc
    with ExitStack() as ctx:
        rows = ctx.enter_context(nc.sbuf_tensor("x_rows", [P, PT + 1, D_MODEL], F32))
        credit = ctx.enter_context(nc.sbuf_tensor("credit", [P, 8], F32))
        block = ctx.enter_context(nc.Block())
        loaded, ln_loaded, copied = T.const_loaded, Count(T.ctx, nc, "ln_loaded"), Count(T.ctx, nc, "x_copied")

        @block.sync
        def _(sp):
            sp.dma_start(T.ident[:, :], ident).then_inc(loaded.h, 16)
            for t in range(PT):
                sp.dma_start(rows[:, t], x_prompt[t * P:(t + 1) * P, :]).then_inc(loaded.h, 16)
            sp.dma_start(rows[NS:P, PT], x_sample).then_inc(loaded.h, 16)
            for slot in range(2):
                load_piece(T, sp, slot, T.pieces, first[slot])

        @block.gpsimd
        def _(pool):
            with nc.allow_non_contiguous_dma(reason="layer norm gains and biases, feature-major"):
                pool.dma_start(T.ln_gain[:, :, :], ln_g.rearrange("r (k p) -> p r k", p=P)).then_inc(ln_loaded.h, 16)
                pool.dma_start(T.ln_bias[:, :, :], ln_b.rearrange("r (k p) -> p r k", p=P)).then_inc(ln_loaded.h, 16)

        @block.tensor
        def _(pe):
            pe.wait_ge(loaded.h, (PT + 2) * 16)
            for k in range(KT):
                b = 2 * (k % 4)
                if k >= 4:
                    pe.wait_ge(copied.h, 2 * (k - 3))
                for t in range(PT):
                    pe.transpose(T.ps[:, b, t * P:(t + 1) * P], rows[:, t, k * P:(k + 1) * P], T.ident[:, :])
                pe.transpose(T.ps[:, b + 1, 0:NS], rows[NS:P, PT, k * P:(k + 1) * P], T.ident[NS:P, NS:P])\
                  .then_inc(T.pe_done.h, 1)

        @block.vector
        def _(dve):
            dve.memset(T.ones[:, :], 1.0).then_inc(T.const_ready.h, 1)
            for scale in (1, 2):
                dve.memset(T.eps[:, scale - 1:scale], LN_EPS * D_MODEL * scale * scale).then_inc(T.const_ready.h, 1)
            for slot in range(2):
                dve.memset(credit[:, slot:slot + 1], 0.0).then_inc(T.w_split[slot].h, 1)
                dve.memset(credit[:, 2 + slot:3 + slot], 0.0).then_inc(T.w_used[slot].h, 1)
                dve.memset(credit[:, 4 + slot:5 + slot], 0.0).then_inc(T.glu_done.h, 1)
                dve.memset(credit[:, 6 + slot:7 + slot], 0.0).then_inc(T.res_done.h, 1)
            for k in range(KT + 1):
                if k < KT:
                    b = 2 * (k % 4)
                    dve.wait_ge(T.pe_done.h, T.pe_done.done(k + 1))
                    dve.tensor_copy(T.x[:, k, 0:SEQ], T.ps[:, b, 0:SEQ]).then_inc(copied.h, 1)
                    dve.tensor_copy(T.x[:, k, SEQ:NT], T.ps[:, b + 1, 0:NS]).then_inc(copied.h, 1)
                if k >= 1:
                    dve.wait_ge(T.act_done.h, T.act_done.done(k))
                    dve.tensor_tensor(T.x_lo[:, k - 1], T.x[:, k - 1], T.x_hi[:, k - 1].bitcast(F32), ALU.subtract)\
                       .then_inc(T.dve_done.h, 1)
            for slot in range(2):
                rest_piece(T, dve, slot, T.pieces, KT * P)
            dve.wait_ge(ln_loaded.h, 32)
            dve.tensor_scalar(T.ln_gain[:, :, :], T.ln_gain[:, :, :], math.sqrt(D_MODEL), None, ALU.mult)\
               .then_inc(T.const_ready.h, 1)

        @block.scalar
        def _(act):
            for k in range(KT):
                act.wait_ge(copied.h, 2 * k + 2)
                act.activation(T.x_hi[:, k], T.x[:, k], ACT.Copy).then_inc(T.act_done.h, 1)
            for slot in range(2):
                round_piece(T, act, slot, T.pieces, KT * P)
    T.const_loaded.close((PT + 2) * 16)
    T.pe_done.close(KT)
    T.dve_done.close(KT)
    T.glu_done.close(2)
    T.res_done.close(2)


def gate_piece(w, ft):
    return w.rearrange("(k p) f -> p k f", p=P)[:, :, bass.ds(ft * P, P)]


def down_piece(w, half, d):
    return w[half * HF * P:(half + 1) * HF * P, :].rearrange("(f p) d -> p f d", p=P)[:, :, bass.ds(d * P, P)]


def phase_ffn(T, w_gate, w_up, w_down, row, nxt, products=True, join=False, beside=None):
    nc = T.nc
    U = T.pieces
    G = KT * P
    D = HF * P
    LOOPED = FT - 2
    DLOOPED = KT - 2
    with ExitStack() as ctx:
        def sb(name, shape, dt=F32):
            return ctx.enter_context(nc.sbuf_tensor(f"{name}_{row}", shape, dt))

        h_hi = sb("h_hi", [P, FT, NT], F32R)
        h_lo = sb("h_lo", [P, FT, NT], F32R)
        gate, prod = T.gate, T.prod
        acc, before = prod[:, 0], T.norm_before
        norm = Norm(T, row, 2.0, KT + 1, U + FT + KT if nxt else None, products)
        silu0, glu0, hr0, h0 = T.silu_done.n, T.glu_done.n, T.h_rounded.n, T.h_done.n
        res0, acc0 = T.res_done.n, T.acc_added.n
        if beside:
            beside.open(ctx)
        block = ctx.enter_context(nc.Block())

        @block.sync
        def _(sp):
            with sp.Fori(1, FT) as ft:
                for slot, w in ((0, w_gate), (1, w_up)):
                    src = gate_piece(w, ft)
                    load_piece(T, sp, slot, U + ft, src)
            with sp.Fori(0, KT) as d:
                for slot in range(2):
                    src = down_piece(w_down, slot, d)
                    load_piece(T, sp, slot, U + FT + d, src)
            for slot in range(2):
                if nxt:
                    load_piece(T, sp, slot, U + FT + KT, nxt[slot])

        @block.tensor
        def _(pe):
            def gate_up(ft, j):
                pe.wait_ge(T.glu_done.h, ft + (glu0 - 1))
                for slot in range(2):
                    pe.wait_ge(T.w_split[slot].h, ft + (U + 2))
                    for n in range(2):
                        for k in range(KT):
                            cols = slice(n * NH, (n + 1) * NH)
                            mm = product3(pe, T.ps[:, 4 * j + 2 * slot + n, 0:NH],
                                          T.w_hi[:, slot, k * P:(k + 1) * P], T.w_lo[:, slot, k * P:(k + 1) * P],
                                          T.x_hi[:, k, cols], T.x_lo[:, k, cols], k == 0, k == KT - 1)
                    mm.then_inc(T.w_used[slot].h, 1)

            def down(d, j):
                pe.wait_ge(T.res_done.h, d + (res0 - 1))
                for slot in range(2):
                    pe.wait_ge(T.h_done.h, h0 + FT - 1 + slot)
                    pe.wait_ge(T.w_split[slot].h, d + (U + FT + 2))
                    for n in range(2):
                        for f in range(HF):
                            cols = slice(n * NH, (n + 1) * NH)
                            ft = slot * HF + f
                            mm = product3(pe, T.ps[:, 2 * j + n, 0:NH],
                                          T.w_hi[:, slot, f * P:(f + 1) * P], T.w_lo[:, slot, f * P:(f + 1) * P],
                                          h_hi[:, ft, cols], h_lo[:, ft, cols], ft == 0, ft == FT - 1)
                    mm.then_inc(T.w_used[slot].h, 1)

            def first_gate_up():
                for slot in range(2):
                    pe.wait_ge(T.w_split[slot].h, U + 2)
                for k in range(KT):
                    if before:
                        before.feature_ready(pe, k)
                    for slot in range(2):
                        for n in range(2):
                            cols = slice(n * NH, (n + 1) * NH)
                            mm = product3(pe, T.ps[:, 2 * slot + n, 0:NH],
                                          T.w_hi[:, slot, k * P:(k + 1) * P], T.w_lo[:, slot, k * P:(k + 1) * P],
                                          T.x_hi[:, k, cols], T.x_lo[:, k, cols], k == 0, k == KT - 1)
                        if k == KT - 1:
                            mm.then_inc(T.w_used[slot].h, 1)

            if before:
                before.tensor(pe)
            first_gate_up()
            gate_up(1, 1)
            with pe.Fori(2, FT, 2) as ft:
                for j in range(2):
                    gate_up(ft + j, j)
            with pe.Fori(0, KT, 2) as d:
                for j in range(2):
                    down(d + j, j)
            if not join:
                norm.tensor(pe)

        @block.scalar
        def _(act):
            def step(ft, j, n):
                for slot in range(2):
                    round_piece(T, act, slot, ft + (U + 1), n)
                act.wait_ge(T.w_used[1].h, ft + (U + 2))
                act.activation(halves(gate[:, j]), T.ps[:, 4 * j:4 * j + 2, 0:NH], ACT.Silu)\
                   .then_inc(T.silu_done.h, 1)

            if before:
                before.scalar(act)
            with act.Fori(0, LOOPED, 2) as ft:
                for j in range(2):
                    step(ft + j, j, G)
            step(FT - 2, 0, G)
            step(FT - 1, 1, D)
            with act.Fori(1, KT) as d:
                for slot in range(2):
                    round_piece(T, act, slot, d + (U + FT), D)
            if not join:
                norm.scalar(act)

        @block.vector
        def _(dve):
            def step(ft, j, n):
                for slot in range(2):
                    rest_piece(T, dve, slot, ft + (U + 1), n)
                dve.wait_ge(T.silu_done.h, ft + (silu0 + 1))
                dve.tensor_tensor(halves(prod[:, j]), halves(gate[:, j]), T.ps[:, 4 * j + 2:4 * j + 4, 0:NH],
                                  ALU.mult).then_inc(T.glu_done.h, 1)
                dve.wait_ge(T.glu_done.h, ft + (glu0 + 1))
                hi = h_hi[:, bass.ds(ft, 1), :].rearrange("p a t -> p (a t)")
                lo = h_lo[:, bass.ds(ft, 1), :].rearrange("p a t -> p (a t)")
                dve.tensor_copy(hi, prod[:, j]).then_inc(T.h_rounded.h, 1)
                dve.wait_ge(T.h_rounded.h, ft + (hr0 + 1))
                dve.tensor_tensor(lo, prod[:, j], hi.bitcast(F32), ALU.subtract).then_inc(T.h_done.h, 1)

            if before:
                before.vector(dve)
            with dve.Fori(0, LOOPED, 2) as ft:
                for j in range(2):
                    step(ft + j, j, G)
            step(FT - 2, 0, G)
            step(FT - 1, 1, D)
            if before:
                dve.wait_ge(T.affine_done.h, before.done(T.affine_done, KT))
            dve.wait_ge(T.h_done.h, h0 + FT)
            dve.memset(acc, 0.0).then_inc(T.acc_added.h, 1)

            def add(d, j):
                dve.wait_ge(T.w_used[1].h, d + (U + FT + 2))
                xd = T.x[:, bass.ds(d, 1), :].rearrange("p a t -> p (a t)")
                dve.scalar_tensor_tensor(halves(xd), halves(xd), 2.0 * ALPHA, T.ps[:, 2 * j:2 * j + 2, 0:NH],
                                         ALU.mult, ALU.add).then_inc(T.res_done.h, 1)
                dve.wait_ge(T.res_done.h, d + (res0 + 1))
                dve.wait_ge(T.acc_added.h, d + (acc0 + 1))
                dve.tensor_tensor(acc, acc, xd, ALU.add).then_inc(T.acc_added.h, 1)

            with dve.Fori(0, DLOOPED, 2) as d:
                for j in range(2):
                    for slot in range(2):
                        rest_piece(T, dve, slot, d + (j + U + FT + 1), D)
                    add(d + j, j)
            for slot in range(2):
                rest_piece(T, dve, slot, U + FT + KT - 1, D)
            add(KT - 2, 0)
            add(KT - 1, 1)
            if not join:
                norm.vector(dve)

        @block.gpsimd
        def _(pool):
            if before:
                before.gpsimd(pool)
            if beside:
                beside.gpsimd(pool)
            if not join:
                norm.gpsimd(pool)
    for c, k in ((T.silu_done, FT), (T.glu_done, FT), (T.h_rounded, FT), (T.h_done, FT), (T.res_done, KT)):
        c.close(k)
    T.pieces += FT + KT
    end_with_norm(T, norm, join)


def phase_store(T, y_prompt, y_sample):
    nc = T.nc
    with ExitStack() as ctx:
        rows = ctx.enter_context(nc.sbuf_tensor("y_rows", [P, PT + 1, D_MODEL], F32))
        block = ctx.enter_context(nc.Block())
        banks = [(t, q) for t in range(PT + 1) for q in range(2)]

        @block.tensor
        def _(pe):
            for i, (t, q) in enumerate(banks):
                m = P if t < PT else NS
                if i >= 8:
                    pe.wait_ge(T.dve_done.h, T.dve_done.done(i - 7))
                for k in range(4):
                    mm = pe.transpose(T.ps[0:m, i % 8, k * P:(k + 1) * P],
                                      T.x[:, 4 * q + k, t * P:t * P + m], T.ident[:, :])
                mm.then_inc(T.pe_done.h, 1)

        @block.vector
        def _(dve):
            for i, (t, q) in enumerate(banks):
                m = P if t < PT else NS
                dve.wait_ge(T.pe_done.h, T.pe_done.done(i + 1))
                dve.tensor_copy(rows[0:m, t, q * 512:(q + 1) * 512], T.ps[0:m, i % 8, 0:512])\
                   .then_inc(T.dve_done.h, 1)

        @block.sync
        def _(sp):
            for t in range(PT + 1):
                sp.wait_ge(T.dve_done.h, T.dve_done.done(2 * t + 2))
                if t < PT:
                    sp.dma_start(y_prompt[t * P:(t + 1) * P, :], rows[:, t]).then_inc(T.stored.h, 16)
                else:
                    sp.dma_start(y_sample, rows[0:NS, t]).then_inc(T.stored.h, 16)
            sp.wait_ge(T.stored.h, T.stored.done((PT + 1) * 16))
    T.pe_done.close(len(banks))
    T.dve_done.close(len(banks))
    T.stored.close((PT + 1) * 16)



SECTIONS = 7
Q_A, K_A, V_A, Q_B, K_B, V_B, G_B = range(SECTIONS)
ROPED = (Q_A, K_A, Q_B, K_B)
TT = PT + 1
KPP = 2
SECTION_PIECES = KT // KPP


def tile_cols(t):
    return slice(t * P, (t + 1) * P) if t < PT else slice(NT - P, NT)


def in_piece(w_in, g):
    s, q = divmod(g, SECTION_PIECES)
    return w_in.rearrange("(k p) c -> p k c", p=P)[:, q * KPP:(q + 1) * KPP, s * MIX:(s + 1) * MIX]


def open_mix(ctx, nc, M, part):
    def sb(name, shape, dt=F32):
        return ctx.enter_context(nc.sbuf_tensor(name, shape, dt))

    if part == "attention":
        M.qaT, M.kaT = sb("qaT", [P, PAIRS, NT]), sb("kaT", [P, PAIRS, NT])
        M.va = sb("va", [P, TT, MIX])
        M.pages = sb("pages", [1, DEC_BATCH * (PAST_LEN // PAGE)], I32)
        M.keep = sb("keep", [P, P])
        M.keep_s = sb("keep_s", [P, NS])
        M.select = sb("select", [P, DEC_BATCH])
        M.power = sb("power", [P, PAIRS])
        M.power_s = sb("power_s", [P, PAIRS])
    else:
        M.qbT, M.kbT = sb("qbT", [P, PAIRS, NT]), sb("kbT", [P, PAIRS, NT])
        M.kb, M.vb, M.gb = (sb(n, [P, TT, MIX]) for n in ("kb", "vb", "gb"))


def phase_project(T, M, w_in, rope_cos, rope_sin, decay_q, decay_k, table, masks, O, nxt):
    nc = T.nc
    U, before = T.pieces, T.norm_before
    NP = SECTIONS * SECTION_PIECES
    N = KPP * MIX
    staged, roped, turned, moved, k_stored, v_stored, tables = (
        Count(T.ctx, nc, n) for n in ("staged", "roped", "turned", "moved", "k_stored", "v_stored", "tables_loaded"))
    M.table_loaded, M.masks_loaded, M.states_loaded = (
        Count(T.ctx, nc, n) for n in ("table_loaded", "masks_loaded", "states_loaded"))
    M.MASKS = len(masks)
    with ExitStack() as ctx:
        def sb(name, shape, dt=F32):
            return ctx.enter_context(nc.sbuf_tensor(name, shape, dt))

        stage, rot = sb("stage", [P, TT, MIX]), sb("rot", [P, TT, MIX])
        by_cos, by_sin = sb("by_cos", [P, MIX]), sb("by_sin", [P, MIX])
        cos, sin = sb("cos", [P, TT, HD // 2]), sb("sin", [P, TT, 2, HD // 2])
        dq, dk = sb("dq", [P, TT, HEADS]), sb("dk", [P, TT, HEADS])
        block = ctx.enter_context(nc.Block())

        def bank(s, t):
            return (TT * s + t) % 6

        @block.sync
        def _(sp):
            sp.dma_start(cos[:, :, :], rope_cos).then_inc(tables.h, 16)
            sp.dma_start(sin[:, :, :, :], rope_sin).then_inc(tables.h, 16)
            sp.dma_start(dq[:, :, :], decay_q).then_inc(tables.h, 16)
            sp.dma_start(dk[:, :, :], decay_k).then_inc(tables.h, 16)
            sp.dma_start(M.pages[:, :], table.rearrange("b n -> (b n)").unsqueeze(0)).then_inc(M.table_loaded.h, 16)
            for dst, src in zip((M.keep, M.power, M.power_s), masks):
                sp.dma_start(dst[:, :], src).then_inc(M.masks_loaded.h, 16)
            for dst, src in zip((M.keep_s, M.select), masks[3:]):
                sp.dma_start(dst[NS:P, :], src).then_inc(M.masks_loaded.h, 16)
            for g in range(2, NP):
                load_piece(T, sp, g % 2, U + g // 2, in_piece(w_in, g))
            for slot in range(2):
                load_piece(T, sp, slot, U + NP // 2, nxt[slot])

        @block.tensor
        def _(pe):
            def turn(r):
                src = M.kb if ROPED[r] == K_B else rot
                for t in range(TT):
                    pe.wait_ge(roped.h, TT * r + t + 1)
                    if TT * r + t >= 2:
                        pe.wait_ge(moved.h, TT * r + t - 1)
                    for p in range(PAIRS):
                        lo = 0 if t < PT else NS
                        mm = pe.transpose(T.ps[:, 6 + t % 2, p * P:p * P + P - lo],
                                          src[lo:P, t, p * P:(p + 1) * P], T.ident[lo:P, lo:P])
                    mm.then_inc(turned.h, 1)

            before.tensor(pe)
            for g in range(NP):
                s, q = divmod(g, SECTION_PIECES)
                slot = g % 2
                if s == 0:
                    before.feature_ready(pe, KPP * q + KPP - 1)
                pe.wait_ge(T.w_split[slot].h, U + g // 2 + 2)
                for t in range(TT):
                    if q == 0 and TT * s + t >= 6:
                        pe.wait_ge(staged.h, TT * s + t - 5)
                    for k in range(KPP):
                        cols = slice(k * MIX, (k + 1) * MIX)
                        kk = q * KPP + k
                        x_hi, x_lo = T.x_hi[:, kk, tile_cols(t)], T.x_lo[:, kk, tile_cols(t)]
                        w_hi, w_lo = T.w_hi[:, slot, cols], T.w_lo[:, slot, cols]
                        out = T.ps[:, bank(s, t), 0:MIX]
                        pe.matmul(out, x_hi, w_hi, start=(kk == 0), stop=False)
                        pe.matmul(out, x_hi, w_lo, start=False, stop=False)
                        mm = pe.matmul(out, x_lo, w_hi, start=False, stop=(kk == KT - 1))
                mm.then_inc(T.w_used[slot].h, 1)
                if q == 2 and s - 1 in ROPED:
                    turn(ROPED.index(s - 1))

        @block.scalar
        def _(act):
            def empty(s):
                act.wait_ge(T.w_used[1].h, U + (4 * s + 3) // 2 + 2)
                dst = {V_A: M.va, V_B: M.vb, G_B: M.gb}.get(s, stage)
                for t in range(TT):
                    if s in ROPED and s > 0:
                        act.wait_ge(roped.h, TT * (ROPED.index(s) - 1) + t + 1)
                    act.activation(dst[:, t], T.ps[:, bank(s, t), 0:MIX], ACT.Silu if s == G_B else ACT.Copy)\
                       .then_inc(staged.h, 1)

            def move(r):
                dst = (M.qaT, M.kaT, M.qbT, M.kbT)[r]
                for t in range(TT):
                    m = P if t < PT else NS
                    act.wait_ge(turned.h, TT * r + t + 1)
                    act.activation(dst[:, :, t * P:t * P + m],
                                   T.ps[:, 6 + t % 2, :].rearrange("p (a t) -> p a t", a=PAIRS)[:, :, 0:m],
                                   ACT.Copy).then_inc(moved.h, 1)

            before.scalar(act)
            for g in range(NP):
                if 2 <= g + 1 < NP:
                    round_piece(T, act, (g + 1) % 2, U + (g + 1) // 2, N)
                s, q = divmod(g, SECTION_PIECES)
                if q == 2 and s - 1 in ROPED:
                    move(ROPED.index(s - 1))
                if q == 3:
                    empty(s)
            for slot in range(2):
                round_piece(T, act, slot, U + NP // 2, KT * P)

        @block.vector
        def _(dve):
            def rotate(s, t):
                r = ROPED.index(s)
                dve.wait_ge(staged.h, TT * s + t + 1)
                heads = stage[:, t].rearrange("p (h j d) -> p h j d", h=HEADS, j=2)
                sums = by_sin[:, :].rearrange("p (h j d) -> p h j d", h=HEADS, j=2)
                flat = [P, HEADS * 2, HD // 2]
                dve.tensor_tensor(by_cos[:, :].rearrange("p (h d) -> p h d", d=HD // 2),
                                  stage[:, t].rearrange("p (h d) -> p h d", d=HD // 2),
                                  cos[:, t:t + 1, :].to_broadcast(flat), ALU.mult)
                for j in range(2):
                    last = dve.tensor_tensor(sums[:, :, j], heads[:, :, 1 - j],
                                             sin[:, t, j:j + 1, :].to_broadcast([P, HEADS, HD // 2]), ALU.mult)
                T.dve_chain(dve, last)
                dst = M.kb if s == K_B else rot
                if r and dst is rot:
                    dve.wait_ge(turned.h, TT * (r - 1) + t + 1)
                    if s == Q_B:
                        dve.wait_ge(k_stored.h, 16 * TT)
                last = dve.tensor_tensor(dst[:, t], by_cos[:, :], by_sin[:, :], ALU.add)
                if s in (Q_B, K_B):
                    T.dve_chain(dve, last)
                    d = (dq if s == Q_B else dk)[:, t, :].unsqueeze(2).to_broadcast([P, HEADS, HD])
                    last = dve.tensor_tensor(dst[:, t].rearrange("p (h d) -> p h d", h=HEADS),
                                             dst[:, t].rearrange("p (h d) -> p h d", h=HEADS), d, ALU.mult)
                last.then_inc(roped.h, 1)
                dve.wait_ge(roped.h, TT * r + t + 1)

            before.vector(dve)
            dve.wait_ge(tables.h, 64)
            for g in range(NP):
                if 2 <= g + 1 < NP:
                    rest_piece(T, dve, (g + 1) % 2, U + (g + 1) // 2, N)
                s, q = divmod(g, SECTION_PIECES)
                if s - 1 in ROPED and q < 2:
                    for t in (0, 1) if q == 0 else (2, 3, 4):
                        rotate(s - 1, t)
            for slot in range(2):
                rest_piece(T, dve, slot, U + NP // 2, KT * P)

        @block.gpsimd
        def _(pool):
            before.gpsimd(pool)
            for stored, src, wait, of_prompt, of_sample in (
                    (k_stored, rot, lambda t: (roped.h, TT + t + 1), O["k_prompt"], O["k_sample"]),
                    (v_stored, M.va, lambda t: (staged.h, TT * V_A + t + 1), O["v_prompt"], O["v_sample"])):
                for t in range(TT):
                    pool.wait_ge(*wait(t))
                    if t < PT:
                        pool.dma_start(of_prompt[t * P:(t + 1) * P, :], src[:, t]).then_inc(stored.h, 16)
                    else:
                        pool.dma_start(of_sample, src[NS:P, t]).then_inc(stored.h, 16)
            pool.wait_ge(k_stored.h, TT * 16)
            pool.wait_ge(v_stored.h, TT * 16)
    T.pieces += NP // 2
    T.norm_before = None



def phase_attend_prompt(T, M, causal_in):
    nc = T.nc
    N = PT * HEADS
    scored, maxed, expd, turned, moved, valued, normed, oturned, rounded, rested, loaded = (
        Count(T.ctx, nc, "pa_" + n) for n in (
            "scored", "maxed", "expd", "turned", "moved", "valued", "normed", "oturned", "rounded", "rested",
            "loaded"))
    with ExitStack() as ctx:
        def sb(name, shape, dt=F32):
            return ctx.enter_context(nc.sbuf_tensor(name, shape, dt))

        prob, prob_t = sb("prob", [P, 3, SEQ]), sb("prob_t", [P, 2, SEQ])
        out = sb("attn_out", [P, 2, MIX])
        causal = sb("causal", [P, P])
        top, shift, total, inv = (sb(n, [P, N]) for n in ("top", "shift", "total", "inv"))
        block = ctx.enter_context(nc.Block())
        jobs = [(i, h) for i in range(PT) for h in range(HEADS)]
        half = [slice(0, HD), slice(HD, P)]

        @block.sync
        def _(sp):
            sp.dma_start(causal[:, :], causal_in).then_inc(loaded.h, 16)

        @block.tensor
        def _(pe):
            def score(n):
                i, h = jobs[n]
                if n >= 3:
                    pe.wait_ge(expd.h, n - 2)
                rows = half[h % 2]
                pe.matmul(T.ps[:, n % 3, 0:(i + 1) * P], M.qaT[rows, h // 2, i * P:(i + 1) * P],
                          M.kaT[rows, h // 2, 0:(i + 1) * P], start=True, stop=True).then_inc(scored.h, 1)

            def turn(n):
                i, h = jobs[n]
                pe.wait_ge(expd.h, n + 1)
                if n >= 2:
                    pe.wait_ge(moved.h, n - 1)
                for j in range(i + 1):
                    mm = pe.transpose(T.ps[:, 3 + n % 2, j * P:(j + 1) * P], prob[:, n % 3, j * P:(j + 1) * P],
                                      T.ident[:, :])
                mm.then_inc(turned.h, 1)

            def value(n):
                i, h = jobs[n]
                pe.wait_ge(moved.h, n + 1)
                if h == 0 and i >= 2:
                    pe.wait_ge(normed.h, i - 1)
                for j in range(i + 1):
                    mm = pe.matmul(T.ps[:, 5 + i % 2, h * HD:(h + 1) * HD], prob_t[:, n % 2, j * P:(j + 1) * P],
                                   M.va[:, j, h * HD:(h + 1) * HD], start=(h == 0 and j == 0),
                                   stop=(h == HEADS - 1 and j == i), skip_group_check=True)
                mm.then_inc(valued.h, 1)

            def turn_out(i):
                pe.wait_ge(normed.h, i + 1)
                if i >= 1:
                    pe.wait_ge(rested.h, i)
                for p in range(PAIRS):
                    mm = pe.transpose(T.ps[:, 7, p * P:(p + 1) * P], out[:, i % 2, p * P:(p + 1) * P],
                                      T.ident[:, :])
                mm.then_inc(oturned.h, 1)

            for n in range(N + 3):
                if n < N:
                    score(n)
                if 2 <= n <= N + 1:
                    turn(n - 2)
                if n >= 3:
                    value(n - 3)
                if n >= HEADS + 5 and (n - 5) % HEADS == 0:
                    turn_out((n - 5) // HEADS - 1)
            turn_out(PT - 1)

        @block.vector
        def _(dve):
            dve.wait_ge(loaded.h, 16)

            def rest(i):
                dve.wait_ge(rounded.h, i + 1)
                cols = slice(i * P, (i + 1) * P)
                dve.tensor_tensor(T.x_lo[:, 0:PAIRS, cols],
                                  T.ps[:, 7, :].rearrange("p (a t) -> p a t", a=PAIRS),
                                  T.x_hi[:, 0:PAIRS, cols].bitcast(F32), ALU.subtract).then_inc(rested.h, 1)

            def norm(i):
                dve.wait_ge(valued.h, HEADS * (i + 1))
                cols = slice(HEADS * i, HEADS * (i + 1))
                T.dve_chain(dve, dve.reciprocal(inv[:, cols], total[:, cols]))
                if i >= 2:
                    dve.wait_ge(oturned.h, i - 1)
                dve.tensor_tensor(out[:, i % 2].rearrange("p (h d) -> p h d", h=HEADS),
                                  T.ps[:, 5 + i % 2, :].rearrange("p (h d) -> p h d", h=HEADS),
                                  inv[:, cols].unsqueeze(2).to_broadcast([P, HEADS, HD]), ALU.mult)\
                   .then_inc(normed.h, 1)

            for n in range(N):
                i, h = jobs[n]
                dve.wait_ge(scored.h, n + 1)
                diag = T.ps[:, n % 3, i * P:(i + 1) * P]
                T.dve_chain(dve, dve.tensor_tensor(diag, diag, causal[:, :], ALU.add))
                T.dve_chain(dve, dve.reduce_max(top[:, n:n + 1], T.ps[:, n % 3, 0:(i + 1) * P], AX_X))
                dve.tensor_scalar(shift[:, n:n + 1], top[:, n:n + 1], -HD ** -0.5, None, ALU.mult)\
                   .then_inc(maxed.h, 1)
                if i and h == 3:
                    norm(i - 1)
                if i and h == 6:
                    rest(i - 1)
            norm(PT - 1)
            rest(PT - 1)

        @block.scalar
        def _(act):
            def move(n):
                i, h = jobs[n]
                act.wait_ge(turned.h, n + 1)
                if n >= 2:
                    act.wait_ge(valued.h, n - 1)
                act.activation(prob_t[:, n % 2, 0:(i + 1) * P], T.ps[:, 3 + n % 2, 0:(i + 1) * P], ACT.Copy)\
                   .then_inc(moved.h, 1)

            def round_out(i):
                act.wait_ge(oturned.h, i + 1)
                act.activation(T.x_hi[:, 0:PAIRS, i * P:(i + 1) * P],
                               T.ps[:, 7, :].rearrange("p (a t) -> p a t", a=PAIRS), ACT.Copy)\
                   .then_inc(rounded.h, 1)

            for n in range(N):
                i, h = jobs[n]
                act.wait_ge(maxed.h, n + 1)
                if n >= 3:
                    act.wait_ge(turned.h, n - 2)
                act.activation(prob[:, n % 3, 0:(i + 1) * P], T.ps[:, n % 3, 0:(i + 1) * P], ACT.Exp,
                               bias=shift[:, n:n + 1], scale=HD ** -0.5, accum_out=total[:, n:n + 1])\
                   .then_inc(expd.h, 1)
                if n >= 2:
                    move(n - 2)
                if i and h == 5:
                    round_out(i - 1)
            move(N - 2)
            move(N - 1)
            round_out(PT - 1)



class GroupNorm:

    def __init__(self, T, M, ctx, name):
        def sb(part, shape):
            return ctx.enter_context(T.nc.sbuf_tensor(name + part, shape, F32))

        self.T, self.M = T, M
        self.ready, self.rooted, self.gated, self.turned, self.rounded, self.rested = (
            Count(T.ctx, T.nc, name + n) for n in ("ready", "rooted", "gated", "turned", "rounded", "rested"))
        free, more = (buf[:, :, :].rearrange("p a t -> p (a t)") for buf in (T.gate, T.prod))
        self.centred, self.squares, self.gate = free[:, 0:MIX], free[:, MIX:2 * MIX], more[:, 0:MIX]
        self.mean, self.var = sb("mean", [P, HEADS]), sb("var", [P, HEADS])

    def vector(self, dve, n, ps, t):
        T, M = self.T, self.M
        r = slice(0 if t < PT else NS, P)
        rows = P - r.start
        wide = [rows, HEADS, HD]

        def heads(ap):
            return ap.rearrange("p (h d) -> p h d", h=HEADS)

        def each(ap):
            return ap.unsqueeze(2).to_broadcast(wide)

        mean, var, centred, squares = self.mean[r, :], self.var[r, :], self.centred[r, :], self.squares[r, :]
        T.dve_chain(dve, dve.tensor_reduce(mean, heads(ps[r, :]), AX_X, ALU.add))
        T.dve_chain(dve, dve.tensor_scalar(mean, mean, -1.0 / HD, None, ALU.mult))
        T.dve_chain(dve, dve.tensor_tensor(heads(centred), heads(ps[r, :]), each(mean), ALU.add))
        T.dve_chain(dve, dve.tensor_tensor(squares, centred, centred, ALU.mult))
        T.dve_chain(dve, dve.tensor_reduce(var, heads(squares), AX_X, ALU.add))
        dve.tensor_scalar(var, var, 1.0 / HD, GN_EPS, ALU.mult, ALU.add).then_inc(self.ready.h, 1)
        dve.wait_ge(self.rooted.h, n + 1)
        T.dve_chain(dve, dve.reciprocal(var, var))
        T.dve_chain(dve, dve.tensor_tensor(heads(centred), heads(centred), each(var), ALU.mult))
        if n >= 1:
            dve.wait_ge(self.turned.h, n)
        dve.tensor_tensor(self.gate[r, :], centred, M.gb[r, t], ALU.mult).then_inc(self.gated.h, 1)

    def rest(self, dve, n, t):
        T = self.T
        m = P if t < PT else NS
        dve.wait_ge(self.rounded.h, n + 1)
        cols = slice(t * P, t * P + m)
        dve.tensor_tensor(T.x_lo[:, PAIRS:KT, cols],
                          T.ps[:, 6 + n % 2, :].rearrange("p (a t) -> p a t", a=PAIRS)[:, :, 0:m],
                          T.x_hi[:, PAIRS:KT, cols].bitcast(F32), ALU.subtract).then_inc(self.rested.h, 1)

    def scalar(self, act, n, t):
        T = self.T
        r = slice(0 if t < PT else NS, P)
        act.wait_ge(self.ready.h, n + 1)
        act.activation(self.var[r, :], self.var[r, :], ACT.Sqrt).then_inc(self.rooted.h, 1)

    def round(self, act, n, t):
        T = self.T
        m = P if t < PT else NS
        act.wait_ge(self.turned.h, n + 1)
        act.activation(T.x_hi[:, PAIRS:KT, t * P:t * P + m],
                       T.ps[:, 6 + n % 2, :].rearrange("p (a t) -> p a t", a=PAIRS)[:, :, 0:m], ACT.Copy)\
           .then_inc(self.rounded.h, 1)

    def tensor(self, pe, n, t):
        T = self.T
        lo = 0 if t < PT else NS
        pe.wait_ge(self.gated.h, n + 1)
        if n >= 2:
            pe.wait_ge(self.rested.h, n - 1)
        for p in range(PAIRS):
            mm = pe.transpose(T.ps[:, 6 + n % 2, p * P:p * P + P - lo], self.gate[lo:P, p * P:(p + 1) * P],
                              T.ident[lo:P, lo:P])
        mm.then_inc(self.turned.h, 1)


def phase_retain_prompt(T, M, state_out, samples_in):
    nc = T.nc
    inner, masked, kept, copied, outed, stored = (
        Count(T.ctx, nc, "rp_" + n) for n in ("inner", "masked", "kept", "copied", "outed", "stored"))
    with ExitStack() as ctx:
        def sb(name, shape, dt=F32):
            return ctx.enter_context(nc.sbuf_tensor(name, shape, dt))

        keep, power = M.keep, M.power
        weight = sb("weight", [P, 2, 2, HEADS // 2, P])
        state = sb("state", [P, PAIRS, P])
        final = sb("final", [P, PAIRS, HD])
        gn = GroupNorm(T, M, ctx, "rp_gn_")
        block = ctx.enter_context(nc.Block())
        half = [slice(0, HD), slice(HD, P)]
        sums = T.ps[:, 4, :].rearrange("p (a e) -> p a e", a=PAIRS)

        @block.sync
        def _(sp):
            for s in range(2):
                sp.dma_start(M.states[half[s], :, half[s]],
                             samples_in.rearrange("b (a s) d e -> s d (b a) e", s=2)[s]).then_inc(M.states_loaded.h, 16)
            sp.wait_ge(copied.h, PT + 1)
            for s in range(2):
                sp.dma_start(state_out.rearrange("(a s) d e -> s d a e", s=2)[s], final[half[s], :, :])\
                  .then_inc(stored.h, 16)
            sp.wait_ge(stored.h, 32)

        @block.tensor
        def _(pe):
            def inner_products(i):
                cols = slice(i * P, (i + 1) * P)
                for g in range(2):
                    if i:
                        pe.wait_ge(masked.h, 2 * i + g - 1)
                    for j in range(HEADS // 2):
                        h = 2 * j + g
                        rows = half[g]
                        mm = pe.matmul(T.ps[:, g, j * P:(j + 1) * P], M.kbT[rows, h // 2, cols],
                                       M.qbT[rows, h // 2, cols], start=True, stop=True)
                    mm.then_inc(inner.h, 1)

            inner_products(0)
            for i in range(PT):
                cols = slice(i * P, (i + 1) * P)
                if i >= 2:
                    pe.wait_ge(gn.gated.h, i - 1)
                out = T.ps[:, 2 + i % 2, :]
                if i:
                    pe.wait_ge(copied.h, i + 1)
                    for p in range(PAIRS):
                        pe.matmul(out[:, p * P:(p + 1) * P], M.qbT[:, p, cols], state[:, p, :],
                                  start=(p == 0), stop=False, skip_group_check=True)
                pe.wait_ge(masked.h, 2 * i + 2)
                for h in range(HEADS):
                    mm = pe.matmul(out[:, h * HD:(h + 1) * HD], weight[:, i % 2, h % 2, h // 2, :],
                                   M.vb[:, i, h * HD:(h + 1) * HD], start=(i == 0 and h == 0),
                                   stop=(h == HEADS - 1), skip_group_check=True)
                mm.then_inc(outed.h, 1)
                for p in range(PAIRS):
                    mm = pe.matmul(sums[:, p, :], M.kb[:, i, p * P:(p + 1) * P], M.vb[:, i, p * P:(p + 1) * P],
                                   start=(i == 0 and p == 0), stop=(i == PT - 1 and p == PAIRS - 1),
                                   skip_group_check=True)
                mm.then_inc(kept.h, 1)
                if i + 1 < PT:
                    inner_products(i + 1)
                if i:
                    gn.tensor(pe, i - 1, i - 1)
            gn.tensor(pe, PT - 1, PT - 1)

        @block.vector
        def _(dve):
            dve.memset(state[:, :, :], 0.0).then_inc(copied.h, 1)
            dve.wait_ge(copied.h, 1)
            dve.wait_ge(M.masks_loaded.h, M.MASKS * 16)
            for i in range(PT + 1):
                if i < PT:
                    for g in range(2):
                        dve.wait_ge(inner.h, 2 * i + g + 1)
                        if i >= 2:
                            dve.wait_ge(outed.h, i - 1)
                        dve.tensor_tensor(weight[:, i % 2, g],
                                          T.ps[:, g, :].rearrange("p (h t) -> p h t", h=HEADS // 2),
                                          keep[:, :].unsqueeze(1).to_broadcast([P, HEADS // 2, P]), ALU.mult)\
                           .then_inc(masked.h, 1)
                if i:
                    gn.vector(dve, i - 1, T.ps[:, 2 + (i - 1) % 2, :], i - 1)
                if i < PT:
                    dve.wait_ge(kept.h, i + 1)
                    for s in range(2):
                        if i < PT - 1:
                            last = dve.tensor_copy(state[half[s], :, half[s]], sums[half[s], :, half[s]])
                        else:
                            last = dve.tensor_tensor(final[half[s], :, :], sums[half[s], :, half[s]],
                                                     power[half[s], :].unsqueeze(2).to_broadcast([HD, PAIRS, HD]),
                                                     ALU.mult)
                    last.then_inc(copied.h, 1)
                if i >= 2:
                    gn.rest(dve, i - 2, i - 2)
            gn.rest(dve, PT - 1, PT - 1)

        @block.scalar
        def _(act):
            for i in range(PT):
                gn.scalar(act, i, i)
                if i:
                    gn.round(act, i - 1, i - 1)
            gn.round(act, PT - 1, PT - 1)

        @block.gpsimd
        def _(pool):
            for s in range(2):
                pool.memset(M.states[half[s], :, half[1 - s]], 0.0).then_inc(T.pool_done.h, 1)


def phase_retain_samples(T, M, state_out):
    nc = T.nc
    B = DEC_BATCH
    names = ("zeroed", "spread", "inner", "masked", "outed", "picked", "updated", "added", "stored")
    zeroed, spread, inner, masked, outed, picked, updated, added, stored = (
        Count(T.ctx, nc, "rs_" + n) for n in names)
    with ExitStack() as ctx:
        def sb(name, shape, dt=F32):
            return ctx.enter_context(nc.sbuf_tensor(name, shape, dt))

        keep, select, power, state = M.keep_s, M.select, M.power_s, M.states
        q_of = sb("q_of", [P, PAIRS, B, NS])
        weight = sb("weight_s", [P, 2, PAIRS, NS])
        v_of = [sb("v_of", [P, MIX]), T.prod[:, :, :].rearrange("p a t -> p (a t)")[:, MIX:2 * MIX]]
        gn = GroupNorm(T, M, ctx, "rs_gn_")
        block = ctx.enter_context(nc.Block())
        half = [slice(0, HD), slice(HD, P)]
        tok = slice(NS, P)

        @block.sync
        def _(sp):
            for b in range(0, B, 2):
                sp.wait_ge(added.h, b + 2)
                mine = slice(PAIRS * b, PAIRS * (b + 2))
                for s in range(2):
                    sp.dma_start(state_out.rearrange("b (a s) d e -> s d (b a) e", s=2)[s][:, mine],
                                 state[half[s], mine, half[s]]).then_inc(stored.h, 16)
            sp.wait_ge(stored.h, B * 16)

        @block.tensor
        def _(pe):
            for h in range(HEADS):
                rows = half[h % 2]
                mm = pe.matmul(T.ps[tok, (0, 4)[h % 2], h // 2 * NS:(h // 2 + 1) * NS], M.kbT[rows, h // 2, SEQ:NT],
                               M.qbT[rows, h // 2, SEQ:NT], start=True, stop=True)
            mm.then_inc(inner.h, 1)
            pe.wait_ge(spread.h, B)
            pe.wait_ge(M.states_loaded.h, 32)
            for p in range(PAIRS):
                for b in range(B):
                    pe.matmul(T.ps[tok, 1, p * P:(p + 1) * P], q_of[:, p, b, :], state[:, PAIRS * b + p, :],
                              start=(p == 0 and b == 0), stop=False, skip_group_check=True)
            pe.wait_ge(masked.h, 1)
            for h in range(HEADS):
                mm = pe.matmul(T.ps[tok, 1, h * HD:(h + 1) * HD], weight[tok, h % 2, h // 2, :],
                               M.vb[tok, PT, h * HD:(h + 1) * HD], start=False, stop=(h == HEADS - 1),
                               skip_group_check=True)
            mm.then_inc(outed.h, 1)
            for b in range(B):
                pe.wait_ge(picked.h, b + 1)
                if b >= 2:
                    pe.wait_ge(added.h, b - 1)
                for p in range(PAIRS):
                    mm = pe.matmul(T.ps[:, 2 + b % 2, p * P:(p + 1) * P], M.kb[tok, PT, p * P:(p + 1) * P],
                                   v_of[b % 2][tok, p * P:(p + 1) * P], start=True, stop=True)
                mm.then_inc(updated.h, 1)
                if b == 2:
                    gn.tensor(pe, 0, PT)

        @block.vector
        def _(dve):
            dve.memset(q_of[:, :, :, :], 0.0).then_inc(zeroed.h, 1)
            dve.wait_ge(zeroed.h, 1)
            for b in range(B):
                cols = slice(b * DEC_SEQ, (b + 1) * DEC_SEQ)
                dve.tensor_copy(q_of[:, :, b, cols], M.qbT[:, :, SEQ + cols.start:SEQ + cols.stop])\
                   .then_inc(spread.h, 1)
            dve.wait_ge(inner.h, 1)
            for s in range(2):
                last = dve.tensor_tensor(weight[tok, s], T.ps[tok, (0, 4)[s], 0:PAIRS * NS]
                                         .rearrange("p (a t) -> p a t", a=PAIRS),
                                         keep[tok, :].unsqueeze(1).to_broadcast([NS, PAIRS, NS]), ALU.mult)
            last.then_inc(masked.h, 1)

            def pick(b):
                if b >= 2:
                    dve.wait_ge(updated.h, b - 1)
                dve.tensor_scalar(v_of[b % 2][tok, :], M.vb[tok, PT, :], select[tok, b:b + 1], None, ALU.mult)\
                   .then_inc(picked.h, 1)

            pick(0)
            pick(1)
            dve.wait_ge(outed.h, 1)
            gn.vector(dve, 0, T.ps[:, 1, :], PT)
            for b in range(B):
                if 2 <= b + 1 < B:
                    pick(b + 1)
                dve.wait_ge(updated.h, b + 1)
                ps = T.ps[:, 2 + b % 2, :].rearrange("p (a e) -> p a e", a=PAIRS)
                mine = slice(PAIRS * b, PAIRS * (b + 1))
                for s in range(2):
                    at = state[half[s], mine, half[s]]
                    T.dve_chain(dve, dve.tensor_tensor(at, at, ps[half[s], :, half[s]], ALU.add))
                    last = dve.tensor_tensor(at, at, power[half[s], :].unsqueeze(2).to_broadcast([HD, PAIRS, HD]),
                                             ALU.mult)
                last.then_inc(added.h, 1)
            gn.rest(dve, 0, PT)

        @block.scalar
        def _(act):
            gn.scalar(act, 0, PT)
            gn.round(act, 0, PT)



BP = DEC_BATCH // 2
PAGES = PAST_LEN // PAGE
BLOCKS = PAST_LEN // 256
GP = PAGES // 2


def linker(eng, sem, base):
    made = [0]

    def link(ins):
        made[0] += 1
        ins.then_inc(sem.h, 1)
        eng.wait_ge(sem.h, base + made[0])
    return link


def phase_attend_samples(T, M, k_pool, v_pool, past_mask, block_no, n_pool):
    nc = T.nc
    k_pages = k_pool.rearrange("n t h d -> n t (h d)")
    v_pages = v_pool.rearrange("n t h d -> n t (h d)")
    SOFT, NORM = 12, 2

    def count(name):
        return Count(T.ctx, nc, "sa_" + name)

    k_loaded = [count(f"k_loaded{i}") for i in range(2)]
    k_turned, k_moved = ([count(n + str(i)) for i in range(2)] for n in ("k_turned", "k_moved"))
    v_loaded, v_used = ([count(n + str(i)) for i in range(4)] for n in ("v_loaded", "v_used"))
    loaded, zeroed, q_ready, scored, shifted, expd, normed = map(
        count, ("loaded", "zeroed", "q_ready", "scored", "shifted", "expd", "normed"))
    p_turned, p_moved0, p_moved1, valued, out_copied, out_turned, rounded, rested, soft_link, norm_link = map(
        count, ("p_turned", "p_moved0", "p_moved1", "valued", "out_copied", "out_turned", "rounded", "rested",
                "soft_link", "norm_link"))
    with ExitStack() as ctx:
        def sb(name, shape, dt=F32):
            return ctx.enter_context(nc.sbuf_tensor(name, shape, dt))

        k_ring = sb("k_ring", [P, PAGES, MIX])
        v_ring = sb("v_ring", [P, 2 * PAGES, MIX])
        keys = sb("keys", [P, PAIRS, PAST_LEN])
        q_of = sb("q_of_s", [P, 2, PAIRS * (HD + 16)])
        prob = T.gate[:, :, :].rearrange("p a t -> p (a t)")[:, 0:PAST_LEN + NS]
        prob_t = T.prod[:, :, :].rearrange("p a t -> p (a t)").rearrange("p (j t) -> p j t", t=P)
        out = sb("out_s", [P, MIX])
        mask, new = sb("mask_s", [P, BP, NS]), sb("new_s", [P, NS])
        pages = M.pages
        number = sb("number", [P, BLOCKS])
        gate, worst, same, last_same = sb("gate_s", [P, BLOCKS]), sb("worst", [P, 1]), sb("same", [P, BLOCKS]), sb("last_same", [P, 1])
        out_of, block_top, top = sb("out_of", [P, BLOCKS]), sb("block_top", [P, BLOCKS + 1]), sb("top_s", [P, 1])
        shift, totals, total = sb("shift_s", [P, BLOCKS + 1]), sb("totals_s", [P, BLOCKS + 1]), sb("total_s", [P, 1])
        credit = sb("credit_s", [P, 7])
        block = ctx.enter_context(nc.Block())
        half = [slice(0, HD), slice(HD, P)]
        past = T.ps[:, 0:2, :].rearrange("p b (c t) -> p (b c) t", c=2)
        tok = slice(NS, P)

        def load(q, pool, ring, at0, arrived, bp, b2, g, free, value):
            srcs = []
            for i in range(GP):
                at = bp * (2 * PAGES) + (b2 * PAGES + g * GP + i)
                page = q.value_load(pages[0:1, bass.ds(at, 1)], min_val=0, max_val=n_pool - 1)
                srcs.append(pool[bass.ds(page, 1)].rearrange("a t c -> (a t) c"))
            if free is not None:
                q.wait_ge(free.h, value)
            for i in range(GP):
                q.dma_start(ring[:, at0 + i], srcs[i]).then_inc(arrived.h, 16)

        @block.sync
        def _(sp):
            def load_k(bp, b2, free_value):
                for g in range(2):
                    load(sp, k_pages, k_ring, GP * g, k_loaded[g], bp, b2, g, k_turned[1 - b2],
                         free_value + GP * (g + 1))

            sp.dma_start(number[:, :], block_no).then_inc(loaded.h, 16)
            sp.dma_start(mask[:, :, :], past_mask).then_inc(loaded.h, 16)
            sp.wait_ge(M.table_loaded.h, 16)
            for g in range(2):
                load(sp, k_pages, k_ring, GP * g, k_loaded[g], 0, 0, g, None, 0)
            load_k(0, 1, 0)
            with sp.Fori(0, BP - 1) as bp:
                load_k(bp + 1, 0, bp * PAGES)
                load_k(bp + 1, 1, bp * PAGES + PAGES)

        @block.gpsimd
        def _(pool):
            pool.wait_ge(M.table_loaded.h, 16)
            with pool.Fori(0, BP) as bp:
                for b2 in range(2):
                    for g in range(2):
                        part = 2 * b2 + g
                        load(pool, v_pages, v_ring, GP * part, v_loaded[part], bp, b2, g, v_used[part], bp + 1)

        @block.tensor
        def _(pe):
            def turn_keys(bp, b2):
                for j in range(PAGES):
                    if j % GP == 0:
                        pe.wait_ge(k_loaded[j // GP].h, bp * 128 + (64 * b2 + 64))
                    if j >= 2:
                        pe.wait_ge(k_moved[b2].h, bp * PAGES + (j - 1))
                    for p in range(PAIRS):
                        mm = pe.transpose(T.ps[:, 3 + j % 2, p * P:(p + 1) * P], k_ring[:, j, p * P:(p + 1) * P],
                                          T.ident[:, :])
                    mm.then_inc(k_turned[b2].h, 1)

            def score(bp, b2, first=False):
                pe.wait_ge(k_moved[b2].h, bp * PAGES + PAGES)
                pe.wait_ge(q_ready.h, bp + 1)
                if b2 == 0 and not first:
                    pe.wait_ge(expd.h, bp)
                rows = half[b2]
                for n in range(3):
                    for p in range(PAIRS):
                        src = keys[:, p, n * 512:(n + 1) * 512] if n < 2 else M.kaT[:, p, SEQ:NT]
                        mm = pe.matmul(T.ps[rows, n, 0:src.shape[1]], q_of[:, b2, p * HD:(p + 1) * HD], src,
                                       start=(p == 0), stop=(p == PAIRS - 1))
                mm.then_inc(scored.h, 1)

            def values(bp):
                pe.wait_ge(rested.h, bp + 1)
                pe.wait_ge(normed.h, bp + 1)
                for g in range(2):
                    for i in range(GP):
                        j = GP * g + i
                        mm = pe.transpose(T.ps[:, 5 + g, i * P:(i + 1) * P], prob[:, j * P:(j + 1) * P], T.ident[:, :])
                    mm.then_inc(p_turned.h, 1)
                pe.transpose(T.ps[0:NS, 2, P:2 * P], prob[:, PAST_LEN:PAST_LEN + NS], T.ident[:, :])\
                  .then_inc(p_turned.h, 1)
                pe.wait_ge(p_moved0.h, bp * 2 + 2)
                pe.wait_ge(p_moved1.h, bp + 1)
                for b2 in range(2):
                    rows = half[b2]
                    for j in range(PAGES):
                        part = 2 * b2 + j // GP
                        if j % GP == 0:
                            pe.wait_ge(v_loaded[part].h, bp * 64 + 64)
                        mm = pe.matmul(T.ps[rows, 7, :], prob_t[:, j, rows], v_ring[:, PAGES * b2 + j, :],
                                       start=(j == 0), stop=False, skip_group_check=True)
                        if j % GP == GP - 1:
                            mm.then_inc(v_used[part].h, 1)
                for b2 in range(2):
                    rows = half[b2]
                    mm = pe.matmul(T.ps[rows, 7, :], prob_t[tok, PAGES, rows], M.va[tok, PT, :],
                                   start=False, stop=True, skip_group_check=True)
                mm.then_inc(valued.h, 1)

            def turn_outputs(bp):
                pe.wait_ge(out_copied.h, bp + 1)
                for p in range(PAIRS):
                    mm = pe.transpose(T.ps[:, 5, p * P:(p + 1) * P], out[:, p * P:(p + 1) * P], T.ident[:, :])
                mm.then_inc(out_turned.h, 1)

            turn_keys(0, 0)
            score(0, 0, True)
            turn_keys(0, 1)
            score(0, 1)
            with pe.Fori(0, BP - 1) as bp:
                turn_keys(bp + 1, 0)
                score(bp + 1, 0)
                values(bp)
                turn_keys(bp + 1, 1)
                turn_outputs(bp)
                score(bp + 1, 1)
            values(BP - 1)
            turn_outputs(BP - 1)

        def move_keys(eng, copy, bp, b2, scores, first=False):
            if not first:
                eng.wait_ge(scored.h, scores)
            for j in range(PAGES):
                eng.wait_ge(k_turned[b2].h, bp * PAGES + (j + 1))
                copy(keys[:, :, j * P:(j + 1) * P], T.ps[:, 3 + j % 2, :].rearrange("p (a t) -> p a t", a=PAIRS))\
                    .then_inc(k_moved[b2].h, 1)

        def outputs(s, bp, buf):
            cols = bass.ds(bp * (2 * DEC_SEQ) + SEQ, 2 * DEC_SEQ)
            for p in range(PAIRS):
                at = p * 2 * DEC_SEQ + s * DEC_SEQ
                yield (buf[half[s], p, cols].rearrange("p (b q) -> p b q", b=2),
                       T.ps[half[s], 5, p * P:(p + 1) * P]
                       .rearrange("p (b c) -> p b c", b=2)[:, :, at:at + DEC_SEQ])

        @block.vector
        def _(dve):
            def spread_q(bp):
                for s in range(2):
                    dst = q_of[half[s], :, :].rearrange("p b (a c) -> p b a c", a=PAIRS)[:, :, :, s * 8:(s + 1) * 8]
                    src = M.qaT[half[s], :, bass.ds(bp * (2 * DEC_SEQ) + SEQ, 2 * DEC_SEQ)]\
                        .rearrange("p a (b q) -> p b a q", b=2)
                    for b2 in range(2):
                        last = dve.tensor_copy(dst[:, b2], src[:, b2])
                last.then_inc(q_ready.h, 1)

            def soft(bp):
                dve.wait_ge(scored.h, bp * 2 + 2)
                link = linker(dve, soft_link, bp * SOFT)
                dve.tensor_reduce(gate[:, :], past, AX_X, ALU.add)
                dve.tensor_reduce(block_top[:, 0:BLOCKS], past, AX_X, ALU.max)
                link(dve.tensor_tensor(new[:, :], T.ps[:, 2, 0:NS],
                                       mask[:, bass.ds(bp, 1), :].rearrange("p a t -> p (a t)"), ALU.add))
                link(dve.reduce_max(block_top[:, BLOCKS:BLOCKS + 1], new[:, :], AX_X))
                link(dve.tensor_reduce(worst[:, :], gate[:, :], AX_X, ALU.min))
                link(dve.tensor_scalar(same[:, :], gate[:, :], worst[:, 0:1], None, ALU.is_equal))
                link(dve.tensor_tensor(same[:, :], same[:, :], number[:, :], ALU.mult))
                link(dve.reduce_max(last_same[:, :], same[:, :], AX_X))
                link(dve.tensor_scalar(out_of[:, :], number[:, :], last_same[:, 0:1], NEG, ALU.is_equal, ALU.mult))
                link(dve.tensor_tensor(block_top[:, 0:BLOCKS], block_top[:, 0:BLOCKS], out_of[:, :], ALU.add))
                link(dve.reduce_max(top[:, :], block_top[:, :], AX_X))
                link(dve.tensor_scalar(shift[:, BLOCKS:BLOCKS + 1], top[:, :], -HD ** -0.5, None, ALU.mult))
                link(dve.tensor_scalar(shift[:, 0:BLOCKS], out_of[:, :], shift[:, BLOCKS:BLOCKS + 1], None, ALU.add))
                link(dve.memset(credit[:, 6:7], 0.0))
                dve.memset(credit[:, 5:6], 0.0).then_inc(shifted.h, 1)

            def norm(bp):
                dve.wait_ge(expd.h, bp + 1)
                link = linker(dve, norm_link, bp * NORM)
                link(dve.tensor_reduce(total[:, :], totals[:, :], AX_X, ALU.add))
                link(dve.reciprocal(total[:, :], total[:, :]))
                dve.tensor_scalar(prob[:, :], prob[:, :], total[:, 0:1], None, ALU.mult).then_inc(normed.h, 1)

            def move_prob(bp):
                dve.wait_ge(p_turned.h, bp * 3 + 2)
                dve.tensor_copy(prob_t[:, GP:PAGES, :], T.ps[:, 6, :].rearrange("p (j t) -> p j t", j=GP))\
                   .then_inc(p_moved1.h, 1)

            def copy_out(bp):
                dve.wait_ge(valued.h, bp + 1)
                dve.tensor_copy(out[:, :], T.ps[:, 7, :]).then_inc(out_copied.h, 1)

            def rest(bp):
                dve.wait_ge(rounded.h, bp + 1)
                for s in range(2):
                    for (hi, ps), (lo, _) in zip(outputs(s, bp, T.x_hi), outputs(s, bp, T.x_lo)):
                        last = dve.tensor_tensor(lo, ps, hi.bitcast(F32), ALU.subtract)
                last.then_inc(rested.h, 1)

            for i, c in enumerate((*v_used, rested)):
                dve.memset(credit[:, i:i + 1], 0.0).then_inc(c.h, 1)
            dve.memset(q_of[:, :, :], 0.0).then_inc(zeroed.h, 1)
            dve.wait_ge(zeroed.h, 1)
            spread_q(0)
            move_keys(dve, dve.tensor_copy, 0, 1, 1)
            dve.wait_ge(loaded.h, 32)
            with dve.Fori(0, BP - 1) as bp:
                soft(bp)
                spread_q(bp + 1)
                norm(bp)
                move_prob(bp)
                copy_out(bp)
                move_keys(dve, dve.tensor_copy, bp + 1, 1, bp * 2 + 3)
                rest(bp)
            soft(BP - 1)
            norm(BP - 1)
            move_prob(BP - 1)
            copy_out(BP - 1)
            rest(BP - 1)

        @block.scalar
        def _(act):
            def copy(out, src):
                return act.activation(out, src, ACT.Copy)

            def exps(bp):
                act.wait_ge(shifted.h, bp + 1)
                for c in range(BLOCKS):
                    act.activation(prob[:, c * 256:(c + 1) * 256], past[:, c], ACT.Exp, bias=shift[:, c:c + 1],
                                   scale=HD ** -0.5, accum_out=totals[:, c:c + 1])
                act.activation(prob[:, PAST_LEN:PAST_LEN + NS], new[:, :], ACT.Exp, bias=shift[:, BLOCKS:BLOCKS + 1],
                               scale=HD ** -0.5, accum_out=totals[:, BLOCKS:BLOCKS + 1]).then_inc(expd.h, 1)

            def finish(bp):
                act.wait_ge(p_turned.h, bp * 3 + 1)
                act.activation(prob_t[:, 0:GP, :], T.ps[:, 5, :].rearrange("p (j t) -> p j t", j=GP), ACT.Copy)\
                   .then_inc(p_moved0.h, 1)
                act.wait_ge(p_turned.h, bp * 3 + 3)
                act.activation(prob_t[tok, PAGES, :], T.ps[0:NS, 2, P:2 * P], ACT.Copy).then_inc(p_moved0.h, 1)
                act.wait_ge(out_turned.h, bp + 1)
                for s in range(2):
                    for hi, ps in outputs(s, bp, T.x_hi):
                        last = act.activation(hi, ps, ACT.Copy)
                last.then_inc(rounded.h, 1)

            move_keys(act, copy, 0, 0, 0, True)
            with act.Fori(0, BP - 1) as bp:
                move_keys(act, copy, bp + 1, 0, bp * 2 + 2)
                exps(bp)
                finish(bp)
            exps(BP - 1)
            finish(BP - 1)



def out_piece(w, d):
    return w.rearrange("(k p) d -> p k d", p=P)[:, :, bass.ds(d * P, P)]


def phase_out(T, w_out, w_gate, row, nxt):
    nc = T.nc
    U = T.pieces
    G = KT * P
    gated = w_gate is not None
    used = KT if gated else KT // 2
    res0, silu0 = T.res_done.n, T.silu_done.n
    with ExitStack() as ctx:
        def sb(name, shape, dt=F32):
            return ctx.enter_context(nc.sbuf_tensor(f"{name}_{row}", shape, dt))

        gate, work, acc = T.gate, sb("work", [P, 2, NT]), T.prod[:, 0]
        norm = Norm(T, row, 1.0, KT + 1, U + used, True)
        acc0 = T.acc_added.n
        block = ctx.enter_context(nc.Block())

        def pieces():
            for d in range(KT):
                if gated:
                    yield d, 0, d, w_out
                    yield d, 1, d, w_gate
                else:
                    yield d, d % 2, d // 2, w_out

        @block.sync
        def _(sp):
            for d, slot, u, w in list(pieces())[2:]:
                load_piece(T, sp, slot, U + u, out_piece(w, d))
            for slot in range(2):
                load_piece(T, sp, slot, U + used, nxt[slot])

        @block.tensor
        def _(pe):
            for d, slot, u, w in pieces():
                j = d % 2
                if w is w_out:
                    pe.wait_ge(T.res_done.h, res0 + d - 1)
                pe.wait_ge(T.w_split[slot].h, U + u + 2)
                for n in range(2):
                    for k in range(KT):
                        cols = slice(n * NH, (n + 1) * NH)
                        mm = product3(pe, T.ps[:, 4 * j + (0 if w is w_out else 2) + n, 0:NH],
                                      T.w_hi[:, slot, k * P:(k + 1) * P], T.w_lo[:, slot, k * P:(k + 1) * P],
                                      T.x_hi[:, k, cols], T.x_lo[:, k, cols], k == 0, k == KT - 1)
                mm.then_inc(T.w_used[slot].h, 1)

        @block.scalar
        def _(act):
            order = list(pieces())
            for d in range(KT):
                for dd, slot, u, w in order:
                    if dd == d + (1 if gated else 2):
                        round_piece(T, act, slot, U + u, G)
                if gated:
                    act.wait_ge(T.w_used[1].h, U + d + 2)
                    act.activation(halves(gate[:, d % 2]), T.ps[:, 4 * (d % 2) + 2:4 * (d % 2) + 4, 0:NH],
                                   ACT.Sigmoid).then_inc(T.silu_done.h, 1)

        @block.vector
        def _(dve):
            order = list(pieces())
            dve.memset(acc, 0.0).then_inc(T.acc_added.h, 1)
            for d in range(KT):
                j = d % 2
                for dd, slot, u, w in order:
                    if dd == d + (1 if gated else 2):
                        rest_piece(T, dve, slot, U + u, G)
                y = T.ps[:, 4 * j:4 * j + 2, 0:NH]
                if gated:
                    dve.wait_ge(T.silu_done.h, silu0 + d + 1)
                    T.dve_chain(dve, dve.tensor_tensor(halves(work[:, j]), halves(gate[:, j]), y, ALU.mult))
                    y = halves(work[:, j])
                else:
                    dve.wait_ge(T.w_used[j].h, U + d // 2 + 2)
                dve.scalar_tensor_tensor(halves(T.x[:, d]), halves(T.x[:, d]), ALPHA, y, ALU.mult, ALU.add)\
                   .then_inc(T.res_done.h, 1)
                dve.wait_ge(T.res_done.h, res0 + d + 1)
                dve.wait_ge(T.acc_added.h, acc0 + d + 1)
                dve.tensor_tensor(acc, acc, T.x[:, d], ALU.add).then_inc(T.acc_added.h, 1)
    T.res_done.close(KT)
    T.silu_done.close(KT if gated else 0)
    T.pieces += used
    end_with_norm(T, norm, True)



GROUPS, GH, STATES = 64, 16, 64
GPAIRS = GROUPS // 2
CL = 8
PC = SEQ // CL
CHUNKS = NT // CL
GT = P // GH
LN2 = math.log(2.0)
LN2_HI = 0.693359375
TWO_PI_HI = 6.28125
TWO_PI_MID = float(np.float32(2 * math.pi - TWO_PI_HI))
TWO_PI_LO = 2 * math.pi - TWO_PI_HI - TWO_PI_MID
TO_INT = 12582912.0


class S5:
    pass


def open_s5_constants(ctx, nc):
    S = S5()

    def sb(name, shape, dt=F32):
        return ctx.enter_context(nc.sbuf_tensor("s5_" + name, shape, dt))

    S.powers = sb("powers", [P, 2, CL + 1, GPAIRS])
    S.coef = sb("coef", [P, 2, GPAIRS])
    S.size2 = sb("size2", [P, GPAIRS])
    S.skip = sb("skip", [GH, GROUPS])
    return S


def open_s5(ctx, nc, S):
    def sb(name, shape, dt=F32):
        return ctx.enter_context(nc.sbuf_tensor("s5_" + name, shape, dt))

    S.b_bar = sb("b_bar", [P, 2, GPAIRS, GH])
    S.c_t = sb("c_t", [P, 2, GPAIRS, GH])
    S.u = sb("u", [P, GROUPS, CHUNKS])
    S.start = sb("start", [P, 2, GPAIRS, CHUNKS])


class S5Constants:

    def __init__(self, T, S, I):
        self.T, self.S, self.I = T, S, I
        self.loaded = Count(T.ctx, T.nc, "s5c_loaded")

    def open(self, ctx):
        def sb(name, shape, dt=F32):
            return ctx.enter_context(self.T.nc.sbuf_tensor("s5c_" + name, shape, dt))

        self.bufs = [sb(n, [P, GPAIRS]) for n in ("l_re", "l_im", "log_dt", "dt", "work", "k", "e_re", "theta", "s", "c",
                                                  "z2", "poly", "tmp")]
        self.k_int = sb("k_int", [P, GPAIRS], I32)
        self.m1, self.m2 = sb("m1", [P, CL // 2, GPAIRS]), sb("m2", [P, CL // 2, GPAIRS])

    def gpsimd(self, pool):
        T, S, I, loaded = self.T, self.S, self.I, self.loaded
        l_re, l_im, log_dt, dt, work, k, e_re, theta, s_, c_, z2, poly, tmp = (b[:, :] for b in self.bufs)
        k_int, m1, m2 = self.k_int[:, :], self.m1, self.m2

        def op(ins):
            T.pool_chain(pool, ins)

        def ts(out, a, s1, s2, op0, op1=None):
            op(pool.tensor_scalar(out, a, s1, s2, op0, op1) if op1 is not None else
               pool.tensor_scalar(out, a, s1, None, op0))

        def tt(out, a, b, o):
            op(pool.tensor_tensor(out, a, b, o))

        def horner(out, z, coefs):
            ts(out, z, coefs[-1], None, ALU.mult)
            for c in coefs[-2::-1]:
                ts(out, out, c, None, ALU.add)
                tt(out, out, z, ALU.mult)

        def less(out, times, part):
            ts(poly, times, -part, None, ALU.mult)
            tt(out, out, poly, ALU.add)

        def exp(out, x):
            ts(work, x, -87.0, 88.0, ALU.max, ALU.min)
            ts(k, work, 1.0 / LN2, TO_INT, ALU.mult, ALU.add)
            ts(k, k, -TO_INT, None, ALU.add)
            less(work, k, LN2_HI)
            less(work, k, LN2 - LN2_HI)
            horner(poly, work, [1.0 / math.factorial(n) for n in range(1, 9)])
            ts(k, k, 127.0, 8388608.0, ALU.add, ALU.mult)
            op(pool.tensor_copy(k_int, k))
            ts(poly, poly, 1.0, None, ALU.add)
            tt(out, poly, k_int.bitcast(F32), ALU.mult)

        with T.nc.allow_non_contiguous_dma(reason="4096 state constants and 1024 skip weights by state and channel"):
            for dst, name in ((l_re, "s5_lam_re"), (l_im, "s5_lam_im")):
                for s in range(2):
                    pool.dma_start(dst[s * STATES:(s + 1) * STATES],
                                   I[name][0].rearrange("(a s) p -> s p a", s=2)[s]).then_inc(loaded.h, 16)
            for s in range(2):
                pool.dma_start(log_dt[s * STATES:(s + 1) * STATES],
                               I["s5_log_dt"][0].rearrange("(a s) -> s a", s=2)[s:s + 1]
                               .to_broadcast([STATES, GPAIRS])).then_inc(loaded.h, 16)
            pool.dma_start(S.skip[:, :], I["s5_d"][0].rearrange("(g h) -> h g", h=GH)).then_inc(loaded.h, 16)
        pool.wait_ge(loaded.h, 7 * 16)
        exp(dt, log_dt)
        tt(tmp, l_re, dt, ALU.mult)
        exp(e_re, tmp)
        tt(theta, l_im, dt, ALU.mult)
        ts(k, theta, 1.0 / (2 * math.pi), TO_INT, ALU.mult, ALU.add)
        ts(k, k, -TO_INT, None, ALU.add)
        for part in (TWO_PI_HI, TWO_PI_MID, TWO_PI_LO):
            less(theta, k, part)
        ts(theta, theta, 0.5, None, ALU.mult)
        tt(z2, theta, theta, ALU.mult)
        horner(s_, z2, [(-1) ** n / math.factorial(2 * n + 1) for n in range(1, 7)])
        ts(s_, s_, 1.0, None, ALU.add)
        tt(s_, s_, theta, ALU.mult)
        horner(c_, z2, [(-1) ** n / math.factorial(2 * n) for n in range(1, 8)])
        ts(c_, c_, 1.0, None, ALU.add)
        tt(c_, s_, c_, ALU.mult)
        tt(s_, s_, s_, ALU.mult)
        ts(s_, s_, -2.0, 1.0, ALU.mult, ALU.add)
        ts(c_, c_, 2.0, None, ALU.mult)
        lam_re, lam_im = S.powers[:, 0, 1], S.powers[:, 1, 1]
        tt(lam_re, e_re, s_, ALU.mult)
        tt(lam_im, e_re, c_, ALU.mult)
        tt(k, l_re, l_re, ALU.mult)
        tt(tmp, l_im, l_im, ALU.mult)
        tt(S.size2[:, :], k, tmp, ALU.add)
        ts(work, lam_re, -1.0, None, ALU.add)
        for r, (x, y, o) in enumerate(((work, lam_im, ALU.add), (lam_im, work, ALU.subtract))):
            tt(tmp, x, l_re, ALU.mult)
            tt(k, y, l_im, ALU.mult)
            tt(S.coef[:, r], tmp, k, o)
        op(pool.memset(S.powers[:, 0, 0], 1.0))
        op(pool.memset(S.powers[:, 1, 0], 0.0))
        n = 1
        while n < CL:
            a = [S.powers[:, r, 1:n + 1] for r in range(2)]
            by = [S.powers[:, r, n:n + 1].to_broadcast([P, n, GPAIRS]) for r in range(2)]
            for r, (x, y, o) in enumerate(((by[0], by[1], ALU.subtract), (by[1], by[0], ALU.add))):
                tt(m1[:, 0:n], a[0], x, ALU.mult)
                tt(m2[:, 0:n], a[1], y, ALU.mult)
                tt(S.powers[:, r, n + 1:2 * n + 1], m1[:, 0:n], m2[:, 0:n], o)
            n *= 2


def phase_s5_inputs(T, S, I):
    nc = T.nc
    turned, moved = Count(T.ctx, nc, "s5i_turned"), [Count(T.ctx, nc, f"s5i_moved{i}") for i in range(2)]
    b_loaded, inverted, rows_loaded, rows_turned, placed = (
        Count(T.ctx, nc, "s5i_" + n) for n in ("b_loaded", "inverted", "rows_loaded", "rows_turned", "placed"))
    with ExitStack() as ctx:
        def sb(name, shape):
            return ctx.enter_context(nc.sbuf_tensor("s5i_" + name, shape, F32))

        chunked = sb("chunked", [P, GROUPS, CL, GH])
        c_rows = sb("c_rows", [P, GT, 2, STATES])
        s_rows = sb("s_rows", [P, 2, 2, P])
        b_raw = sb("b_raw", [P, 2, GPAIRS, GH])
        m1, m2 = sb("m1", [P, GPAIRS, GH]), sb("m2", [P, GPAIRS, GH])
        block = ctx.enter_context(nc.Block())
        N1 = CL * 2
        N2 = GROUPS // 4
        N = N1 + N2

        @block.sync
        def _(sp):
            for r, part in enumerate(("re", "im")):
                sp.dma_start(b_raw[:, r], I["s5_b_" + part][0].rearrange("(a s) p h -> (s p) a h", s=2))                  .then_inc(b_loaded.h, 16)
            for r, part in enumerate(("re", "im")):
                sp.dma_start(c_rows[:, :, r, :],
                             I["s5_c_" + part][0].rearrange("(k q) h p -> (q h) k p", q=GT)).then_inc(rows_loaded.h, 16)
                sp.dma_start(s_rows[:, r, :, :],
                             I["state_s5_" + part][0].rearrange("(j b) (a s) p -> (b a) j (s p)", j=2, s=2))                  .then_inc(rows_loaded.h, 16)

        @block.gpsimd
        def _(pool):
            pool.wait_ge(inverted.h, 1)
            T.pool_chain(pool, pool.tensor_tensor(S.coef[:, :, :], S.coef[:, :, :],
                                                  S.size2[:, :].unsqueeze(1).to_broadcast([P, 2, GPAIRS]), ALU.mult))
            pool.wait_ge(b_loaded.h, 32)
            co = [S.coef[:, r].unsqueeze(2).to_broadcast([P, GPAIRS, GH]) for r in range(2)]
            for r, (x, y, o) in enumerate(((co[0], co[1], ALU.subtract), (co[1], co[0], ALU.add))):
                T.pool_chain(pool, pool.tensor_tensor(m1[:, :, :], b_raw[:, 0], x, ALU.mult))
                T.pool_chain(pool, pool.tensor_tensor(m2[:, :, :], b_raw[:, 1], y, ALU.mult))
                T.pool_chain(pool, pool.tensor_tensor(S.b_bar[:, r], m1[:, :, :], m2[:, :, :], o))

        @block.tensor
        def _(pe):
            for n in range(N):
                if n == N1:
                    for i in range(2):
                        pe.wait_ge(moved[i].h, N1 // 2)
                elif n >= 8:
                    pe.wait_ge(moved[n % 2].h, (n - 8) // 2 + 1)
                for i in range(4):
                    if n < N1:
                        t, k = n // 2, 4 * (n % 2) + i
                        mm = pe.transpose(T.ps[0:CHUNKS, n % 8, i * P:(i + 1) * P], T.x[:, k, t:NT:CL], T.ident[:, :])
                    else:
                        g = 4 * (n - N1) + i
                        mm = pe.transpose(T.ps[:, n % 8, i * CHUNKS:(i + 1) * CHUNKS],
                                          chunked[0:CHUNKS, g].rearrange("p t h -> p (t h)"),
                                          T.ident[0:CHUNKS, 0:CHUNKS])
                mm.then_inc(turned.h, 1)
            pe.wait_ge(rows_loaded.h, 4 * 16)
            for i in range(2):
                pe.wait_ge(moved[i].h, N // 2 - 2)
            for t in range(GT):
                mm = pe.transpose(T.ps[:, t // 4, (t % 4) * P:(t % 4 + 1) * P],
                                  c_rows[:, t].rearrange("p r s -> p (r s)"), T.ident[:, :])
            mm.then_inc(rows_turned.h, 1)
            for r in range(2):
                for j in range(2):
                    mm = pe.transpose(T.ps[:, 2 + r, j * P:(j + 1) * P], s_rows[:, r, j, :], T.ident[:, :])
            mm.then_inc(rows_turned.h, 1)

        def move(eng, copy, i):
            for n in range(i, N, 2):
                eng.wait_ge(turned.h, n + 1)
                if n < N1:
                    t, k = n // 2, 4 * (n % 2)
                    out = chunked[0:CHUNKS, k * GT:(k + 4) * GT, t, :]
                    src = T.ps[0:CHUNKS, n % 8, :].rearrange("p (g h) -> p g h", h=GH)
                else:
                    g = 4 * (n - N1)
                    out = S.u[:, g:g + 4, :]
                    src = T.ps[:, n % 8, 0:4 * CHUNKS].rearrange("p (g c) -> p g c", g=4)
                copy(out, src).then_inc(moved[i].h, 1)
            eng.wait_ge(rows_turned.h, 1)
            src = T.ps[:, 0:2, :].rearrange("p b (k q s h) -> p (b k) q s h", k=4, s=2, h=GH)
            for s in range(2):
                for kk in range(2):
                    copy(S.c_t[s * HD:(s + 1) * HD, i, 16 * kk:16 * kk + 16, :].rearrange("p (k q) h -> p k q h", q=4),
                         src[i * HD:(i + 1) * HD, 4 * kk:4 * kk + 4, :, s, :]).then_inc(placed.h, 1)
            eng.wait_ge(rows_turned.h, 2)
            copy(S.start[:, i, :, PC:CHUNKS],
                 T.ps[:, 2 + i, 0:2 * P].rearrange("p (b a) -> p a b", b=DEC_BATCH)).then_inc(placed.h, 1)

        @block.vector
        def _(dve):
            dve.reciprocal(S.size2[:, :], S.size2[:, :]).then_inc(inverted.h, 1)
            move(dve, dve.tensor_copy, 0)

        @block.scalar
        def _(act):
            move(act, lambda out, src: act.activation(out, src, ACT.Copy), 1)


def phase_s5_scan(T, S, c_pow, O):
    nc = T.nc
    Q = 4
    STEPS = GPAIRS // Q
    RUN = 8
    RUNS = PC // RUN
    FIX = 8
    formed, b_turned, b_moved, added, moved, jumped, states_done, turned, out_moved, stored = (
        Count(T.ctx, nc, "s5s_" + n) for n in ("formed", "b_turned", "b_moved", "added", "moved", "jumped",
                                               "states_done", "turned", "out_moved", "stored"))
    with ExitStack() as ctx:
        def sb(name, shape, dt=F32):
            return ctx.enter_context(nc.sbuf_tensor("s5s_" + name, shape, dt))

        falling = sb("falling", [P, 2, CL, GPAIRS])
        b_pow, b_rows = sb("b_pow", [P, 2, 2, Q, CL, GH]), sb("b_rows", [P, 2, Q, P])
        jump = sb("jump", [P, 2, RUN, GPAIRS])
        ends = sb("ends", [P, 2, DEC_BATCH, GPAIRS])
        end = sb("end", [P, 2, GPAIRS])
        out_rows = sb("out_rows", [P, 5, P])
        signal = sb("signal", [P, 3])
        m2, minus = sb("m2", [P, 4, CL + 1, GH]), sb("minus", [P, 2, CL + 1, GPAIRS])
        part = sb("part", [P, 4, FIX * (RUNS - 1) * (RUN - 1)])
        m1 = part[:, 0:2].rearrange("p i n -> p (i n)")[:, 0:Q * CL * GH]\
            .rearrange("p (a t h) -> p a t h", a=Q, t=CL)
        block = ctx.enter_context(nc.Block())
        half = [slice(0, HD), slice(HD, P)]
        runs = S.start[:, :, :, 0:PC].rearrange("p r a (b j) -> p r a b j", j=RUN)

        @block.vector
        def _(dve):
            def op(ins):
                T.dve_chain(dve, ins)

            for t in range(CL):
                last = dve.tensor_copy(falling[:, :, t], S.powers[:, :, CL - 1 - t])
            op(last)
            for q in range(STEPS):
                a = slice(Q * q, Q * (q + 1))
                wide = [P, Q, CL, GH]
                b = [S.b_bar[:, r, a, :].unsqueeze(2).to_broadcast(wide) for r in range(2)]
                f = [falling[:, r, :, a].rearrange("p t a -> p a t").unsqueeze(3).to_broadcast(wide)
                     for r in range(2)]
                if q >= 2:
                    dve.wait_ge(b_turned.h, q - 1)
                out = [b_pow[:, q % 2, r] for r in range(2)]
                for r, (x, y, o) in enumerate(((f[0], f[1], ALU.subtract), (f[1], f[0], ALU.add))):
                    dve.tensor_tensor(out[r], b[0], x, ALU.mult)
                    op(dve.tensor_tensor(m1, b[1], y, ALU.mult))
                    last = dve.tensor_tensor(out[r], out[r], m1, o)
                    if r == 0:
                        op(last)
                last.then_inc(formed.h, 1)
                dve.wait_ge(formed.h, q + 1)

            def advance(out, src, f, shape):
                n = int(np.prod(shape[1:]))
                names = " ".join(f"d{i}" for i in range(len(shape) - 1))
                sizes = {f"d{i}": k for i, k in enumerate(shape[1:])}
                buf = [part[:, i, 0:n].rearrange(f"p ({names}) -> p {names}", **sizes) for i in range(4)]
                dve.tensor_tensor(buf[0], src[0], f[0], ALU.mult)
                dve.tensor_tensor(buf[1], src[1], f[0], ALU.mult)
                dve.tensor_tensor(buf[2], src[1], f[1], ALU.mult)
                op(dve.tensor_tensor(buf[3], src[0], f[1], ALU.mult))
                dve.tensor_tensor(out[0], out[0], buf[0], ALU.add)
                op(dve.tensor_tensor(out[1], out[1], buf[1], ALU.add))
                dve.tensor_tensor(out[0], out[0], buf[2], ALU.subtract)
                op(dve.tensor_tensor(out[1], out[1], buf[3], ALU.add))

            op(dve.memset(S.start[:, :, :, 0:1], 0.0))
            dve.wait_ge(moved.h, STEPS)
            dve.wait_ge(jumped.h, 1)

            def over(k, shape):
                f = [jump[:, r, k] for r in range(2)]
                if len(shape) == 3:
                    f = [x.unsqueeze(2).to_broadcast(shape) for x in f]
                return f

            wide = [P, GPAIRS, DEC_BATCH]
            advance([ends[:, r].rearrange("p b a -> p a b") for r in range(2)],
                    [S.start[:, r, :, PC:CHUNKS] for r in range(2)], over(0, wide), wide)
            dve.memset(signal[:, 1:2], 0.0).then_inc(states_done.h, 1)
            for j in range(1, RUN - 1):
                wide = [P, GPAIRS, RUNS]
                advance([runs[:, r, :, :, j + 1] for r in range(2)], [runs[:, r, :, :, j] for r in range(2)],
                        over(0, wide), wide)
            wide = [P, GPAIRS, RUNS - 1]
            advance([runs[:, r, :, 1:RUNS, 0] for r in range(2)],
                    [runs[:, r, :, 0:RUNS - 1, RUN - 1] for r in range(2)], over(0, wide), wide)
            flat = [P, GPAIRS]
            advance([end[:, r] for r in range(2)], [runs[:, r, :, RUNS - 1, RUN - 1] for r in range(2)],
                    over(0, flat), flat)
            for b in range(1, RUNS):
                out = [runs[:, r, :, b + 1, 0] if b + 1 < RUNS else end[:, r] for r in range(2)]
                advance(out, [runs[:, r, :, b, 0] for r in range(2)], over(RUN - 1, flat), flat)
            dve.memset(signal[:, 2:3], 0.0).then_inc(states_done.h, 1)
            for a0 in range(0, GPAIRS, FIX):
                a = slice(a0, a0 + FIX)
                wide = [P, FIX, RUNS - 1, RUN - 1]
                advance([runs[:, r, a, 1:RUNS, 1:RUN] for r in range(2)],
                        [runs[:, r, a, 1:RUNS, 0:1].to_broadcast(wide) for r in range(2)],
                        [jump[:, r, 0:RUN - 1, a].rearrange("p j a -> p a j").unsqueeze(2).to_broadcast(wide)
                         for r in range(2)], wide)

        @block.scalar
        def _(act):
            def move(q):
                a = slice(Q * q, Q * (q + 1))
                for r in range(2):
                    src = T.ps[:, 2 + 2 * (q % 2) + r, 0:Q * CHUNKS].rearrange("p (a c) -> p a c", a=Q)
                    act.activation(S.start[:, r, a, 1:PC], src[:, :, 0:PC - 1], ACT.Copy)
                    act.activation(end[:, r, a], src[:, :, PC - 1], ACT.Copy)
                    last = act.activation(ends[:, r, :, a].rearrange("p b a -> p a b"), src[:, :, PC:CHUNKS], ACT.Copy)
                last.then_inc(moved.h, 1)

            for q in range(STEPS):
                act.wait_ge(b_turned.h, q + 1)
                if q:
                    act.wait_ge(added.h, q)
                for r in range(2):
                    last = act.activation(b_rows[:, r], T.ps[:, r, :].rearrange("p (a s) -> p a s", a=Q), ACT.Copy)
                last.then_inc(b_moved.h, 1)
                if q:
                    move(q - 1)
            act.wait_ge(added.h, STEPS)
            move(STEPS - 1)
            for n in range(5):
                act.wait_ge(turned.h, n + 1)
                m = P if n < 4 else 2 * GPAIRS
                act.activation(out_rows[0:m, n, :], T.ps[0:m, n, 0:P], ACT.Copy).then_inc(out_moved.h, 1)

        @block.tensor
        def _(pe):
            def increments(q):
                pe.wait_ge(b_moved.h, q + 1)
                if q >= 2:
                    pe.wait_ge(moved.h, q - 1)
                for a in range(Q):
                    for s in range(2):
                        for r in range(2):
                            mm = pe.matmul(T.ps[half[s], 2 + 2 * (q % 2) + r, a * CHUNKS:(a + 1) * CHUNKS],
                                           b_rows[:, r, a, half[s]], S.u[:, 2 * (Q * q + a) + s, :],
                                           start=True, stop=True)
                mm.then_inc(added.h, 1)

            for q in range(STEPS):
                pe.wait_ge(formed.h, q + 1)
                if q:
                    pe.wait_ge(b_moved.h, q)
                for r in range(2):
                    for a in range(Q):
                        mm = pe.transpose(T.ps[:, r, a * P:(a + 1) * P],
                                          b_pow[:, q % 2, r, a].rearrange("p t h -> p (t h)"), T.ident[:, :])
                mm.then_inc(b_turned.h, 1)
                increments(q)
            pe.wait_ge(states_done.h, 1)
            for r in range(2):
                for j in range(2):
                    pe.transpose(T.ps[:, 2 * r + j, 0:P],
                                 ends[:, r, 4 * j:4 * j + 4, :].rearrange("p b a -> p (b a)"), T.ident[:, :])\
                      .then_inc(turned.h, 1)
            pe.wait_ge(states_done.h, 2)
            pe.transpose(T.ps[0:2 * GPAIRS, 4, 0:P], end[:, :, :].rearrange("p r a -> p (r a)"), T.ident[:, :])\
              .then_inc(turned.h, 1)

        @block.sync
        def _(sp):
            for r, part_ in enumerate(("re", "im")):
                for j in range(2):
                    sp.wait_ge(out_moved.h, 2 * r + j + 1)
                    sp.dma_start(O[f"s5_{part_}_sample"].rearrange("(j b) (a s) p -> j (b a) (s p)", j=2, s=2)[j],
                                 out_rows[:, 2 * r + j, :]).then_inc(stored.h, 16)
            sp.wait_ge(out_moved.h, 5)
            for r, part_ in enumerate(("re", "im")):
                sp.dma_start(O[f"s5_{part_}_prompt"].rearrange("(a s) p -> a (s p)", s=2),
                             out_rows[r * GPAIRS:(r + 1) * GPAIRS, 4, :]).then_inc(stored.h, 16)
            sp.wait_ge(stored.h, 6 * 16)

        @block.gpsimd
        def _(pool):
            def tt(out, a, b, o):
                T.pool_chain(pool, pool.tensor_tensor(out, a, b, o))

            T.pool_chain(pool, pool.tensor_copy(jump[:, :, 0], S.powers[:, :, CL]))
            t1, t2 = (m2[:, i].rearrange("p k h -> p (k h)")[:, 0:4 * GPAIRS].rearrange("p (n a) -> p n a", n=4)
                      for i in range(2))
            n = 1
            while n < RUN:
                a = [jump[:, r, 0:n] for r in range(2)]
                by = [jump[:, r, n - 1:n].to_broadcast([P, n, GPAIRS]) for r in range(2)]
                for r, (x, y, o) in enumerate(((by[0], by[1], ALU.subtract), (by[1], by[0], ALU.add))):
                    tt(t1[:, 0:n], a[0], x, ALU.mult)
                    tt(t2[:, 0:n], a[1], y, ALU.mult)
                    tt(jump[:, r, n:2 * n], t1[:, 0:n], t2[:, 0:n], o)
                n *= 2
            T.pool_chain(pool, pool.tensor_scalar(minus[:, :, :, :], S.powers[:, :, :, :], -1.0, None, ALU.mult))
            pool.memset(signal[:, 0:1], 0.0).then_inc(jumped.h, 1)
            for q in range(GPAIRS // 4):
                a = slice(4 * q, 4 * q + 4)
                wide = [P, 4, CL + 1, GH]
                c = [S.c_t[:, r, a, :].unsqueeze(2).to_broadcast(wide) for r in range(2)]
                f, g = ([x[:, r, :, a].rearrange("p k a -> p a k").unsqueeze(3).to_broadcast(wide) for r in range(2)]
                        for x in (S.powers, minus))
                for r, (x, y) in enumerate(((f[0], g[1]), (g[1], g[0]))):
                    pool.tensor_tensor(c_pow[:, r, a], c[0], x, ALU.mult)
                    tt(m2[:, :, :, :], c[1], y, ALU.mult)
                    tt(c_pow[:, r, a], c_pow[:, r, a], m2[:, :, :, :], ALU.add)


def phase_s5_outputs(T, S, c_pow):
    nc = T.nc
    names = ("kernels", "placed", "mixed", "gelued", "turned", "rounded", "rested")
    kernels, placed, mixed, gelued, turned, rounded, rested = (Count(T.ctx, nc, "s5o_" + n) for n in names)
    zeroed = Count(T.ctx, nc, "s5o_zeroed")
    spread, stacked = ([Count(T.ctx, nc, f"s5o_{n}{i}") for i in range(2)] for n in ("spread", "stacked"))
    A = GT // 2
    with ExitStack() as ctx:
        def sb(name, shape, dt=F32):
            return ctx.enter_context(nc.sbuf_tensor("s5o_" + name, shape, dt))

        kernel_of = sb("kernel", [GH, 2 * A, 2 * P])
        toeplitz = sb("toeplitz", [P, 2, 2 * A, P])
        starts = sb("starts", [P, 2 * A, CHUNKS])
        decays = sb("decays", [P, 2 * A, P])
        diag = sb("diag", [GH, 2 * A, GH])
        gel = sb("gel", [P, CL, A, 2, GH])
        block = ctx.enter_context(nc.Block())
        half = [slice(0, HD), slice(HD, P)]

        @block.tensor
        def _(pe):
            def make_kernels(e):
                if e:
                    pe.wait_ge(placed.h, e)
                for s in range(2):
                    for a in range(A):
                        gp = A * e + a
                        for r in range(2):
                            mm = pe.matmul(T.ps[0:GH, s, a * P:(a + 1) * P], S.b_bar[half[s], r, gp, :],
                                           c_pow[half[s], r, gp, 0:CL, :].rearrange("p k h -> p (k h)"),
                                           start=(r == 0), stop=(r == 1))
                mm.then_inc(kernels.h, 1)

            def outputs(e):
                pe.wait_ge(spread[e % 2].h, (e // 2 + 1) * CL * 16)
                for i in range(2):
                    pe.wait_ge(stacked[i].h, e + 1)
                if e:
                    pe.wait_ge(gelued.h, 2 * e)
                for s in range(2):
                    for a in range(A):
                        gp = A * e + a
                        out = T.ps[0:CHUNKS, 2 + s, a * P:(a + 1) * P]
                        pe.matmul(out, S.u[:, 2 * gp + s, :], toeplitz[:, e % 2, s * A + a, :], start=True, stop=False)
                        mm = pe.matmul(out, starts[:, s * A + a, :], decays[:, s * A + a, :],
                                       start=False, stop=True)
                mm.then_inc(mixed.h, 1)

            def turn(e):
                pe.wait_ge(gelued.h, 2 * e + 2)
                if e:
                    pe.wait_ge(rested.h, e)
                for t in range(CL):
                    mm = pe.transpose(T.ps[:, 4 + t // 4, (t % 4) * CHUNKS:(t % 4 + 1) * CHUNKS],
                                      gel[0:CHUNKS, t].rearrange("p a s h -> p (a s h)"), T.ident[0:CHUNKS, 0:CHUNKS])
                mm.then_inc(turned.h, 1)

            make_kernels(0)
            make_kernels(1)
            for e in range(KT):
                outputs(e)
                if e + 2 < KT:
                    make_kernels(e + 2)
                turn(e)

        def stack(eng, copy, e, s):
            if e:
                eng.wait_ge(mixed.h, e)
            pairs, to = slice(A * e, A * (e + 1)), slice(A * s, A * (s + 1))
            for r in range(2):
                copy(starts[half[r], to, :], S.start[half[s], r, pairs, :])
                last = copy(decays[half[r], to, :].rearrange("p a (k h) -> p a k h", h=GH),
                            c_pow[half[s], r, pairs, 1:CL + 1, :])
            last.then_inc(stacked[s].h, 1)

        @block.vector
        def _(dve):
            def place(e):
                dve.wait_ge(kernels.h, e + 1)
                if e >= 1:
                    dve.wait_ge(spread[(e - 1) % 2].h, ((e - 1) // 2 + 1) * CL * 16)
                dst = kernel_of[:, :, P:2 * P]
                T.dve_chain(dve, dve.tensor_copy(dst.rearrange("p (s a) k -> p s a k", s=2),
                                                 T.ps[0:GH, 0:2, :].rearrange("p s (a k) -> p s a k", a=A)))
                skip = S.skip[:, GT * e:GT * (e + 1)].rearrange("p (a s) -> p s a", s=2)
                for s in range(2):
                    last = dve.tensor_tensor(diag[:, s * A:(s + 1) * A, :],
                                             T.ident[0:GH, 0:GH].unsqueeze(1).to_broadcast([GH, A, GH]),
                                             skip[:, s].unsqueeze(2).to_broadcast([GH, A, GH]), ALU.mult)
                T.dve_chain(dve, last)
                dve.tensor_tensor(dst[:, :, 0:GH], dst[:, :, 0:GH], diag[:, :, :], ALU.add).then_inc(placed.h, 1)
                dve.wait_ge(placed.h, e + 1)

            def rest(e):
                dve.wait_ge(rounded.h, e + 1)
                dve.tensor_tensor(T.x_lo[:, e].rearrange("p (c b t) -> p b t c", b=2, t=4),
                                  T.ps[:, 4:6, 0:4 * CHUNKS].rearrange("p b (t c) -> p b t c", t=4),
                                  T.x_hi[:, e].rearrange("p (c b t) -> p b t c", b=2, t=4).bitcast(F32),
                                  ALU.subtract).then_inc(rested.h, 1)

            dve.memset(kernel_of[:, :, 0:P], 0.0).then_inc(zeroed.h, 1)
            dve.wait_ge(zeroed.h, 1)
            stack(dve, dve.tensor_copy, 0, 1)
            place(0)
            place(1)
            for e in range(KT):
                if e + 1 < KT:
                    stack(dve, dve.tensor_copy, e + 1, 1)
                if e + 2 < KT:
                    place(e + 2)
                rest(e)

        @block.scalar
        def _(act):
            def copy(out, src):
                return act.activation(out, src, ACT.Copy)

            stack(act, copy, 0, 0)
            for e in range(KT):
                act.wait_ge(mixed.h, e + 1)
                if e:
                    act.wait_ge(turned.h, e)
                for s in range(2):
                    act.activation(gel[0:CHUNKS, :, :, s, :].rearrange("p t a h -> p a t h"),
                                   T.ps[0:CHUNKS, 2 + s, :].rearrange("p (a t h) -> p a t h", a=A, h=GH),
                                   ACT.Gelu_apprx_tanh).then_inc(gelued.h, 1)
                if e + 1 < KT:
                    stack(act, copy, e + 1, 0)
                act.wait_ge(turned.h, e + 1)
                act.activation(T.x_hi[:, e].rearrange("p (c b t) -> p b t c", b=2, t=4),
                               T.ps[:, 4:6, 0:4 * CHUNKS].rearrange("p b (t c) -> p b t c", t=4), ACT.Copy)\
                   .then_inc(rounded.h, 1)

        @block.sync
        def _(sp):
            for e in range(KT):
                sp.wait_ge(placed.h, e + 1)
                if e >= 2:
                    sp.wait_ge(mixed.h, e - 1)
                for t in range(CL):
                    sp.dma_start(toeplitz[t * GH:(t + 1) * GH, e % 2],
                                 kernel_of[:, :, P - t * GH:2 * P - t * GH]).then_inc(spread[e % 2].h, 16)


def host_tables():
    half = HD // 2
    inv = (10000.0 ** (-np.arange(half) / half)).astype(np.float32)
    pos = np.zeros((P, TT), np.float32)
    step = np.zeros((P, TT), np.float64)
    for t in range(PT):
        pos[:, t] = t * P + np.arange(P)
        step[:, t] = pos[:, t]
    pos[NS:, PT] = PAST_LEN + np.arange(NS) % DEC_SEQ
    step[NS:, PT] = np.arange(NS) % DEC_SEQ
    ang = (pos[:, :, None] * inv).astype(np.float64)
    log_g = np.log1p(-np.exp2(-5.0 - np.arange(HEADS)))
    f = lambda a: np.ascontiguousarray(a, np.float32)
    at = np.arange(P)
    causal = np.where(at[None, :] <= at[:, None], 0.0, NEG)
    keep = at[None, :] >= at[:, None]
    s = np.arange(NS)
    keep_s = (s[None, :] >= s[:, None]) & (s[None, :] // DEC_SEQ == s[:, None] // DEC_SEQ)
    select = s[:, None] // DEC_SEQ == np.arange(DEC_BATCH)
    of_row = log_g.reshape(PAIRS, 2)[:, np.arange(P) // HD].T
    row_b, row_q = at // HD, at % DEC_SEQ
    past_mask = np.full((P, BP, NS), NEG)
    for bp in range(BP):
        seen = (s // DEC_SEQ == 2 * bp + row_b[:, None]) & (s % DEC_SEQ <= row_q[:, None])
        past_mask[:, bp][seen] = 0.0
    return {"past_mask": f(past_mask), "block_no": f(np.tile(np.arange(BLOCKS) + 1.0, (P, 1))),
            "causal": f(causal), "keep": f(keep), "keep_s": f(keep_s), "select": f(select),
            "power": f(np.exp(of_row * SEQ)), "power_s": f(np.exp(of_row * DEC_SEQ)),
            "ident": np.eye(P, dtype=np.float32), "rope_cos": f(np.cos(ang)),
            "rope_sin": f(np.stack([-np.sin(ang), np.sin(ang)], 2)),
            "decay_q": f(np.exp(log_g * (step[:, :, None] + 1))),
            "decay_k": f(np.exp(-log_g * (step[:, :, None] + 1)) * HD ** -0.5)}


def program(nc, I, O):
    rows = lambda a: a.rearrange("b s d -> (b s) d")
    ffn = [[(I[f"ffn{n}_w_gate"][layer], I[f"ffn{n}_w_up"][layer], I[f"ffn{n}_w_down"][layer]) for n in (1, 2)]
           for layer in range(DEPTH)]
    first = lambda w: [gate_piece(w[0], 0), gate_piece(w[1], 0)]
    w_in, w_out = I["w_in_ab"][0], I["w_out_ab"][0]
    s5_out, s5_gate = I["s5_w_out"][0], I["s5_w_gate"][0]
    with ExitStack() as ctx:
        T = open_trunk(ctx, nc)
        phase_load(T, rows(I["x_prompt"]), rows(I["x_sample"]), rows(I["ln_g"]), rows(I["ln_b"]), I["ident"],
                   first(ffn[0][0]))
        S = open_s5_constants(ctx, nc)
        with ExitStack() as nctx:
            open_norm_buffers(nctx, T)
            phase_ffn(T, *ffn[0][0], 0, [in_piece(w_in, 0), in_piece(w_in, 1)], join=True)
            M = Trunk()
            with ExitStack() as actx:
                open_mix(actx, nc, M, "attention")
                with ExitStack() as rctx:
                    open_mix(rctx, nc, M, "retention")
                    phase_project(T, M, w_in, I["rope_cos"], I["rope_sin"], I["decay_q"], I["decay_k"],
                                  I["page_table"],
                                  [I[n] for n in ("keep", "power", "power_s", "keep_s", "select")], O,
                                  [out_piece(w_out, 0), out_piece(w_out, 1)])
                    phase_attend_prompt(T, M, I["causal"])
                    M.states = rctx.enter_context(nc.sbuf_tensor("states", [P, DEC_BATCH * PAIRS, P], F32))
                    phase_retain_prompt(T, M, O["state_prompt"], I["state_ret"][0])
                    phase_retain_samples(T, M, O["state_sample"])
                phase_attend_samples(T, M, I["cache_k"][0], I["cache_v"][0], I["past_mask"],
                                     I["block_no"], I["cache_k"].shape[1])
            phase_out(T, w_out, None, 1, first(ffn[0][1]))
            phase_ffn(T, *ffn[0][1], 2, first(ffn[1][0]), join=True)
            phase_ffn(T, *ffn[1][0], 3, [out_piece(s5_out, 0), out_piece(s5_gate, 0)], products=False,
                      beside=S5Constants(T, S, I))
        with ExitStack() as sctx:
            open_s5(sctx, nc, S)
            phase_s5_inputs(T, S, I)
            c_pow = sctx.enter_context(nc.sbuf_tensor("s5_c_pow", [P, 2, GPAIRS, CL + 1, GH], F32))
            phase_s5_scan(T, S, c_pow, O)
            phase_s5_outputs(T, S, c_pow)
        with ExitStack() as nctx:
            open_norm_buffers(nctx, T)
            phase_out(T, s5_out, s5_gate, 4, first(ffn[1][1]))
            phase_ffn(T, *ffn[1][1], 5, None, products=False)
        phase_store(T, O["y_prompt"], O["y_sample"])


OUTPUTS = (
    ("y_prompt", (SEQ, D_MODEL), (1, SEQ, D_MODEL)),
    ("y_sample", (NS, D_MODEL), (DEC_BATCH, DEC_SEQ, D_MODEL)),
    ("k_prompt", (SEQ, MIX), (1, 1, PT, PAGE, HEADS, HD)),
    ("v_prompt", (SEQ, MIX), (1, 1, PT, PAGE, HEADS, HD)),
    ("k_sample", (NS, MIX), (1, DEC_BATCH, DEC_SEQ, HEADS, HD)),
    ("v_sample", (NS, MIX), (1, DEC_BATCH, DEC_SEQ, HEADS, HD)),
    ("state_prompt", (HEADS, HD, HD), (1, 1, HEADS, HD, HD)),
    ("state_sample", (DEC_BATCH, HEADS, HD, HD), (1, DEC_BATCH, HEADS, HD, HD)),
    ("s5_re_prompt", (GROUPS, STATES), (1, 1, GROUPS, STATES)),
    ("s5_im_prompt", (GROUPS, STATES), (1, 1, GROUPS, STATES)),
    ("s5_re_sample", (DEC_BATCH, GROUPS, STATES), (1, DEC_BATCH, GROUPS, STATES)),
    ("s5_im_sample", (DEC_BATCH, GROUPS, STATES), (1, DEC_BATCH, GROUPS, STATES)),
)


def kernel(**inputs):
    import concourse.bacc as bacc
    from concourse.bass_utils import run_bass_kernel_spmd

    nc = bacc.Bacc("TRN2", target_bir_lowering=False, num_devices=1)
    arrays = {name: np.ascontiguousarray(a) for name, a in inputs.items()}
    arrays.update(host_tables())
    I = {name: nc.dram_tensor(f"in_{name}", a.shape, mybir.dt.from_np(a.dtype), kind="ExternalInput").ap()
         for name, a in arrays.items()}
    O = {name: nc.dram_tensor(f"out_{name}", shape, F32, kind="ExternalOutput").ap() for name, shape, _ in OUTPUTS}
    program(nc, I, O)
    r = run_bass_kernel_spmd(nc, [{f"in_{name}": a for name, a in arrays.items()}], core_ids=[0])
    return tuple(np.reshape(r.results[0][f"out_{name}"], shape) for name, _, shape in OUTPUTS)
```
